# Optimizing a Trainium2 kernel written in Bass

```python
import math
import jax
import jax.numpy as jnp
from jax import lax
import numpy as np

D_MODEL = 1024
BATCH = 1
SEQ = 512
DEPTH = 2

CHUNK = 64
Q_BLOCK = 128
N_MEM = 256
MAX_STREAM_OFFSET = 4096
LN_EPS = 1e-5
RMS_EPS = 1e-6

DA_HEAD_DIM = 64
DA_V_DIM = 2 * DA_HEAD_DIM
DA_WIDTH = D_MODEL // 2
DA_HEADS = DA_WIDTH // DA_V_DIM
DA_QK = 2 * DA_HEADS * DA_HEAD_DIM
ROPE_THETA = 10000.0

RW_HEAD_DIM = 64
RW_WIDTH = D_MODEL // 4
RW_HEADS = RW_WIDTH // RW_HEAD_DIM
RW_DECAY_RANK = 32
RW_AAA_RANK = 32
RW_GATE_RANK = 64
RW_IN = 3 * RW_WIDTH + RW_DECAY_RANK + RW_AAA_RANK + RW_GATE_RANK
RW_SPLITS = tuple(int(v) for v in np.cumsum([RW_WIDTH, RW_WIDTH, RW_WIDTH, RW_DECAY_RANK, RW_AAA_RANK]))
RW_DECAY_SCALE = math.exp(-0.5)
RW_LNX_EPS = 64e-5

S5_WIDTH = D_MODEL - DA_WIDTH - RW_WIDTH
S5_GROUP_CH = 16
S5_GROUPS = S5_WIDTH // S5_GROUP_CH
S5_STATE = 64

MIX_WIDTH = DA_WIDTH + RW_WIDTH + S5_WIDTH
IN_SIZES = (DA_QK, DA_QK, DA_WIDTH, RW_IN, S5_WIDTH)
IN_WIDTH = sum(IN_SIZES)
IN_SPLITS = tuple(int(v) for v in np.cumsum(IN_SIZES)[:-1])

MEM_HEADS = 4
MEM_HEAD_DIM = D_MODEL // MEM_HEADS

D_FF = ((8 * D_MODEL // 3 + 127) // 128) * 128
FFN_CONV = 3

ALPHA = (2.0 * DEPTH) ** 0.25
BETA = (8.0 * DEPTH) ** -0.25

kernel_name = 'hybrid_streaming_encoder_trunk'

def layer_norm(x, g, b):
    x32 = x.astype(jnp.float32)
    mu = jnp.mean(x32, axis=-1, keepdims=True)
    var = jnp.mean(jnp.square(x32 - mu), axis=-1, keepdims=True)
    return ((x32 - mu) * lax.rsqrt(var + LN_EPS) * g + b).astype(x.dtype)

def rms_norm(x, g):
    x32 = x.astype(jnp.float32)
    y = x32 * lax.rsqrt(jnp.mean(jnp.square(x32), axis=-1, keepdims=True) + RMS_EPS)
    return (y * g).astype(x.dtype)

def rope_tables(positions):
    inv_freq = ROPE_THETA ** (-jnp.arange(0, DA_HEAD_DIM, 2, dtype=jnp.float32) / DA_HEAD_DIM)
    ang = positions.astype(jnp.float32)[..., None] * inv_freq
    ang = jnp.concatenate([ang, ang], axis=-1)
    return jnp.cos(ang), jnp.sin(ang)

def apply_rope(t, cos, sin):
    c = cos[:, :, None, None, :].astype(t.dtype)
    s = sin[:, :, None, None, :].astype(t.dtype)
    half = t.shape[-1] // 2
    rot = jnp.concatenate([-t[..., half:], t[..., :half]], axis=-1)
    return t * c + rot * s

def diff_attention(pq, pk, pv, cos, sin, lam_q1, lam_k1, lam_q2, lam_k2, subln_g, lambda_init):
    bsz, seq, _ = pq.shape
    nb = seq // Q_BLOCK
    q = apply_rope(pq.reshape(bsz, seq, DA_HEADS, 2, DA_HEAD_DIM), cos, sin) * (DA_HEAD_DIM ** -0.5)
    k = apply_rope(pk.reshape(bsz, seq, DA_HEADS, 2, DA_HEAD_DIM), cos, sin)
    q = q.transpose(3, 0, 2, 1, 4)
    k = k.transpose(3, 0, 2, 1, 4)
    v = pv.reshape(bsz, seq, DA_HEADS, DA_V_DIM).transpose(0, 2, 1, 3)
    lam = (jnp.exp(jnp.sum((lam_q1 * lam_k1).astype(jnp.float32)))
           - jnp.exp(jnp.sum((lam_q2 * lam_k2).astype(jnp.float32))) + lambda_init)
    q_blocks = q.reshape(2, bsz, DA_HEADS, nb, Q_BLOCK, DA_HEAD_DIM).transpose(3, 0, 1, 2, 4, 5)
    key_chunk = jnp.arange(seq) // CHUNK

    def block(args):
        i, qb = args
        q_chunk = (i * Q_BLOCK + jnp.arange(Q_BLOCK)) // CHUNK
        mask = key_chunk[None, :] <= q_chunk[:, None]
        s = jnp.einsum('nbhqd,nbhkd->nbhqk', qb, k).astype(jnp.float32)
        p = jax.nn.softmax(jnp.where(mask, s, -jnp.inf), axis=-1)
        attn = p[0] - lam * p[1]
        return jnp.einsum('bhqk,bhkv->bhqv', attn.astype(v.dtype), v)

    o = lax.map(block, (jnp.arange(nb), q_blocks))
    o = o.transpose(1, 2, 0, 3, 4).reshape(bsz, DA_HEADS, seq, DA_V_DIM)
    o = rms_norm(o, subln_g) * (1.0 - lambda_init)
    return o.transpose(0, 2, 1, 3).reshape(bsz, seq, DA_WIDTH)

def rwkv7_time_mix(p, mu, w0, w2, a0, a2, g2, k_k, k_a, r_k, lnx_g, lnx_b):
    bsz, seq, _ = p.shape
    prev = jnp.pad(p, ((0, 0), (1, 0), (0, 0)))[:, :-1]
    p = p + (prev - p) * mu
    r, k, v, wd, ad, gd = jnp.split(p, RW_SPLITS, axis=-1)

    def heads(t):
        return t.astype(jnp.float32).reshape(bsz, seq, RW_HEADS, RW_HEAD_DIM)

    decay = jnp.exp(-RW_DECAY_SCALE * jax.nn.sigmoid((w0 + jnp.tanh(wd) @ w2).astype(jnp.float32)))
    a = jax.nn.sigmoid((a0 + ad @ a2).astype(jnp.float32))
    g = jax.nn.sigmoid(gd) @ g2
    kk = heads(k * k_k)
    kk = kk * lax.rsqrt(jnp.maximum(jnp.sum(kk * kk, axis=-1, keepdims=True), 1e-24))
    k = k.astype(jnp.float32) * (1.0 + (a - 1.0) * k_a)
    r_h, k_h, v_h, w_h, a_h = heads(r), heads(k), heads(v), heads(decay), heads(a)

    def step(state, inp):
        r_t, w_t, k_t, v_t, kk_t, a_t = inp
        sa = jnp.einsum('bhvk,bhk->bhv', state, -kk_t)
        state = (state * w_t[:, :, None, :] + sa[..., None] * (kk_t * a_t)[:, :, None, :]
                 + v_t[..., None] * k_t[:, :, None, :])
        return state, jnp.einsum('bhvk,bhk->bhv', state, r_t)

    xs = tuple(jnp.moveaxis(t, 1, 0) for t in (r_h, w_h, k_h, v_h, kk, a_h))
    s0 = jnp.zeros((bsz, RW_HEADS, RW_HEAD_DIM, RW_HEAD_DIM), jnp.float32)
    _, y = lax.scan(step, s0, xs)
    y = jnp.moveaxis(y, 0, 1)
    mean = jnp.mean(y, axis=-1, keepdims=True)
    var = jnp.mean(jnp.square(y - mean), axis=-1, keepdims=True)
    y = ((y - mean) * lax.rsqrt(var + RW_LNX_EPS)).reshape(bsz, seq, RW_WIDTH) * lnx_g + lnx_b
    bonus = jnp.sum(r_h * k_h * r_k, axis=-1, keepdims=True) * v_h
    y = y + bonus.reshape(bsz, seq, RW_WIDTH)
    return (y * g).astype(p.dtype)

def s5_ssm(u, a_re, a_im, b_re, b_im, c_re, c_im, d_skip, log_step, glu_w, glu_b, out_g):
    bsz, seq, _ = u.shape
    u32 = u.astype(jnp.float32).reshape(bsz, seq, S5_GROUPS, S5_GROUP_CH)
    A = lax.complex(a_re.astype(jnp.float32), a_im.astype(jnp.float32))
    delta = jnp.exp(log_step.astype(jnp.float32))[:, None]
    a_bar = jnp.exp(delta * A)
    Bc = lax.complex(b_re.astype(jnp.float32), b_im.astype(jnp.float32))
    b_bar = ((a_bar - 1.0) / A)[..., None] * Bc
    bu = lax.complex(jnp.einsum('gph,blgh->blgp', jnp.real(b_bar), u32),
                     jnp.einsum('gph,blgh->blgp', jnp.imag(b_bar), u32))
    a_seq = jnp.broadcast_to(a_bar, bu.shape)

    def combine(e1, e2):
        a1, b1 = e1
        a2, b2 = e2
        return a1 * a2, a2 * b1 + b2

    _, states = lax.associative_scan(combine, (a_seq, bu), axis=1)
    Cc = lax.complex(c_re.astype(jnp.float32), c_im.astype(jnp.float32))
    y = jnp.real(jnp.einsum('ghp,blgp->blgh', Cc, states))
    y = (y + d_skip.astype(jnp.float32).reshape(S5_GROUPS, S5_GROUP_CH) * u32).reshape(bsz, seq, S5_WIDTH)
    z = jax.nn.gelu(y)
    z = z * jax.nn.sigmoid(z @ glu_w.astype(jnp.float32) + glu_b)
    return rms_norm(z, out_g).astype(u.dtype)

def memory_cross_attention(x, mem, wq, wkv, wo):
    bsz, seq, _ = x.shape
    q = (x @ wq).reshape(bsz, seq, MEM_HEADS, MEM_HEAD_DIM)
    k, v = jnp.split(mem @ wkv, 2, axis=-1)
    k = k.reshape(bsz, N_MEM, MEM_HEADS, MEM_HEAD_DIM)
    v = v.reshape(bsz, N_MEM, MEM_HEADS, MEM_HEAD_DIM)
    s = jnp.einsum('blhd,bmhd->bhlm', q, k).astype(jnp.float32) * (MEM_HEAD_DIM ** -0.5)
    p = jax.nn.softmax(s, axis=-1).astype(v.dtype)
    o = jnp.einsum('bhlm,bmhd->blhd', p, v).reshape(bsz, seq, D_MODEL)
    return o @ wo

def conv_ffn(x, w_up, conv_w, conv_b, w_down):
    seq = x.shape[1]
    a, g = jnp.split(x @ w_up, 2, axis=-1)
    ap = jnp.pad(a, ((0, 0), (FFN_CONV - 1, 0), (0, 0)))
    a = conv_b + sum(conv_w[j] * ap[:, j:j + seq] for j in range(FFN_CONV))
    return (jax.nn.silu(a) * g) @ w_down

def setup_inputs(seed: int = 0) -> dict:
    key = jax.random.key(seed)
    keys = iter(jax.random.split(key, 64))

    def normal(shape, scale):
        return scale * jax.random.normal(next(keys), shape, jnp.float32)

    def uniform(shape, lo, hi):
        return jax.random.uniform(next(keys), shape, jnp.float32, lo, hi)

    L = DEPTH
    n_idx = jnp.arange(S5_STATE, dtype=jnp.float32)
    positions = (jax.random.randint(next(keys), (BATCH, 1), 0, MAX_STREAM_OFFSET, dtype=jnp.int32)
                 + jnp.arange(SEQ, dtype=jnp.int32)[None, :])
    return {
        'x': normal((BATCH, SEQ, D_MODEL), 1.0),
        'mem': normal((BATCH, N_MEM, D_MODEL), 1.0),
        'positions': positions,
        'w_in': normal((L, D_MODEL, IN_WIDTH), D_MODEL ** -0.5),
        'da_lam_q1': normal((L, DA_HEAD_DIM), 0.1),
        'da_lam_k1': normal((L, DA_HEAD_DIM), 0.1),
        'da_lam_q2': normal((L, DA_HEAD_DIM), 0.1),
        'da_lam_k2': normal((L, DA_HEAD_DIM), 0.1),
        'da_subln_g': 1.0 + normal((L, DA_V_DIM), 0.02),
        'rw_mu': uniform((L, RW_IN), 0.0, 1.0),
        'rw_w0': normal((L, RW_WIDTH), 1.0),
        'rw_w2': normal((L, RW_DECAY_RANK, RW_WIDTH), 0.1 * RW_DECAY_RANK ** -0.5),
        'rw_a0': normal((L, RW_WIDTH), 0.1),
        'rw_a2': normal((L, RW_AAA_RANK, RW_WIDTH), 0.1 * RW_AAA_RANK ** -0.5),
        'rw_g2': normal((L, RW_GATE_RANK, RW_WIDTH), RW_GATE_RANK ** -0.5),
        'rw_k_k': 0.85 + normal((L, RW_WIDTH), 0.02),
        'rw_k_a': 1.0 + normal((L, RW_WIDTH), 0.02),
        'rw_r_k': normal((L, RW_HEADS, RW_HEAD_DIM), 0.1),
        'rw_lnx_g': 1.0 + normal((L, RW_WIDTH), 0.02),
        'rw_lnx_b': normal((L, RW_WIDTH), 0.02),
        's5_a_re': -0.5 + normal((L, S5_GROUPS, S5_STATE), 0.01),
        's5_a_im': math.pi * n_idx + normal((L, S5_GROUPS, S5_STATE), 0.01),
        's5_b_re': normal((L, S5_GROUPS, S5_STATE, S5_GROUP_CH), (2.0 * S5_GROUP_CH) ** -0.5),
        's5_b_im': normal((L, S5_GROUPS, S5_STATE, S5_GROUP_CH), (2.0 * S5_GROUP_CH) ** -0.5),
        's5_c_re': normal((L, S5_GROUPS, S5_GROUP_CH, S5_STATE), S5_STATE ** -0.5),
        's5_c_im': normal((L, S5_GROUPS, S5_GROUP_CH, S5_STATE), S5_STATE ** -0.5),
        's5_d': normal((L, S5_WIDTH), 1.0),
        's5_log_step': uniform((L, S5_GROUPS), math.log(1e-3), math.log(1e-1)),
        's5_glu_w': normal((L, S5_WIDTH, S5_WIDTH), S5_WIDTH ** -0.5),
        's5_glu_b': normal((L, S5_WIDTH), 0.02),
        's5_out_g': 1.0 + normal((L, S5_WIDTH), 0.02),
        'w_out': normal((L, MIX_WIDTH, D_MODEL), BETA * MIX_WIDTH ** -0.5),
        'ln1_g': 1.0 + normal((L, D_MODEL), 0.02),
        'ln1_b': normal((L, D_MODEL), 0.02),
        'ca_wq': normal((L, D_MODEL, D_MODEL), D_MODEL ** -0.5),
        'ca_wkv': normal((L, D_MODEL, 2 * D_MODEL), D_MODEL ** -0.5),
        'ca_wo': normal((L, D_MODEL, D_MODEL), BETA * D_MODEL ** -0.5),
        'ln2_g': 1.0 + normal((L, D_MODEL), 0.02),
        'ln2_b': normal((L, D_MODEL), 0.02),
        'ffn_w_up': normal((L, D_MODEL, 2 * D_FF), D_MODEL ** -0.5),
        'ffn_conv_w': normal((L, FFN_CONV, D_FF), 0.5),
        'ffn_conv_b': normal((L, D_FF), 0.02),
        'ffn_w_down': normal((L, D_FF, D_MODEL), BETA * D_FF ** -0.5),
        'ln3_g': 1.0 + normal((L, D_MODEL), 0.02),
        'ln3_b': normal((L, D_MODEL), 0.02),
    }

def reference(x, mem, positions, w_in, da_lam_q1, da_lam_k1, da_lam_q2, da_lam_k2, da_subln_g,
              rw_mu, rw_w0, rw_w2, rw_a0, rw_a2, rw_g2, rw_k_k, rw_k_a, rw_r_k, rw_lnx_g, rw_lnx_b,
              s5_a_re, s5_a_im, s5_b_re, s5_b_im, s5_c_re, s5_c_im, s5_d, s5_log_step,
              s5_glu_w, s5_glu_b, s5_out_g, w_out, ln1_g, ln1_b, ca_wq, ca_wkv, ca_wo, ln2_g, ln2_b,
              ffn_w_up, ffn_conv_w, ffn_conv_b, ffn_w_down, ln3_g, ln3_b):
    cos, sin = rope_tables(positions)
    for l in range(DEPTH):
        lambda_init = 0.8 - 0.6 * math.exp(-0.3 * l)
        p_q, p_k, p_v, p_rw, p_s5 = jnp.split(x @ w_in[l], IN_SPLITS, axis=-1)
        h_da = diff_attention(p_q, p_k, p_v, cos, sin, da_lam_q1[l], da_lam_k1[l], da_lam_q2[l],
                              da_lam_k2[l], da_subln_g[l], lambda_init)
        h_rw = rwkv7_time_mix(p_rw, rw_mu[l], rw_w0[l], rw_w2[l], rw_a0[l], rw_a2[l], rw_g2[l],
                              rw_k_k[l], rw_k_a[l], rw_r_k[l], rw_lnx_g[l], rw_lnx_b[l])
        h_s5 = s5_ssm(p_s5, s5_a_re[l], s5_a_im[l], s5_b_re[l], s5_b_im[l], s5_c_re[l], s5_c_im[l],
                      s5_d[l], s5_log_step[l], s5_glu_w[l], s5_glu_b[l], s5_out_g[l])
        h = jnp.concatenate([h_da.astype(x.dtype), h_rw.astype(x.dtype), h_s5.astype(x.dtype)], axis=-1)
        x = layer_norm(ALPHA * x + h @ w_out[l], ln1_g[l], ln1_b[l])
        h = memory_cross_attention(x, mem, ca_wq[l], ca_wkv[l], ca_wo[l])
        x = layer_norm(ALPHA * x + h, ln2_g[l], ln2_b[l])
        h = conv_ffn(x, ffn_w_up[l], ffn_conv_w[l], ffn_conv_b[l], ffn_w_down[l])
        x = layer_norm(ALPHA * x + h, ln3_g[l], ln3_b[l])
    return x


_drawn_inputs = setup_inputs


def setup_inputs(seed=0):
    import zlib

    import numpy as np

    out = dict(_drawn_inputs(seed))
    spreads = {}
    factors = {'da_lam_q1': 4.784,
     'da_lam_q2': 3.113,
     'da_lam_k2': 2.943,
     'da_subln_g': 23.215,
     'rw_w2': 8.0,
     'rw_a0': 7.704,
     'rw_a2': 8.0,
     'rw_k_k': 64.0,
     'rw_k_a': 28.374,
     'rw_lnx_g': 45.879,
     'rw_lnx_b': 33.836,
     's5_a_re': 64.0,
     's5_b_re': 3.599,
     's5_b_im': 3.653,
     's5_c_re': 3.612,
     's5_c_im': 3.624,
     's5_glu_b': 8.0,
     's5_out_g': 8.0,
     'ffn_conv_b': 8.0}
    for name, (base, spread) in spreads.items():
        noise = np.random.default_rng([zlib.crc32(name.encode()), seed]).standard_normal(out[name].shape)
        drawn = base * np.exp(spread * noise) if base else spread * noise
        out[name] = jnp.asarray(drawn.astype(out[name].dtype))
    for name, factor in factors.items():
        out[name] = (out[name] * factor).astype(out[name].dtype)
    return out
```

```python
import math
from contextlib import ExitStack

import numpy as np

import concourse.bass as bass
from concourse import mybir

DEPTH, D, T = 2, 1024, 512
P = 128
KT, NT = D // P, T // P
DA_HEADS, DA_W = 4, 512
RW_W, RW_IN, RW_TILES = 256, 896, 7
S5_W, S5_GROUPS, S5_STATE, S5_CH = 256, 16, 64, 16
S5_TILES = S5_GROUPS * S5_STATE // P
IN_W = 3 * DA_W + RW_IN + S5_W
N_MEM, MT, MEM_HEADS = 256, 2, 4
D_FF = 2816
FT = D_FF // P
CH = 64
NCH = T // CH
ALPHA = (2.0 * DEPTH) ** 0.25
DECAY = math.exp(-0.5)
LN_EPS, RMS_EPS, LNX_EPS = 1e-5, 1e-6, 64e-5
NEG = -1e37
ROUND = 1.5 * 2.0 ** 23
ROUND13 = ROUND / 2.0 ** 13
INV_2PI = 1.0 / (2.0 * math.pi)
TWO_PI_SAFE = 6.283184
PI_SAFE = 3.1415925
RING = 5
SLOT = 2048

C_ID, C_SU, C_IU, C_L1U, C_L1L, C_ONE, C_BONE, C_ROT = (P * i for i in range(8))
C_EYE = 8 * P
C_S5M = C_EYE + CH
C_IOTA = C_S5M + 4 * P
C_NEG = C_IOTA + T
C_MROW = C_NEG + CH
C_FREQ = C_MROW + P
C_SC = C_FREQ + 1
SC = {"ln_eps": LN_EPS, "rms_eps": RMS_EPS, "lnx_eps": LNX_EPS, "half_pi": math.pi / 2, "zero": 0.0, "one": 1.0}
C_W = C_SC + len(SC)
LEVELS = [2, 4, 8, 16, 32]

S1 = {}
S2 = {}


def _rows(table, names):
    at = 0
    for name, n in names:
        table[name] = (at, n)
        at += n
    return at


S1_N = _rows(S1, [("ffn_conv_w", 3 * FT), ("ffn_conv_b", FT)])
S2_N = _rows(S2, [("rw_mu", 7), ("rw_w0", 2), ("rw_a0", 2), ("rw_k_k", 2), ("rw_k_a", 2), ("rw_r_k", 2),
                  ("rw_lnx_g", 2), ("rw_lnx_b", 2), ("s5_d", 2), ("s5_glu_b", 2), ("s5_out_g", 2),
                  ("da_subln_g", 1)])


def two_pi_parts():
    hi = np.float32(round(2 * math.pi * 2 ** 9) / 2 ** 9)
    mid = np.float32(round((2 * math.pi - float(hi)) * 2 ** 22) / 2 ** 22)
    lo = np.float32(2 * math.pi - float(hi) - float(mid))
    return float(hi), float(mid), float(lo)


def constants():
    c = np.zeros((P, C_W), np.float32)
    p, m = np.arange(P)[:, None], np.arange(P)[None, :]
    same = p // CH == m // CH
    c[:, C_ID:C_ID + P] = p == m
    c[:, C_SU:C_SU + P] = same & (p < m)
    c[:, C_IU:C_IU + P] = same & (p <= m)
    c[:, C_L1U:C_L1U + P] = (p // 2 == m // 2) & (p < m)
    c[:, C_L1L:C_L1L + P] = (p // 2 == m // 2) & (p > m)
    c[:, C_ONE:C_ONE + P] = 1
    c[:, C_BONE:C_BONE + P] = same
    c[:, C_ROT:C_ROT + P] = np.where((p == m + 32) & (m % 64 < 32), -1.0, np.where((p == m - 32) & (m % 64 >= 32), 1.0, 0.0))
    c[:, C_EYE:C_EYE + CH] = p % CH == np.arange(CH)[None, :]
    for j in range(4):
        c[:, C_S5M + j * P:C_S5M + (j + 1) * P] = m // S5_CH == 2 * j + p // S5_STATE
    c[:, C_IOTA:C_IOTA + T] = np.arange(T)[None, :]
    c[:, C_NEG:C_NEG + CH] = NEG
    c[:, C_MROW:C_MROW + P] = m < CH
    inv = np.float32(10000.0) ** (-np.arange(0, 64, 2, dtype=np.float32) / np.float32(64))
    c[:, C_FREQ] = inv.astype(np.float32)[np.arange(P) % 32]
    for i, v in enumerate(SC.values()):
        c[:, C_SC + i] = v
    lev = np.zeros((P, len(LEVELS), 2, P), np.float32)
    for i, b in enumerate(LEVELS):
        joined = (p // (2 * b) == m // (2 * b)) & (p // b != m // b)
        lev[:, i, 0] = joined & (p > m)
        lev[:, i, 1] = joined & (p < m)
    lam = np.zeros((DEPTH, 2), np.float32)
    for l in range(DEPTH):
        lam[l] = 0.8 - 0.6 * math.exp(-0.3 * l), 1.0 - (0.8 - 0.6 * math.exp(-0.3 * l))
    return {"const": c, "level_masks": lev, "lambda_inits": lam}


class Sem:

    def __init__(self, handle):
        self.h, self.n = handle, 0


def build(nc, io):
    f32, u32, i32 = mybir.dt.float32, mybir.dt.uint32, mybir.dt.int32
    ALU, ACT, AX = mybir.AluOpType, mybir.ActivationFunctionType, mybir.AxisListType
    ctx = ExitStack()
    with ctx:
        def sb(name, shape, dt=f32):
            return ctx.enter_context(nc.sbuf_tensor(name, shape, dt))

        x = sb("x", [P, NT, D])
        xT = sb("xT", [P, KT, T])
        hT = xT
        memT = sb("memT", [P, KT, N_MEM])
        ring = sb("ring", [P, RING, SLOT])
        ropeC, ropeS = sb("ropeC", [P, T]), sb("ropeS", [P, T])
        K = sb("consts", [P, C_W])
        lev = sb("level_masks", [P, len(LEVELS), 2, P])
        lnrow = sb("lnrow", [P, 2, D])
        col1, col2, col3 = sb("col1", [P, S1_N]), sb("col2", [P, S2_N]), sb("col3", [P, 24])
        stat = sb("stat", [P, 2, 40])
        lamc = sb("lamc", [P, 4])
        s5c = sb("s5c", [P, 24, S5_TILES])
        arena = sb("arena", [P, 24448])

        def view(at, *shape):
            n = int(np.prod(shape))
            assert at + n <= 24448, (at, n)
            v = arena[:, at:at + n]
            if len(shape) == 2:
                v = v.rearrange("p (a b) -> p a b", b=shape[1])
            if len(shape) == 3:
                v = v.rearrange("p (a b c) -> p a b c", b=shape[1], c=shape[2])
            return v

        qT, kT, vtok = view(0, 4, T), view(2048, 4, T), view(4096, NT, DA_W)
        PR = view(6144, RW_TILES, T + 2)
        uT = view(9744, 2, T)
        lrw = view(10768, RW_W)
        bn = view(11024, 2, S5_TILES, S5_CH)
        cn = view(11280, 2, 2, P)
        WK = 11792
        gluw = view(WK, 2, S5_W)
        AP_ = view(WK + 512, 4, T)
        aT = view(WK + 2560, 4, T)
        oh, osq, orr = view(WK + 4608, T), view(WK + 5120, T), view(WK + 5632, T)
        S = WK + 6144
        cT = view(S, 4, P)
        bpad, bT, cpad = view(S + 512, 2, P), view(S + 768, 2, P), view(S + 1024, 2, P)
        s_c, s_s = view(S + 1280, T), view(S + 1792, T)
        s_m = [view(S + 2304 + 512 * i, T) for i in range(4)]
        s_z = [view(S + 4352 + 512 * i, T) for i in range(2)]
        s_x = [view(S + 5376 + 512 * i, T) for i in range(2)]
        assert S + 6400 <= 24448
        yT, zT, s_r = view(WK + 4608, 2, T), view(WK + 2560, 2, T), view(WK + 512, 2, T)
        R = WK + 512
        rw = {n: view(R + 512 * i, T) for i, n in enumerate(
            ["LR", "a", "g", "t0", "iP", "kk", "kmod", "A", "B", "Bh", "K", "Kh", "R", "bonus", "t1"])}
        rP = view(R + 7680, NCH, CH + 1)
        vT_, bT_, kT_ = (view(R + 8200 + 512 * i, NT, P) for i in range(3))
        zA = view(R + 9736, 2, NT * P)
        uw = view(R + 10760, 2, NT * P)
        rZ = view(R + 512 * 7, 2, NT * P)
        rH, rS, rG, rQ = rw["K"], rw["iP"], rw["Bh"], rw["Kh"]
        rY = uT[:, 0, :]
        assert R + 11784 <= 24448
        mAB, mRB, mRK, mAK, Ti, TiT = (view(1024 * i, 2, NT * P) for i in range(6))
        mK, mV, q2, o2 = view(0, KT, N_MEM), view(2048, MT, D), view(4096, KT, T), view(8192, KT, T)
        p2, pT2 = view(12288, 2, N_MEM), view(12800, MT, T)
        hid, wdn = view(0, FT, T), view(FT * T, FT, 512)
        fa = [view(2 * FT * T + 514 * i, T + 2) for i in range(2)]
        fc = view(2 * FT * T + 1028, T)
        assert 2 * FT * T + 1540 <= 24448
        memtok = view(0, MT, D)
        posr, posf, ang, tn, tr = (view(2048 + 512 * i, T) for i in range(5))
        sheet = view(0, 3, P)
        lamr = view(512, 6, 64)

        def const(name):
            i = C_SC + list(SC).index(name)
            return K[:, i:i + 1]

        ident, ones, bones, rot = (K[:, c:c + P] for c in (C_ID, C_ONE, C_BONE, C_ROT))

        banks = [ctx.enter_context(nc.psum_tensor(f"bank{i}", [P, 512], f32)) for i in range(8)]

        def sem(name):
            return Sem(ctx.enter_context(nc.semaphore(name)))

        quiet = sem("engines_quiet")
        go = {n: sem(f"go_{n}") for n in ("pe", "act", "dve", "pool")}
        out_done = sem("output_written")
        S = {}

        def ev(name):
            if name not in S:
                S[name] = sem(name)
            return S[name]

        for i in range(8):
            ev(f"bank{i}_filled"), ev(f"bank{i}_emptied")
        for i in range(RING):
            ev(f"slot{i}_loaded")
        for name in ("act_step", "dve_step", "pool_step", "chunk_used", "small_loaded", "rows_loaded", "wdn_loaded",
                     "shift_done", "s5_tables", "s5_b", "s5_c", "s5_w", "s5_n", "s5_x", "s5_y", "s5_z", "s5_g",
                     "s5_sq", "hT_s5", "lr_ready", "rw_kk", "rw_sq", "rw_gram_in", "rw_T", "rw_state", "rw_ysq",
                     "rw_bonus", "hT_rw", "attn_max", "attn_p", "attn_rs", "hT_da", "rope_done", "ln_var", "ln_rstd",
                     "ln_hat", "ln_out", "ca_max", "ca_p", "ffn_a", "ffn_c", "ffn_s", "sheets", "lam_in", "lam_exp",
                     "lam_row", "s5_col_v", "s5_col_a"):
            ev(name)

        def new_segment():
            for one in S.values():
                one.n = 0

        def raises(name):
            S[name].n += 1
            return S[name].h, 1

        def latest(name):
            return S[name].h, S[name].n

        def bank(g):
            return banks[groups[g][0]]

        def fills(g):
            return S[f"bank{groups[g][0]}_filled"].h, 1

        def filled(g):
            return S[f"bank{groups[g][0]}_filled"].h, groups[g][1] + 1

        def empties(g):
            return S[f"bank{groups[g][0]}_emptied"].h, 1

        def emptied(g):
            return S[f"bank{groups[g][0]}_emptied"].h, groups[g][1] + 1

        def free_for(g):
            return S[f"bank{groups[g][0]}_emptied"].h, groups[g][1]

        def chan(w, c0, n=256):
            return ("chan", w, c0, n)

        def tok(w, k0, nk, n0):
            return ("tok", w, k0, nk, n0)

        RW0 = 3 * DA_W
        chunks = [chan("w_in", RW0 + 256 * i) for i in range(4)] + [chan("w_in", RW0 + 1024, 128)]
        chunks += [chan("w_in", 256 * i) for i in range(4)]
        chunks += [tok("w_in", 4 * i, 4, 2 * DA_W) for i in range(2)]
        chunks += [tok("w_out", 4 * i, 4, 512 * h) for h in range(2) for i in range(2)]
        chunks += [chan("ca_wq", 256 * i) for i in range(4)]
        chunks += [chan("ca_wkv", 256 * i) for i in range(4)]
        chunks += [tok("ca_wkv", 4 * i, 4, D + 512 * h) for h in range(2) for i in range(2)]
        chunks += [tok("ca_wo", 4 * i, 4, 512 * h) for h in range(2) for i in range(2)]
        for i in range(FT // 2):
            chunks += [chan("ffn_w_up", 256 * i), chan("ffn_w_up", D_FF + 256 * i)]
        chunks += [tok("ffn_w_down", 4 * i, min(4, FT - 4 * i), 0) for i in range(6)]

        def slot(c):
            v = ring[:, c % RING, :]
            kind = chunks[c]
            if kind[0] == "chan":
                return v[:, 0:8 * kind[3]].rearrange("p (k n) -> p k n", n=kind[3])
            return v[:, 0:kind[3] * 512].rearrange("p (k n) -> p k n", n=512)

        groups = {}
        used = {}
        block = ctx.enter_context(nc.Block())

        def layers(eng, name, prologue, body):
            def rest():
                eng.drain().then_inc(quiet.h, 1)
                eng.wait_ge(go[name].h, 1)
                eng.sem_clear(go[name].h)

            new_segment()
            prologue()
            rest()
            with eng.Fori(0, DEPTH) as l:
                new_segment()
                body(l)
                rest()

        @block.tensor
        def _(pe):
            state = {}

            def fresh():
                state.update(rot=0, long=0, uses=[0] * 8, chunk=0)

            def take_bank(g, long=False):
                b = 6 + state["long"] % 2 if long else state["rot"] % 6
                state["long" if long else "rot"] += 1
                assert g not in groups, g
                groups[g] = (b, state["uses"][b])
                state["uses"][b] += 1
                return banks[b]

            mm = nc.tensor.matmul

            def next_chunk():
                c = state["chunk"]
                state["chunk"] += 1
                return c, slot(c)

            def loaded(c):
                return S[f"slot{c % RING}_loaded"].h, 16 * (c // RING + 1)

            def used_with_group(c, g):
                used[c] = filled(g)

            def used_with_step(c):
                one = raises("chunk_used")
                used[c] = latest("chunk_used")
                return one

            def transposes(g, srcs):
                ps = take_bank(g)
                pe.wait_ge(*free_for(g))
                for i, s in enumerate(srcs):
                    ins = nc.tensor.transpose(ps[:, i * P:(i + 1) * P], s, ident)
                ins.then_inc(*fills(g))

            def to_channels(tag, t):
                for h in range(2):
                    transposes(f"{tag}{t}{h}", [x[:, t, (4 * h + i) * P:(4 * h + i + 1) * P] for i in range(4)])

            def project_channels(names, rhs, n=T):
                names = list(names)
                while names:
                    c, w = next_chunk()
                    pe.wait_ge(*loaded(c))
                    for j in range(chunks[c][3] // P):
                        g = names.pop(0)
                        ps = take_bank(g)
                        pe.wait_ge(*free_for(g))
                        for k in range(KT):
                            ins = mm(ps[:, 0:n], w[:, k, j * P:(j + 1) * P], rhs[:, k, :], start=k == 0, stop=k == KT - 1)
                        ins.then_inc(*fills(g))
                    used_with_group(c, g)

            def project_tokens_resident(tag, lhs, weights):
                for t in range(NT):
                    for h in range(2):
                        g = f"{tag}{t}{h}"
                        ps = take_bank(g)
                        pe.wait_ge(*free_for(g))
                        for k in range(KT):
                            ins = mm(ps[:, :], lhs[:, k, t * P:(t + 1) * P], weights(h, k), start=k == 0, stop=k == KT - 1)
                        ins.then_inc(*fills(g))
                return g

            def four_chunks(tag, lhs):
                cs = [next_chunk() for _ in range(4)]
                for c, _ in cs:
                    pe.wait_ge(*loaded(c))
                g = project_tokens_resident(tag, lhs, lambda h, k: cs[2 * h + k // 4][1][:, k % 4, :])
                for c, _ in cs:
                    used_with_group(c, g)

            def prologue():
                fresh()
                pe.wait_ge(S["small_loaded"].h, 16 * 6)
                for m in range(MT):
                    for h in range(2):
                        transposes(f"mem{m}{h}", [memtok[:, m, (4 * h + i) * P:(4 * h + i + 1) * P] for i in range(4)])

            def s5_main(j):
                ct, jj = j // 4, j % 4
                pe.wait_ge(S["s5_b"].h, j + 1)
                ps = take_bank(f"bT{j}")
                pe.wait_ge(*free_for(f"bT{j}"))
                for i in range(2):
                    ins = nc.tensor.transpose(ps[:, i * P:(i + 1) * P], bpad[:, i, :], ident)
                ins.then_inc(*fills(f"bT{j}"))
                pe.wait_ge(*emptied(f"bT{j}"))
                for i in range(2):
                    ps = take_bank(f"bu{j}{i}")
                    pe.wait_ge(*free_for(f"bu{j}{i}"))
                    mm(ps[:, :], bT[:, i, :], uT[:, ct, :], start=True, stop=True).then_inc(*fills(f"bu{j}{i}"))

            def s5_out(j):
                ct, jj = j // 4, j % 4
                if jj == 0:
                    state["y"] = take_bank(f"y{ct}", long=True)
                    pe.wait_ge(*free_for(f"y{ct}"))
                pe.wait_ge(S["s5_x"].h, 2 * (j + 1))
                pe.wait_ge(S["s5_c"].h, j + 1)
                for i in range(2):
                    ins = mm(state["y"][:, :], cpad[:, i, :], s_x[i], start=jj == 0 and i == 0, stop=jj == 3 and i == 1)
                if jj == 3:
                    ins.then_inc(*fills(f"y{ct}"))
                else:
                    ins.then_inc(S["s5_y"].h, 1)

            def s5_tail():
                pe.wait_ge(S["s5_z"].h, 2)
                for n in range(2):
                    ps = take_bank(f"glu{n}")
                    pe.wait_ge(*free_for(f"glu{n}"))
                    for k in range(2):
                        ins = mm(ps[:, :], gluw[:, k, n * P:(n + 1) * P], zT[:, k, :], start=k == 0, stop=k == 1)
                    ins.then_inc(*fills(f"glu{n}"))
                pe.wait_ge(S["s5_sq"].h, 1)
                ps = take_bank("s5ss")
                pe.wait_ge(*free_for("s5ss"))
                for k in range(2):
                    ins = mm(ps[:, :], ones, s_r[:, k, :], start=k == 0, stop=k == 1)
                ins.then_inc(*fills("s5ss"))

            def attention():
                todo = [(h, i) for h in range(DA_HEADS) for i in range(NT)]

                def scores(n):
                    h, i = todo[n]
                    for s in range(2):
                        g = f"sc{h}{i}{s}"
                        ps = take_bank(g)
                        pe.wait_ge(*free_for(g))
                        r = slice(64 * s, 64 * s + 64)
                        mm(ps[:, 0:(i + 1) * P], qT[r, h, i * P:(i + 1) * P], kT[r, h, 0:(i + 1) * P], start=True, stop=False)
                        ins = mm(ps[:, i * P + 64:(i + 1) * P], K[0:1, C_MROW:C_MROW + P], K[0:1, C_NEG:C_NEG + CH],
                                 start=False, stop=True)
                        ins.then_inc(*fills(g))

                def weights(n):
                    h, i = todo[n]
                    pe.wait_ge(S["attn_p"].h, n + 1)
                    transposes(f"aT{h}{i}", [AP_[:, 2 * (n % 2), b * P:(b + 1) * P] for b in range(i + 1)])
                    if i == NT - 1:
                        for ii in range(NT):
                            pe.wait_ge(*emptied(f"aT{h}{ii}"))
                        ps = take_bank(f"o{h}")
                        pe.wait_ge(*free_for(f"o{h}"))
                        for b in range(NT):
                            ins = mm(ps[:, b * P:T], vtok[:, b, h * P:(h + 1) * P], aT[:, b, b * P:T], start=b == 0, stop=b == NT - 1)
                        ins.then_inc(*fills(f"o{h}"))

                def norm(h):
                    pe.wait_ge(*emptied(f"o{h}"))
                    ps = take_bank(f"oss{h}")
                    pe.wait_ge(*free_for(f"oss{h}"))
                    mm(ps[:, :], ones, osq, start=True, stop=True).then_inc(*fills(f"oss{h}"))

                for n in range(len(todo) + 1):
                    if n < len(todo):
                        scores(n)
                    if n:
                        weights(n - 1)
                        if (n - 1) % NT == 1 and (n - 1) // NT:
                            norm((n - 1) // NT - 1)
                norm(DA_HEADS - 1)

            def rwkv(j):
                if j == 0:
                    pe.wait_ge(S["lr_ready"].h, 3)
                for nm, r in (("w", slice(0, 32)), ("a", slice(32, 64)), ("g", slice(64, 128))):
                    g = f"lr{nm}{j}"
                    ps = take_bank(g)
                    pe.wait_ge(*free_for(g))
                    mm(ps[:, :], lrw[r, j * P:(j + 1) * P], rw["LR"][r, :], start=True, stop=True).then_inc(*fills(g))
                pe.wait_ge(S["rw_sq"].h, 2 * j + 1)
                ps = take_bank(f"kss{j}")
                pe.wait_ge(*free_for(f"kss{j}"))
                mm(ps[:, :], bones, rw["t1"], start=True, stop=True).then_inc(*fills(f"kss{j}"))
                pe.wait_ge(S["rw_bonus"].h, j + 1)
                ps = take_bank(f"bon{j}")
                pe.wait_ge(*free_for(f"bon{j}"))
                mm(ps[:, :], bones, rw["bonus"], start=True, stop=True).then_inc(*fills(f"bon{j}"))
                pe.wait_ge(S["rw_gram_in"].h, j + 1)
                for nm, src in (("A", rw["A"]), ("v", PR[:, 4 + j, 2:]), ("Bh", rw["Bh"]), ("Kh", rw["Kh"])):
                    transposes(f"tk{nm}{j}", [src[:, i * P:(i + 1) * P] for i in range(NT)])
                if j == 0:
                    pe.wait_ge(S["hT_da"].h, DA_HEADS)
                for hh in range(2):
                    r = slice(64 * hh, 64 * hh + 64)
                    for nm, a, b in (("ABT", "B", "A"), ("AB", "A", "B"), ("RBT", "B", "R"), ("RKT", "K", "R"), ("AKT", "K", "A")):
                        g = f"gr{nm}{j}{hh}"
                        ps = take_bank(g)
                        pe.wait_ge(*free_for(g))
                        for i in range(NT):
                            c = slice(i * P, (i + 1) * P)
                            ins = mm(ps[:, c], rw[a][r, c], rw[b][r, c], start=True, stop=True)
                        ins.then_inc(*fills(g))
                for lv in range(len(LEVELS)):
                    for hh in range(2):
                        for nm in ("T", "TT"):
                            if lv:
                                pe.wait_ge(*emptied(f"d{nm}{j}{lv - 1}{hh}"))
                    if lv == 0:
                        pe.wait_ge(S["rw_T"].h, 4 * (j + 1))
                    for hh in range(2):
                        g = f"Z{j}{lv}{hh}"
                        ps = take_bank(g)
                        pe.wait_ge(*free_for(g))
                        for i in range(NT):
                            c = slice(i * P, (i + 1) * P)
                            ins = mm(ps[:, c], mAB[:, hh, c], Ti[:, hh, c], start=True, stop=True)
                        ins.then_inc(*fills(g))
                    for hh in range(2):
                        pe.wait_ge(*emptied(f"Z{j}{lv}{hh}"))
                        for nm, a, b in (("T", TiT, rZ), ("TT", rZ, TiT)):
                            g = f"d{nm}{j}{lv}{hh}"
                            ps = take_bank(g)
                            pe.wait_ge(*free_for(g))
                            for i in range(NT):
                                c = slice(i * P, (i + 1) * P)
                                ins = mm(ps[:, c], a[:, hh, c], b[:, hh, c], start=True, stop=True)
                            ins.then_inc(*fills(g))
                for hh in range(2):
                    for nm in ("RBT", "RKT", "AKT"):
                        pe.wait_ge(*emptied(f"gr{nm}{j}{hh}"))
                for nm in ("v", "Bh", "Kh"):
                    pe.wait_ge(*emptied(f"tk{nm}{j}"))
                for hh in range(2):
                    g = f"MV{j}{hh}"
                    ps = take_bank(g)
                    pe.wait_ge(*free_for(g))
                    for i in range(NT):
                        ins = mm(ps[:, i * CH:(i + 1) * CH], mAK[:, hh, i * P:(i + 1) * P], vT_[:, i, 64 * hh:64 * hh + 64],
                                 start=True, stop=True)
                    ins.then_inc(*fills(g))
                for hh in range(2):
                    pe.wait_ge(*emptied(f"dT{j}{len(LEVELS) - 1}{hh}"))
                    pe.wait_ge(*emptied(f"dTT{j}{len(LEVELS) - 1}{hh}"))
                for hh in range(2):
                    pe.wait_ge(*emptied(f"MV{j}{hh}"))
                    pe.wait_ge(*emptied(f"tkA{j}"))
                    g = f"UW{j}{hh}"
                    ps = take_bank(g)
                    pe.wait_ge(*free_for(g))
                    for i in range(NT):
                        c = slice(i * P, (i + 1) * P)
                        ins = mm(ps[:, c], TiT[:, hh, c], zA[:, hh, c], start=True, stop=True)
                    ins.then_inc(*fills(g))
                for hh in range(2):
                    pe.wait_ge(*emptied(f"UW{j}{hh}"))

                def U(hh, i, rows=slice(0, P)):
                    return uw[rows, hh, i * P:i * P + CH]

                def W(hh, i, rows=slice(0, P)):
                    return uw[rows, hh, i * P + CH:(i + 1) * P]

                ps = take_bank(f"Q{j}")
                pe.wait_ge(*free_for(f"Q{j}"))
                for hh in range(2):
                    for i in range(NT):
                        c = slice(i * P, (i + 1) * P)
                        ins = mm(ps[64 * hh:64 * hh + 64, c], W(hh, i), mRB[:, hh, c], start=True, stop=True)
                ins.then_inc(*fills(f"Q{j}"))
                for par in range(2):
                    rows = slice(64 * par, 64 * par + 64)
                    g = f"GH{j}{par}"
                    ps = take_bank(g)
                    pe.wait_ge(*free_for(g))
                    for hh in range(2):
                        out = slice(64 * hh, 64 * hh + 64)
                        hc = slice(64 * hh, 64 * hh + 64)
                        for i in range(NT):
                            mm(ps[out, i * CH:(i + 1) * CH], W(hh, i, rows), bT_[rows, i, hc], start=True, stop=True)
                        for i in range(NT):
                            c = slice(256 + i * CH, 256 + (i + 1) * CH)
                            mm(ps[out, c], bT_[rows, i, hc], U(hh, i, rows), start=True, stop=False)
                            ins = mm(ps[out, c], kT_[rows, i, hc], vT_[rows, i, hc], start=False, stop=True)
                    ins.then_inc(*fills(g))
                for par in range(2):
                    pe.wait_ge(*emptied(f"GH{j}{par}"))
                pe.wait_ge(S["rw_state"].h, j + 1)
                for c in range(1, NCH - 1):
                    for hh in range(2):
                        r = slice(64 * hh, 64 * hh + 64)
                        g = f"S{j}{c}{hh}"
                        ps = take_bank(g)
                        pe.wait_ge(*free_for(g))
                        mm(ps[r, 0:CH], rG[r, c * CH:(c + 1) * CH], rS[r, c * CH:(c + 1) * CH], start=True, stop=True).then_inc(*fills(g))
                    for hh in range(2):
                        pe.wait_ge(*emptied(f"S{j}{c}{hh}"))
                pe.wait_ge(*emptied(f"Q{j}"))
                for hh in range(2):
                    r = slice(64 * hh, 64 * hh + 64)
                    g = f"Y{j}{hh}"
                    ps = take_bank(g)
                    pe.wait_ge(*free_for(g))
                    for i in range(NT):
                        c = slice(i * P, (i + 1) * P)
                        mm(ps[r, c], U(hh, i), mRB[:, hh, c], start=i == 0, stop=False, skip_group_check=True)
                        mm(ps[r, c], vT_[:, i, r], mRK[:, hh, c], start=False, stop=False, skip_group_check=True)
                    for c in range(1, NCH):
                        cc = slice(c * CH, (c + 1) * CH)
                        ins = mm(ps[r, cc], rS[r, cc], rQ[r, cc], start=False, stop=c == NCH - 1, skip_group_check=True)
                    ins.then_inc(*fills(g))
                for hh in range(2):
                    pe.wait_ge(*emptied(f"Y{j}{hh}"))
                ps = take_bank(f"ym{j}")
                pe.wait_ge(*free_for(f"ym{j}"))
                mm(ps[:, :], bones, rY, start=True, stop=True).then_inc(*fills(f"ym{j}"))
                pe.wait_ge(S["rw_ysq"].h, j + 1)
                ps = take_bank(f"yv{j}")
                pe.wait_ge(*free_for(f"yv{j}"))
                mm(ps[:, :], bones, rw["t1"], start=True, stop=True).then_inc(*fills(f"yv{j}"))

            def cross():
                todo = [(h, i) for h in range(MEM_HEADS) for i in range(NT)]

                def scores(n):
                    h, i = todo[n]
                    g = f"cs{h}{i}"
                    ps = take_bank(g)
                    pe.wait_ge(*free_for(g))
                    for k in range(2):
                        ins = mm(ps[:, 0:N_MEM], q2[:, 2 * h + k, i * P:(i + 1) * P], mK[:, 2 * h + k, :], start=k == 0, stop=k == 1)
                    ins.then_inc(*fills(g))

                def weights(n):
                    h, i = todo[n]
                    pe.wait_ge(S["ca_p"].h, n + 1)
                    transposes(f"pT{h}{i}", [p2[:, n % 2, m * P:(m + 1) * P] for m in range(MT)])
                    if i == NT - 1:
                        for ii in range(NT):
                            pe.wait_ge(*emptied(f"pT{h}{ii}"))
                        for d in range(2):
                            g = f"co{h}{d}"
                            ps = take_bank(g)
                            pe.wait_ge(*free_for(g))
                            for m in range(MT):
                                ins = mm(ps[:, :], mV[:, m, (2 * h + d) * P:(2 * h + d + 1) * P], pT2[:, m, :], start=m == 0, stop=m == 1)
                            ins.then_inc(*fills(g))

                for n in range(len(todo) + 1):
                    if n < len(todo):
                        scores(n)
                    if n:
                        weights(n - 1)

            def body(l):
                fresh()
                for t in range(NT):
                    to_channels("x0", t)
                pe.wait_ge(S["sheets"].h, 1)
                for i, n in enumerate((S1_N, S2_N, 24)):
                    ps = take_bank(f"sheet{i}")
                    pe.wait_ge(*free_for(f"sheet{i}"))
                    nc.tensor.transpose(ps[:, 0:n], sheet[0:n, i, :], ident[0:n, 0:n]).then_inc(*fills(f"sheet{i}"))
                ps = take_bank("cT")
                pe.wait_ge(*free_for("cT"))
                for i in range(2):
                    for ct in range(2):
                        ins = nc.tensor.transpose(ps[:, (2 * i + ct) * P:(2 * i + ct + 1) * P], cn[:, i, ct, :], ident)
                ins.then_inc(*fills("cT"))
                pe.wait_ge(S["lam_row"].h, 1)
                ps = take_bank("lam")
                pe.wait_ge(*free_for("lam"))
                mm(ps[:, 0:2], ones[0:1, :], lamr[0:1, 4, 0:2], start=True, stop=True).then_inc(*fills("lam"))
                for t in range(NT):
                    for h in range(2):
                        pe.wait_ge(*emptied(f"x0{t}{h}"))
                for nm in ("sheet0", "sheet1", "sheet2", "lam"):
                    pe.wait_ge(*emptied(nm))
                project_channels([f"rw{i}" for i in range(RW_TILES)] + ["u0", "u1"], xT)
                project_channels([f"q{i}" for i in range(4)] + [f"k{i}" for i in range(4)], xT)
                for i in range(8):
                    nm = f"{'qk'[i // 4]}{i % 4}"
                    pe.wait_ge(*emptied(nm))
                    ps = take_bank(f"rot{i}")
                    pe.wait_ge(*free_for(f"rot{i}"))
                    mm(ps[:, :], rot, (qT if i < 4 else kT)[:, i % 4, :], start=True, stop=True).then_inc(*fills(f"rot{i}"))
                vs = [take_bank(f"v{t}") for t in range(NT)]
                for t in range(NT):
                    pe.wait_ge(*free_for(f"v{t}"))
                for half in range(2):
                    c, w = next_chunk()
                    pe.wait_ge(*loaded(c))
                    for t in range(NT):
                        for k in range(4):
                            kk = 4 * half + k
                            ins = mm(vs[t][:, :], xT[:, kk, t * P:(t + 1) * P], w[:, k, :], start=kk == 0, stop=kk == KT - 1)
                        if half:
                            ins.then_inc(*fills(f"v{t}"))
                    if half:
                        used_with_group(c, f"v{NT - 1}")
                    else:
                        ins.then_inc(*used_with_step(c))
                pe.wait_ge(*emptied("u0"))
                pe.wait_ge(*emptied("u1"))
                for j in range(S5_TILES):
                    s5_main(j)
                    s5_out(j)
                s5_tail()
                for t in range(NT):
                    pe.wait_ge(*emptied(f"v{t}"))
                pe.wait_ge(S["rope_done"].h, 8)
                attention()
                for j in range(2):
                    rwkv(j)
                pe.wait_ge(S["hT_s5"].h, 2)
                pe.wait_ge(S["hT_da"].h, DA_HEADS)
                pe.wait_ge(S["hT_rw"].h, 2)
                four_chunks("wo", hT)
                for t in range(NT):
                    pe.wait_ge(S["ln_out"].h, t + 1)
                    to_channels("x1", t)
                for t in range(NT):
                    for h in range(2):
                        pe.wait_ge(*emptied(f"x1{t}{h}"))
                project_channels([f"cq{i}" for i in range(KT)], xT)
                project_channels([f"mk{i}" for i in range(KT)], memT, N_MEM)
                for h in range(2):
                    vs = [take_bank(f"mv{m}{h}") for m in range(MT)]
                    for m in range(MT):
                        pe.wait_ge(*free_for(f"mv{m}{h}"))
                    for half in range(2):
                        c, w = next_chunk()
                        pe.wait_ge(*loaded(c))
                        for m in range(MT):
                            for k in range(4):
                                kk = 4 * half + k
                                ins = mm(vs[m][:, :], memT[:, kk, m * P:(m + 1) * P], w[:, k, :], start=kk == 0, stop=kk == KT - 1)
                            if half:
                                ins.then_inc(*fills(f"mv{m}{h}"))
                        if half:
                            used_with_group(c, f"mv1{h}")
                        else:
                            ins.then_inc(*used_with_step(c))
                for i in range(KT):
                    pe.wait_ge(*emptied(f"cq{i}"))
                    pe.wait_ge(*emptied(f"mk{i}"))
                for m in range(MT):
                    pe.wait_ge(*emptied(f"mv{m}0"))
                    pe.wait_ge(*emptied(f"mv{m}1"))
                cross()
                for h in range(MEM_HEADS):
                    pe.wait_ge(*emptied(f"co{h}0"))
                    pe.wait_ge(*emptied(f"co{h}1"))
                four_chunks("cw", o2)
                for t in range(NT):
                    pe.wait_ge(S["ln_out"].h, NT + t + 1)
                    to_channels("x2", t)
                for t in range(NT):
                    for h in range(2):
                        pe.wait_ge(*emptied(f"x2{t}{h}"))
                names = []
                for i in range(FT // 2):
                    names += [f"fa{2 * i}", f"fa{2 * i + 1}", f"fg{2 * i}", f"fg{2 * i + 1}"]
                project_channels(names, xT)
                for i in range(FT):
                    pe.wait_ge(*emptied(f"fg{i}"))
                ds = [take_bank(f"dn{t}0") for t in range(NT)]
                for t in range(NT):
                    pe.wait_ge(*free_for(f"dn{t}0"))
                for i in range(6):
                    c, w = next_chunk()
                    pe.wait_ge(*loaded(c))
                    for t in range(NT):
                        for k in range(chunks[c][3]):
                            kk = 4 * i + k
                            ins = mm(ds[t][:, :], hid[:, kk, t * P:(t + 1) * P], w[:, k, :], start=kk == 0, stop=kk == FT - 1)
                        if i == 5:
                            ins.then_inc(*fills(f"dn{t}0"))
                    if i == 5:
                        used_with_group(c, f"dn{NT - 1}0")
                    else:
                        ins.then_inc(*used_with_step(c))
                pe.wait_ge(S["wdn_loaded"].h, 32)
                for t in range(NT):
                    g = f"dn{t}1"
                    ps = take_bank(g)
                    pe.wait_ge(*free_for(g))
                    for k in range(FT):
                        ins = mm(ps[:, :], hid[:, k, t * P:(t + 1) * P], wdn[:, k, :], start=k == 0, stop=k == FT - 1)
                    ins.then_inc(*fills(g))

            layers(pe, "pe", prologue, body)

        small = {}

        @block.sync
        def _(sp):
            def rest():
                sp.wait_ge(quiet.h, 4)
                sp.sem_clear(quiet.h)
                nums = sorted(s.h.num for s in S.values())
                assert nums == list(range(nums[0], nums[-1] + 1))
                sp.sem_clear(range(nums[0], nums[-1] + 1))
                for n in go:
                    sp.sem_inc(go[n].h, 1)

            def load(dst, src):
                sp.dma_start(dst, src).then_inc(S["small_loaded"].h, 16)
                S["small_loaded"].n += 16

            new_segment()
            load(K[:, :], io["const"])
            load(lev[:, :, :, :], io["level_masks"])
            load(memtok, io["mem"][0].rearrange("(m p) d -> p m d", p=P))
            load(posr.bitcast(i32), io["positions"].to_broadcast([P, T]))
            for h in range(2):
                load(x[:, 2 * h:2 * h + 2, :], io["x"][0, 2 * h * P:(2 * h + 2) * P, :].rearrange("(t p) d -> p t d", p=P))
            rest()
            with sp.Fori(0, DEPTH) as l:
                new_segment()

                def layer_chunk(c):
                    kind = chunks[c]
                    w = io[kind[1]][l]
                    if kind[0] == "chan":
                        return w[:, kind[2]:kind[2] + kind[3]].rearrange("(k p) n -> p k n", p=P)
                    k0, nk, n0 = kind[2:]
                    return w[k0 * P:(k0 + nk) * P, n0:n0 + 512].rearrange("(k p) n -> p k n", p=P)

                def load_chunk(c):
                    if c >= RING:
                        sp.wait_ge(*used[c - RING])
                    sp.dma_start(slot(c), layer_chunk(c)).then_inc(S[f"slot{c % RING}_loaded"].h, 16)

                load(sheet[0:S1["ffn_conv_w"][1], 0, :], io["ffn_conv_w"][l].rearrange("j (c p) -> (j c) p", p=P))
                load(sheet[S1["ffn_conv_b"][0]:S1_N, 0, :], io["ffn_conv_b"][l].rearrange("(c p) -> c p", p=P))
                for name, (at, n) in S2.items():
                    src = io[name][l]
                    if name == "rw_r_k":
                        src = src.rearrange("(c a) d -> c (a d)", a=2)
                    else:
                        src = src.rearrange("(c p) -> c p", p=P)
                    load(sheet[at:at + n, 1, :], src)
                load(sheet[8:16, 2, :], io["s5_a_re"][l].rearrange("(j a) p -> j (a p)", a=2))
                load(sheet[16:24, 2, :], io["s5_a_im"][l].rearrange("(j a) p -> j (a p)", a=2))
                load(lamr[0:8, 5, 0:2], io["s5_log_step"][l].rearrange("(j a) -> j a", a=2))
                for i, name in enumerate(("da_lam_q1", "da_lam_k1", "da_lam_q2", "da_lam_k2")):
                    load(lamr[0:1, i, :], io[name][l].unsqueeze(0))
                load(lamr[0:1, 4, 2:4], io["lambda_inits"][l].unsqueeze(0))
                load_chunk(0)
                load(lrw[0:32, :], io["rw_w2"][l])
                load(lrw[32:64, :], io["rw_a2"][l])
                load(lrw[64:128, :], io["rw_g2"][l])
                for i, nm in enumerate(("re", "im")):
                    load(bn[:, i, :, :], io[f"s5_b_{nm}"][l].rearrange("(j a) p h -> (a p) j h", a=2))
                    for dup in range(2):
                        load(cn[:, i, :, dup * 64:dup * 64 + 64], io[f"s5_c_{nm}"][l].rearrange("(c g) h p -> (g h) c p", c=2))
                load(gluw, io["s5_glu_w"][l].rearrange("(k p) n -> p k n", p=P))
                small["layer"] = S["small_loaded"].n
                for c in range(1, len(chunks)):
                    load_chunk(c)
                rest()
            for h in range(2):
                sp.dma_start(io["out"][0, 2 * h * P:(2 * h + 2) * P, :].rearrange("(t p) d -> p t d", p=P),
                             x[:, 2 * h:2 * h + 2, :]).then_inc(out_done.h, 16)
            sp.wait_ge(out_done.h, 32)

        @block.scalar
        def _(act):
            A = nc.scalar.activation

            def prologue():
                for m in range(MT):
                    for h in range(2):
                        act.wait_ge(*filled(f"mem{m}{h}"))
                        ps = bank(f"mem{m}{h}")
                        A(memT[:, 4 * h:4 * h + 4, m * P:(m + 1) * P], ps[:, :].rearrange("p (k t) -> p k t", k=4), ACT.Copy).then_inc(*empties(f"mem{m}{h}"))
                        act.wait_ge(*emptied(f"mem{m}{h}"))
                act.wait_ge(S["s5_col_v"].h, 1)
                A(ropeS[:, :], tr, ACT.Sin).then_inc(*raises("act_step"))
                act.wait_ge(*latest("act_step"))
                A(tn, tr, ACT.Abs).then_inc(*raises("act_step"))
                act.wait_ge(*latest("act_step"))
                A(ropeC[:, :], tn, ACT.Sin, bias=const("half_pi"), scale=-1.0).then_inc(*raises("act_step"))
                act.wait_ge(*latest("act_step"))

            def body(l):

                def rows(n):
                    if n > 1:
                        act.wait_ge(S["ln_out"].h, NT * (n - 1))
                    for i, nm in enumerate("gb"):
                        act.dma_start(lnrow[:, i, :], io[f"ln{n}_{nm}"][l].unsqueeze(0).to_broadcast([P, D])).then_inc(S["rows_loaded"].h, 16)

                def copy_out(g, dst, n=T):
                    act.wait_ge(*filled(g))
                    ps = bank(g)
                    A(dst, ps[:, 0:n], ACT.Copy).then_inc(*empties(g))
                    act.wait_ge(*emptied(g))

                def channels_out(tag, t):
                    for h in range(2):
                        g = f"{tag}{t}{h}"
                        act.wait_ge(*filled(g))
                        ps = bank(g)
                        A(xT[:, 4 * h:4 * h + 4, t * P:(t + 1) * P], ps[:, :].rearrange("p (k t) -> p k t", k=4), ACT.Copy).then_inc(*empties(g))
                        act.wait_ge(*emptied(g))

                def layer_norm(n, t):
                    act.wait_ge(S["ln_var"].h, NT * n + t + 1)
                    v = stat[:, t % 2, 1:2]
                    A(v, v, ACT.Ln, bias=const("ln_eps")).then_inc(*raises("act_step"))
                    act.wait_ge(*latest("act_step"))
                    A(v, v, ACT.Exp, scale=-0.5).then_inc(*raises("ln_rstd"))
                    act.wait_ge(*latest("ln_rstd"))

                rows(1)
                for t in range(NT):
                    channels_out("x0", t)
                act.wait_ge(S["lam_in"].h, 1)
                A(lamr[0:1, 4, 4:6], lamr[0:1, 4, 6:8], ACT.Exp).then_inc(*raises("lam_exp"))
                act.wait_ge(*latest("lam_exp"))
                act.wait_ge(S["s5_col_v"].h, 1)
                A(s5c[:, 0, :], col3[:, 0:8], ACT.Exp).then_inc(*raises("s5_col_a"))
                act.wait_ge(*latest("s5_col_a"))
                act.wait_ge(S["s5_col_v"].h, 2)
                A(s5c[:, 3, :], s5c[:, 1, :], ACT.Exp).then_inc(*raises("s5_col_a"))
                act.wait_ge(*latest("s5_col_a"))
                A(s5c[:, 8, :], s5c[:, 5, :], ACT.Sin).then_inc(*raises("act_step"))
                act.wait_ge(*latest("act_step"))
                A(s5c[:, 9, :], s5c[:, 5, :], ACT.Abs).then_inc(*raises("act_step"))
                act.wait_ge(*latest("act_step"))
                A(s5c[:, 9, :], s5c[:, 9, :], ACT.Sin, bias=const("half_pi"), scale=-1.0).then_inc(*raises("s5_col_a"))
                act.wait_ge(*latest("s5_col_a"))
                act.wait_ge(*filled("cT"))
                ps = bank("cT")
                A(cT[:, 0:2, :], ps[:, 0:2 * P].rearrange("p (a b) -> p a b", a=2), ACT.Copy).then_inc(*raises("act_step"))
                act.wait_ge(*latest("act_step"))
                A(cT[:, 2:4, :], ps[:, 2 * P:].rearrange("p (a b) -> p a b", a=2), ACT.Copy, scale=-1.0).then_inc(*empties("cT"))
                act.wait_ge(*emptied("cT"))
                for i in range(RW_TILES):
                    copy_out(f"rw{i}", PR[:, i, 2:T + 2])
                copy_out("u0", uT[:, 0, :])
                copy_out("u1", uT[:, 1, :])
                for i in range(8):
                    copy_out(f"{'qk'[i // 4]}{i % 4}", (qT if i < 4 else kT)[:, i % 4, :])
                for t in range(NT):
                    copy_out(f"v{t}", vtok[:, t, :])
                for j in range(S5_TILES):
                    act.wait_ge(S["s5_tables"].h, j + 1)
                    if j:
                        act.wait_ge(S["s5_n"].h, 4 * j)
                    A(s_s, s_z[0], ACT.Sin, scale=TWO_PI_SAFE).then_inc(*raises("act_step"))
                    act.wait_ge(*latest("act_step"))
                    A(s_z[1], s_z[0], ACT.Abs).then_inc(*raises("act_step"))
                    act.wait_ge(*latest("act_step"))
                    A(s_c, s_z[1], ACT.Sin, bias=const("half_pi"), scale=-TWO_PI_SAFE).then_inc(*raises("s5_col_a"))
                    act.wait_ge(*latest("s5_col_a"))
                    act.wait_ge(*filled(f"bT{j}"))
                    ps = bank(f"bT{j}")
                    A(bT, ps[:, 0:2 * P].rearrange("p (a b) -> p a b", a=2), ACT.Copy).then_inc(*empties(f"bT{j}"))
                    act.wait_ge(*emptied(f"bT{j}"))
                for ct in range(2):
                    act.wait_ge(*emptied(f"y{ct}"))
                    A(zT[:, ct, :], yT[:, ct, :], ACT.Gelu_apprx_tanh).then_inc(*raises("s5_z"))
                    act.wait_ge(*latest("s5_z"))
                for n in range(2):
                    act.wait_ge(*filled(f"glu{n}"))
                    ps = bank(f"glu{n}")
                    A(s_r[:, n, :], ps[:, :], ACT.Sigmoid, bias=col2[:, S2["s5_glu_b"][0] + n:S2["s5_glu_b"][0] + n + 1]).then_inc(*empties(f"glu{n}"))
                    act.wait_ge(*emptied(f"glu{n}"))
                act.wait_ge(S["s5_g"].h, 2)
                A(s_r, zT, ACT.Square).then_inc(*raises("s5_sq"))
                act.wait_ge(*latest("s5_sq"))
                act.wait_ge(*filled("s5ss"))
                ps = bank("s5ss")
                A(yT[:, 0, :], ps[:, :], ACT.Ln, bias=const("rms_eps"), scale=1.0 / S5_W).then_inc(*raises("act_step"))
                act.wait_ge(*latest("act_step"))
                A(yT[:, 1, :], yT[:, 0, :], ACT.Exp, scale=-0.5).then_inc(*empties("s5ss"))
                act.wait_ge(*emptied("s5ss"))
                def attn_head_out(h):
                    act.wait_ge(*filled(f"o{h}"))
                    ps = bank(f"o{h}")
                    if h:
                        act.wait_ge(S["hT_da"].h, h)
                    A(oh, ps[:, :], ACT.Copy).then_inc(*raises("act_step"))
                    act.wait_ge(*latest("act_step"))
                    A(osq, ps[:, :], ACT.Square).then_inc(*empties(f"o{h}"))
                    act.wait_ge(*emptied(f"o{h}"))

                def attn_head_norm(h):
                    act.wait_ge(*filled(f"oss{h}"))
                    ps = bank(f"oss{h}")
                    A(orr, ps[:, :], ACT.Ln, bias=const("rms_eps"), scale=1.0 / P).then_inc(*empties(f"oss{h}"))
                    act.wait_ge(*emptied(f"oss{h}"))
                    A(orr, orr, ACT.Exp, scale=-0.5).then_inc(*raises("attn_rs"))
                    act.wait_ge(*latest("attn_rs"))

                def attn_weights_out(n):
                    h, i = n // NT, n % NT
                    g = f"aT{h}{i}"
                    act.wait_ge(*filled(g))
                    ps = bank(g)
                    if h:
                        act.wait_ge(*filled(f"o{h - 1}"))
                    A(aT[:, 0:i + 1, i * P:(i + 1) * P], ps[:, 0:(i + 1) * P].rearrange("p (a b) -> p a b", a=i + 1), ACT.Copy).then_inc(*empties(g))
                    act.wait_ge(*emptied(g))

                for n in range(DA_HEADS * NT + 1):
                    h, i = n // NT, n % NT
                    if n < DA_HEADS * NT:
                        for s in range(2):
                            g = f"sc{h}{i}{s}"
                            act.wait_ge(*filled(g))
                            ps = bank(g)
                            act.wait_ge(S["attn_max"].h, 2 * n + s + 1)
                            if n >= 2:
                                act.wait_ge(*filled(f"aT{(n - 2) // NT}{(n - 2) % NT}"))
                            A(AP_[:, 2 * (n % 2) + s, 0:(i + 1) * P], ps[:, 0:(i + 1) * P], ACT.Exp,
                                   bias=stat[:, n % 2, 4 + s:5 + s], scale=0.125, accum_out=stat[:, n % 2, 6 + s:7 + s]).then_inc(*empties(g))
                            act.wait_ge(*emptied(g))
                    if n:
                        attn_weights_out(n - 1)
                        if (n - 1) % NT == NT - 1:
                            attn_head_out((n - 1) // NT)
                        if (n - 1) % NT == 1 and (n - 1) // NT:
                            attn_head_norm((n - 1) // NT - 1)
                attn_head_norm(DA_HEADS - 1)
                act.wait_ge(S["shift_done"].h, 7)
                LR = rw["LR"]
                A(LR[0:32, :], PR[0:32, 6, 2:], ACT.Tanh).then_inc(*raises("lr_ready"))
                act.wait_ge(*latest("lr_ready"))
                A(LR[32:64, :], PR[32:64, 6, 2:], ACT.Copy).then_inc(*raises("lr_ready"))
                act.wait_ge(*latest("lr_ready"))
                A(LR[64:128, :], PR[64:128, 6, 2:], ACT.Sigmoid).then_inc(*raises("lr_ready"))
                act.wait_ge(*latest("lr_ready"))
                for j in range(2):
                    def c2(name):
                        return col2[:, S2[name][0] + j:S2[name][0] + j + 1]

                    if j:
                        act.wait_ge(S["hT_rw"].h, 1)
                    act.wait_ge(S["rw_kk"].h, j + 1)
                    A(rw["t1"], rw["kk"], ACT.Square).then_inc(*raises("rw_sq"))
                    act.wait_ge(*latest("rw_sq"))
                    act.wait_ge(*filled(f"lrw{j}"))
                    ps = bank(f"lrw{j}")
                    A(rw["t0"], ps[:, :], ACT.Sigmoid, bias=c2("rw_w0")).then_inc(*raises("act_step"))
                    act.wait_ge(*latest("act_step"))
                    A(rw["t0"], rw["t0"], ACT.Exp, scale=-DECAY).then_inc(*empties(f"lrw{j}"))
                    act.wait_ge(*emptied(f"lrw{j}"))
                    act.wait_ge(*filled(f"lra{j}"))
                    ps = bank(f"lra{j}")
                    A(rw["a"], ps[:, :], ACT.Sigmoid, bias=c2("rw_a0")).then_inc(*empties(f"lra{j}"))
                    act.wait_ge(*emptied(f"lra{j}"))
                    act.wait_ge(*filled(f"lrg{j}"))
                    ps = bank(f"lrg{j}")
                    A(rw["g"], ps[:, :], ACT.Copy).then_inc(*empties(f"lrg{j}"))
                    act.wait_ge(*emptied(f"lrg{j}"))
                    act.wait_ge(*emptied(f"kss{j}"))
                    A(rw["t1"], rw["t1"], ACT.Sqrt).then_inc(*raises("rw_sq"))
                    act.wait_ge(*latest("rw_sq"))
                    act.wait_ge(*filled(f"tkA{j}"))
                    ps = bank(f"tkA{j}")
                    for i in range(2):
                        copy = A(zA.rearrange("p h (t c) -> p h t c", c=P)[:, i, :, CH:],
                                 ps[:, :].rearrange("p (t c) -> p t c", c=P)[:, :, i * CH:(i + 1) * CH], ACT.Copy)
                        if i:
                            copy.then_inc(*empties(f"tkA{j}"))
                            act.wait_ge(*emptied(f"tkA{j}"))
                        else:
                            copy.then_inc(*raises("act_step"))
                            act.wait_ge(*latest("act_step"))
                    for nm, dst in (("v", vT_), ("Bh", bT_), ("Kh", kT_)):
                        act.wait_ge(*filled(f"tk{nm}{j}"))
                        ps = bank(f"tk{nm}{j}")
                        A(dst, ps[:, :].rearrange("p (t c) -> p t c", c=P), ACT.Copy).then_inc(*empties(f"tk{nm}{j}"))
                        act.wait_ge(*emptied(f"tk{nm}{j}"))
                    for lv in range(len(LEVELS)):
                        for hh in range(2):
                            g = f"Z{j}{lv}{hh}"
                            act.wait_ge(*filled(g))
                            ps = bank(g)
                            A(rZ[:, hh, :], ps[:, :], ACT.Copy).then_inc(*empties(g))
                            act.wait_ge(*emptied(g))
                    for hh in range(2):
                        g = f"MV{j}{hh}"
                        act.wait_ge(*filled(g))
                        ps = bank(g)
                        A(zA.rearrange("p h (t c) -> p h t c", c=P)[:, hh, :, 0:CH], ps[:, 0:NT * CH].rearrange("p (t c) -> p t c", c=CH), ACT.Copy).then_inc(*empties(g))
                        act.wait_ge(*emptied(g))
                    for hh in range(2):
                        copy_out(f"UW{j}{hh}", uw[:, hh, :])
                    for hh in range(2):
                        r = slice(64 * hh, 64 * hh + 64)
                        g = f"Y{j}{hh}"
                        act.wait_ge(*filled(g))
                        ps = bank(g)
                        A(rY[r, :], ps[r, :], ACT.Copy).then_inc(*empties(g))
                        act.wait_ge(*emptied(g))
                    act.wait_ge(*emptied(f"ym{j}"))
                    A(rw["t1"], rY, ACT.Square).then_inc(*raises("rw_ysq"))
                    act.wait_ge(*latest("rw_ysq"))
                    act.wait_ge(*filled(f"yv{j}"))
                    ps = bank(f"yv{j}")
                    A(rw["t1"], ps[:, :], ACT.Ln, bias=const("lnx_eps"), scale=1.0 / CH).then_inc(*raises("act_step"))
                    act.wait_ge(*latest("act_step"))
                    A(rw["t1"], rw["t1"], ACT.Exp, scale=-0.5).then_inc(*empties(f"yv{j}"))
                    act.wait_ge(*emptied(f"yv{j}"))
                for t in range(NT):
                    layer_norm(0, t)
                for t in range(NT):
                    channels_out("x1", t)
                rows(2)
                for i in range(KT):
                    copy_out(f"cq{i}", q2[:, i, :])
                for i in range(KT):
                    copy_out(f"mk{i}", mK[:, i, :], N_MEM)
                for h in range(2):
                    for m in range(MT):
                        copy_out(f"mv{m}{h}", mV[:, m, h * 512:(h + 1) * 512])
                for n in range(MEM_HEADS * NT + 1):
                    h, i = n // NT, n % NT
                    if n < MEM_HEADS * NT:
                        g = f"cs{h}{i}"
                        act.wait_ge(*filled(g))
                        ps = bank(g)
                        act.wait_ge(S["ca_max"].h, n + 1)
                        if n >= 2:
                            act.wait_ge(*filled(f"pT{(n - 2) // NT}{(n - 2) % NT}"))
                        A(p2[:, n % 2, :], ps[:, 0:N_MEM], ACT.Exp, bias=stat[:, n % 2, 9:10], scale=1.0 / 16,
                                  accum_out=stat[:, n % 2, 10:11]).then_inc(*empties(g))
                        act.wait_ge(*emptied(g))
                    if n:
                        hh, ii = (n - 1) // NT, (n - 1) % NT
                        g = f"pT{hh}{ii}"
                        act.wait_ge(*filled(g))
                        ps = bank(g)
                        if hh:
                            act.wait_ge(*filled(f"co{hh - 1}1"))
                        A(pT2[:, :, ii * P:(ii + 1) * P], ps[:, 0:2 * P].rearrange("p (a b) -> p a b", a=2), ACT.Copy).then_inc(*empties(g))
                        act.wait_ge(*emptied(g))
                        if ii == NT - 1:
                            for d in range(2):
                                copy_out(f"co{hh}{d}", o2[:, 2 * hh + d, :])
                for t in range(NT):
                    layer_norm(1, t)
                for t in range(NT):
                    channels_out("x2", t)
                rows(3)
                for i in range(2):
                    act.dma_start(wdn[:, 11 * i:11 * i + 11, :], io["ffn_w_down"][l][11 * i * P:(11 * i + 11) * P, 512:1024]
                                  .rearrange("(k p) n -> p k n", p=P)).then_inc(S["wdn_loaded"].h, 16)
                act.wait_ge(S["ffn_a"].h, 2)
                for i in range(FT + 1):
                    if i < FT:
                        g = f"fa{i}"
                        act.wait_ge(*filled(g))
                        ps = bank(g)
                        if i >= 2:
                            act.wait_ge(S["ffn_c"].h, i - 1)
                        A(fa[i % 2][:, 2:T + 2], ps[:, :], ACT.Copy).then_inc(*empties(g))
                        act.wait_ge(*emptied(g))
                    if i:
                        act.wait_ge(S["ffn_c"].h, i)
                        A(fc, fc, ACT.Silu).then_inc(*raises("ffn_s"))
                        act.wait_ge(*latest("ffn_s"))
                for t in range(NT):
                    layer_norm(2, t)

            layers(act, "act", prologue, body)

        @block.vector
        def _(dve):
            V = nc.vector
            tt, ts, stt = V.tensor_tensor, V.tensor_scalar, V.scalar_tensor_tensor
            mult, add, sub = ALU.mult, ALU.add, ALU.subtract

            def reduce_angle(dst, src, n, last):
                ts(n, src, INV_2PI, ROUND, mult, add).then_inc(*raises("dve_step"))
                dve.wait_ge(*latest("dve_step"))
                ts(n, n, ROUND, None, sub).then_inc(*raises("dve_step"))
                dve.wait_ge(*latest("dve_step"))
                hi, mid, lo = two_pi_parts()
                stt(dst, n, -hi, src, mult, add).then_inc(*raises("dve_step"))
                dve.wait_ge(*latest("dve_step"))
                stt(dst, n, -mid, dst, mult, add).then_inc(*raises("dve_step"))
                dve.wait_ge(*latest("dve_step"))
                stt(dst, n, -lo, dst, mult, add).then_inc(*raises("dve_step"))
                dve.wait_ge(*latest("dve_step"))
                ts(dst, dst, PI_SAFE, -PI_SAFE, ALU.min, ALU.max).then_inc(*raises(last))
                dve.wait_ge(*latest(last))

            def prologue():
                dve.wait_ge(S["small_loaded"].h, 16 * 6)
                V.tensor_copy(posf, posr.bitcast(i32)).then_inc(*raises("dve_step"))
                dve.wait_ge(*latest("dve_step"))
                ts(ang, posf, K[:, C_FREQ:C_FREQ + 1], None, mult).then_inc(*raises("dve_step"))
                dve.wait_ge(*latest("dve_step"))
                reduce_angle(tr, ang, tn, "s5_col_v")

            def body(l):
                dve.wait_ge(S["small_loaded"].h, small["layer"])
                V.tensor_copy(sheet[0:8, 2, :].rearrange("p (a b) -> p a b", a=2), lamr[0:8, 5, 0:2].unsqueeze(2).to_broadcast([8, 2, 64])).then_inc(*raises("sheets"))
                dve.wait_ge(*latest("sheets"))
                for i in range(2):
                    tt(lamr[0:1, 2 * i, :], lamr[0:1, 2 * i, :], lamr[0:1, 2 * i + 1, :], mult).then_inc(*raises("dve_step"))
                    dve.wait_ge(*latest("dve_step"))
                    V.reduce_sum(lamr[0:1, 4, 6 + i:7 + i], lamr[0:1, 2 * i, :], AX.X).then_inc(*raises("lam_in" if i else "dve_step"))
                    dve.wait_ge(*latest("lam_in" if i else "dve_step"))
                dve.wait_ge(S["lam_exp"].h, 1)
                tt(lamr[0:1, 4, 0:1], lamr[0:1, 4, 5:6], lamr[0:1, 4, 4:5], sub).then_inc(*raises("dve_step"))
                dve.wait_ge(*latest("dve_step"))
                tt(lamr[0:1, 4, 0:1], lamr[0:1, 4, 0:1], lamr[0:1, 4, 2:3], sub).then_inc(*raises("dve_step"))
                dve.wait_ge(*latest("dve_step"))
                V.tensor_copy(lamr[0:1, 4, 1:2], lamr[0:1, 4, 3:4]).then_inc(*raises("lam_row"))
                dve.wait_ge(*latest("lam_row"))
                dve.wait_ge(*filled("sheet0"))
                ps = bank("sheet0")
                V.tensor_copy(col1[:, :], ps[:, 0:S1_N]).then_inc(*empties("sheet0"))
                dve.wait_ge(*emptied("sheet0"))
                dve.wait_ge(*filled("sheet1"))
                ps = bank("sheet1")
                V.tensor_copy(col2[:, :], ps[:, 0:S2_N]).then_inc(*empties("sheet1"))
                dve.wait_ge(*emptied("sheet1"))
                dve.wait_ge(*filled("sheet2"))
                ps = bank("sheet2")
                V.tensor_copy(col3[:, :], ps[:, 0:24]).then_inc(*empties("sheet2"))
                dve.wait_ge(*emptied("sheet2"))
                dve.wait_ge(*filled("lam"))
                ps = bank("lam")
                V.tensor_copy(lamc[:, 0:2], ps[:, 0:2]).then_inc(*empties("lam"))
                dve.wait_ge(*emptied("lam"))
                g0 = S2["da_subln_g"][0]
                tt(lamc[:, 2:3], col2[:, g0:g0 + 1], lamc[:, 1:2], mult).then_inc(*raises("dve_step"))
                dve.wait_ge(*latest("dve_step"))
                s = [s5c[:, i, :] for i in range(24)]
                are, aim = col3[:, 8:16], col3[:, 16:24]
                V.memset(stat[:, 0, 38:39], 0.0).then_inc(*raises("s5_col_v"))
                dve.wait_ge(*latest("s5_col_v"))
                dve.wait_ge(S["s5_col_a"].h, 1)
                tt(s[1], s[0], are, mult).then_inc(*raises("dve_step"))
                dve.wait_ge(*latest("dve_step"))
                tt(s[2], s[0], aim, mult).then_inc(*raises("dve_step"))
                dve.wait_ge(*latest("dve_step"))
                reduce_angle(s[5], s[2], s[4], "s5_col_v")
                ts(s[6], s[5], INV_2PI, None, mult).then_inc(*raises("dve_step"))
                dve.wait_ge(*latest("dve_step"))
                ts(s[7], s[6], ROUND13, ROUND13, add, sub).then_inc(*raises("dve_step"))
                dve.wait_ge(*latest("dve_step"))
                tt(s[6], s[6], s[7], sub).then_inc(*raises("dve_step"))
                dve.wait_ge(*latest("dve_step"))
                dve.wait_ge(S["s5_col_a"].h, 3)
                rho, sn, cs = s[3], s[8], s[9]
                tt(s[10], rho, cs, mult).then_inc(*raises("dve_step"))
                dve.wait_ge(*latest("dve_step"))
                ts(s[10], s[10], -1.0, None, add).then_inc(*raises("dve_step"))
                dve.wait_ge(*latest("dve_step"))
                tt(s[11], rho, sn, mult).then_inc(*raises("dve_step"))
                dve.wait_ge(*latest("dve_step"))
                tt(s[12], are, are, mult).then_inc(*raises("dve_step"))
                dve.wait_ge(*latest("dve_step"))
                tt(s[13], aim, aim, mult).then_inc(*raises("dve_step"))
                dve.wait_ge(*latest("dve_step"))
                tt(s[12], s[12], s[13], add).then_inc(*raises("dve_step"))
                dve.wait_ge(*latest("dve_step"))
                V.reciprocal(s[12], s[12]).then_inc(*raises("dve_step"))
                dve.wait_ge(*latest("dve_step"))
                tt(s[13], s[10], are, mult).then_inc(*raises("dve_step"))
                dve.wait_ge(*latest("dve_step"))
                tt(s[14], s[11], aim, mult).then_inc(*raises("dve_step"))
                dve.wait_ge(*latest("dve_step"))
                tt(s[13], s[13], s[14], add).then_inc(*raises("dve_step"))
                dve.wait_ge(*latest("dve_step"))
                tt(s[13], s[13], s[12], mult).then_inc(*raises("dve_step"))
                dve.wait_ge(*latest("dve_step"))
                tt(s[14], s[11], are, mult).then_inc(*raises("dve_step"))
                dve.wait_ge(*latest("dve_step"))
                tt(s[15], s[10], aim, mult).then_inc(*raises("dve_step"))
                dve.wait_ge(*latest("dve_step"))
                tt(s[14], s[14], s[15], sub).then_inc(*raises("dve_step"))
                dve.wait_ge(*latest("dve_step"))
                tt(s[14], s[14], s[12], mult).then_inc(*raises("dve_step"))
                dve.wait_ge(*latest("dve_step"))
                dve.wait_ge(*emptied("cT"))
                V.memset(PR[:, :, 0:2], 0.0).then_inc(*raises("dve_step"))
                dve.wait_ge(*latest("dve_step"))
                for i in range(RW_TILES):
                    dve.wait_ge(*emptied(f"rw{i}"))
                    tt(s_m[0], PR[:, i, 1:T + 1], PR[:, i, 2:T + 2], sub).then_inc(*raises("dve_step"))
                    dve.wait_ge(*latest("dve_step"))
                    stt(PR[:, i, 2:T + 2], s_m[0], col2[:, i:i + 1], PR[:, i, 2:T + 2], mult, add).then_inc(*raises("shift_done"))
                    dve.wait_ge(*latest("shift_done"))
                for i in range(8):
                    raw = (qT if i < 4 else kT)[:, i % 4, :]
                    dve.wait_ge(*filled(f"rot{i}"))
                    ps = bank(f"rot{i}")
                    tt(s_m[1], ps[:, :], ropeS[:, :], mult).then_inc(*empties(f"rot{i}"))
                    dve.wait_ge(*emptied(f"rot{i}"))
                    tt(s_m[2], raw, ropeC[:, :], mult).then_inc(*raises("dve_step"))
                    dve.wait_ge(*latest("dve_step"))
                    tt(raw, s_m[1], s_m[2], add).then_inc(*raises("rope_done"))
                    dve.wait_ge(*latest("rope_done"))
                iota = K[:, C_IOTA:C_IOTA + T]
                for j in range(S5_TILES):
                    ct, jj = j // 4, j % 4

                    def c(i):
                        return s5c[:, i, j:j + 1]

                    mask = K[:, C_S5M + jj * P:C_S5M + (jj + 1) * P]
                    q, m = s_z[0], s_z[1]
                    ts(q, iota, c(7), None, mult).then_inc(*raises("dve_step"))
                    dve.wait_ge(*latest("dve_step"))
                    ts(m, q, ROUND, ROUND, add, sub).then_inc(*raises("dve_step"))
                    dve.wait_ge(*latest("dve_step"))
                    tt(q, q, m, sub).then_inc(*raises("dve_step"))
                    dve.wait_ge(*latest("dve_step"))
                    stt(q, iota, c(6), q, mult, add).then_inc(*raises("dve_step"))
                    dve.wait_ge(*latest("dve_step"))
                    ts(m, q, ROUND, ROUND, add, sub).then_inc(*raises("dve_step"))
                    dve.wait_ge(*latest("dve_step"))
                    tt(q, q, m, sub).then_inc(*raises("s5_tables"))
                    dve.wait_ge(*latest("s5_tables"))
                    if j:
                        dve.wait_ge(S["s5_x"].h, 2 * j)
                    br, bi = bn[:, 0, j, :], bn[:, 1, j, :]
                    b4 = s_m[0][:, 0:64].rearrange("p (a b) -> p a b", b=16)
                    ts(b4[:, 0, :], bi, c(14), None, mult).then_inc(*raises("dve_step"))
                    dve.wait_ge(*latest("dve_step"))
                    ts(b4[:, 1, :], bi, c(13), None, mult).then_inc(*raises("dve_step"))
                    dve.wait_ge(*latest("dve_step"))
                    stt(b4[:, 2, :], br, c(13), b4[:, 0, :], mult, sub).then_inc(*raises("dve_step"))
                    dve.wait_ge(*latest("dve_step"))
                    stt(b4[:, 3, :], br, c(14), b4[:, 1, :], mult, add).then_inc(*raises("dve_step"))
                    dve.wait_ge(*latest("dve_step"))
                    if j:
                        dve.wait_ge(*emptied(f"bT{j - 1}"))
                    for i in range(2):
                        tt(bpad[:, i, :].rearrange("p (g h) -> p g h", h=16), b4[:, 2 + i, :].unsqueeze(1).to_broadcast([P, 8, 16]),
                                mask.rearrange("p (g h) -> p g h", h=16), mult).then_inc(*raises("s5_b" if i else "dve_step"))
                        dve.wait_ge(*latest("s5_b" if i else "dve_step"))
                    if j:
                        if jj == 0:
                            dve.wait_ge(*filled(f"y{ct - 1}"))
                        else:
                            dve.wait_ge(S["s5_y"].h, j - ct)
                    for i in range(2):
                        tt(cpad[:, i, :], cT[:, 2 * i + ct, :], mask, mult).then_inc(*raises("s5_c" if i else "dve_step"))
                        dve.wait_ge(*latest("s5_c" if i else "dve_step"))
                    dve.wait_ge(S["s5_col_a"].h, 4 + j)
                    dve.wait_ge(*filled(f"bu{j}0"))
                    pr = bank(f"bu{j}0")
                    dve.wait_ge(*filled(f"bu{j}1"))
                    pi = bank(f"bu{j}1")
                    tt(s_m[0], pr[:, :], s_c, mult).then_inc(*raises("dve_step"))
                    dve.wait_ge(*latest("dve_step"))
                    tt(s_m[1], pi[:, :], s_s, mult).then_inc(*raises("dve_step"))
                    dve.wait_ge(*latest("dve_step"))
                    tt(s_m[2], pi[:, :], s_c, mult).then_inc(*empties(f"bu{j}1"))
                    dve.wait_ge(*emptied(f"bu{j}1"))
                    tt(s_m[3], pr[:, :], s_s, mult).then_inc(*empties(f"bu{j}0"))
                    dve.wait_ge(*emptied(f"bu{j}0"))
                    dve.wait_ge(S["s5_w"].h, 2 * j + 2)
                    for i in range(2):
                        V.tensor_tensor_scan(s_z[i], c(3).to_broadcast([P, T]), s_x[i], 0.0, mult, add).then_inc(*raises("dve_step"))
                        dve.wait_ge(*latest("dve_step"))
                    tt(s_m[0], s_z[0], s_c, mult).then_inc(*raises("s5_n"))
                    dve.wait_ge(*latest("s5_n"))
                    tt(s_m[1], s_z[1], s_s, mult).then_inc(*raises("s5_n"))
                    dve.wait_ge(*latest("s5_n"))
                    tt(s_m[2], s_z[0], s_s, mult).then_inc(*raises("s5_n"))
                    dve.wait_ge(*latest("s5_n"))
                    tt(s_m[3], s_z[1], s_c, mult).then_inc(*raises("s5_n"))
                    dve.wait_ge(*latest("s5_n"))
                    if jj == 3:
                        dve.wait_ge(*filled(f"y{ct}"))
                        ps = bank(f"y{ct}")
                        stt(yT[:, ct, :], uT[:, ct, :], col2[:, S2["s5_d"][0] + ct:S2["s5_d"][0] + ct + 1], ps[:, :], mult, add).then_inc(*empties(f"y{ct}"))
                        dve.wait_ge(*emptied(f"y{ct}"))
                dve.wait_ge(*filled("glu1"))
                for n in range(2):
                    dve.wait_ge(*emptied(f"glu{n}"))
                    tt(zT[:, n, :], zT[:, n, :], s_r[:, n, :], mult).then_inc(*raises("s5_g"))
                    dve.wait_ge(*latest("s5_g"))
                dve.wait_ge(*emptied("s5ss"))
                dve.wait_ge(*filled(f"v{NT - 1}"))
                for ct in range(2):
                    g0 = S2["s5_out_g"][0] + ct
                    stt(hT[:, 6 + ct, :], zT[:, ct, :], col2[:, g0:g0 + 1], yT[:, 1, :], mult, mult).then_inc(*raises("hT_s5"))
                    dve.wait_ge(*latest("hT_s5"))
                def head_out(h):
                    dve.wait_ge(S["attn_rs"].h, h + 1)
                    stt(hT[:, h, :], oh, lamc[:, 2:3], orr, mult, mult).then_inc(*raises("hT_da"))
                    dve.wait_ge(*latest("hT_da"))

                for n in range(DA_HEADS * NT):
                    h, i = n // NT, n % NT
                    st = stat[:, n % 2, :]
                    w = (i + 1) * P
                    for b in range(2):
                        dve.wait_ge(*filled(f"sc{h}{i}{b}"))
                        ps = bank(f"sc{h}{i}{b}")
                        V.reduce_max(st[:, 8 + b:9 + b], ps[:, 0:w], AX.X).then_inc(*raises("dve_step"))
                        dve.wait_ge(*latest("dve_step"))
                        ts(st[:, 4 + b:5 + b], st[:, 8 + b:9 + b], -0.125, None, mult).then_inc(*raises("attn_max"))
                        dve.wait_ge(*latest("attn_max"))
                    dve.wait_ge(*emptied(f"sc{h}{i}0"))
                    dve.wait_ge(*emptied(f"sc{h}{i}1"))
                    V.reciprocal(st[:, 6:8], st[:, 6:8]).then_inc(*raises("dve_step"))
                    dve.wait_ge(*latest("dve_step"))
                    tt(st[:, 7:8], st[:, 7:8], lamc[:, 0:1], mult).then_inc(*raises("dve_step"))
                    dve.wait_ge(*latest("dve_step"))
                    p0, p1 = AP_[:, 2 * (n % 2), 0:w], AP_[:, 2 * (n % 2) + 1, 0:w]
                    ts(p1, p1, st[:, 7:8], None, mult).then_inc(*raises("dve_step"))
                    dve.wait_ge(*latest("dve_step"))
                    stt(p0, p0, st[:, 6:7], p1, mult, add).then_inc(*raises("attn_p"))
                    dve.wait_ge(*latest("attn_p"))
                    if n % NT == 2 and h:
                        head_out(h - 1)
                head_out(DA_HEADS - 1)
                for j in range(2):
                    def c2(name):
                        return col2[:, S2[name][0] + j:S2[name][0] + j + 1]

                    if j == 0:
                        dve.wait_ge(S["lr_ready"].h, 3)
                    r_, k_, v_ = PR[:, j, 2:], PR[:, 2 + j, 2:], PR[:, 4 + j, 2:]
                    t0, t1 = rw["t0"], rw["t1"]
                    ts(rw["kk"], k_, c2("rw_k_k"), None, mult).then_inc(*raises("rw_kk"))
                    dve.wait_ge(*latest("rw_kk"))
                    dve.wait_ge(*filled(f"kss{j}"))
                    ps = bank(f"kss{j}")
                    ts(t1, ps[:, :], 1e-24, None, ALU.max).then_inc(*empties(f"kss{j}"))
                    dve.wait_ge(*emptied(f"kss{j}"))
                    dve.wait_ge(*emptied(f"lrw{j}"))
                    V.memset(rP[:, :, 0:1], 1.0).then_inc(*raises("dve_step"))
                    dve.wait_ge(*latest("dve_step"))
                    zero = const("zero").to_broadcast([P, CH])
                    for c in range(NCH):
                        V.tensor_tensor_scan(rP[:, c, 1:], t0[:, c * CH:(c + 1) * CH], zero, 1.0, mult, add).then_inc(*raises("dve_step"))
                        dve.wait_ge(*latest("dve_step"))
                    ip3 = rw["iP"].rearrange("p (c t) -> p c t", c=NCH)
                    V.reciprocal(ip3, rP[:, :, 1:]).then_inc(*raises("dve_step"))
                    dve.wait_ge(*latest("dve_step"))
                    dve.wait_ge(*emptied(f"lra{j}"))
                    ts(t0, rw["a"], -1.0, c2("rw_k_a"), add, mult).then_inc(*raises("dve_step"))
                    dve.wait_ge(*latest("dve_step"))
                    stt(rw["kmod"], t0, 1.0, k_, add, mult).then_inc(*raises("dve_step"))
                    dve.wait_ge(*latest("dve_step"))
                    tt(t0, r_, rw["kmod"], mult).then_inc(*raises("dve_step"))
                    dve.wait_ge(*latest("dve_step"))
                    ts(rw["bonus"], t0, c2("rw_r_k"), None, mult).then_inc(*raises("rw_bonus"))
                    dve.wait_ge(*latest("rw_bonus"))
                    dve.wait_ge(S["rw_sq"].h, 2 * j + 2)
                    V.reciprocal(t1, t1).then_inc(*raises("dve_step"))
                    dve.wait_ge(*latest("dve_step"))
                    tt(rw["kk"], rw["kk"], t1, mult).then_inc(*raises("dve_step"))
                    dve.wait_ge(*latest("dve_step"))

                    def c3(a):
                        return a.rearrange("p (c t) -> p c t", c=NCH)

                    pend = rP[:, :, CH:CH + 1].to_broadcast([P, NCH, CH])
                    stt(c3(rw["A"]), c3(rw["kk"]), -1.0, rP[:, :, 0:CH], mult, mult).then_inc(*raises("dve_step"))
                    dve.wait_ge(*latest("dve_step"))
                    tt(t0, rw["kk"], rw["a"], mult).then_inc(*raises("dve_step"))
                    dve.wait_ge(*latest("dve_step"))
                    tt(rw["B"], t0, rw["iP"], mult).then_inc(*raises("dve_step"))
                    dve.wait_ge(*latest("dve_step"))
                    tt(c3(rw["Bh"]), c3(rw["B"]), pend, mult).then_inc(*raises("dve_step"))
                    dve.wait_ge(*latest("dve_step"))
                    tt(rw["K"], rw["kmod"], rw["iP"], mult).then_inc(*raises("dve_step"))
                    dve.wait_ge(*latest("dve_step"))
                    tt(c3(rw["Kh"]), c3(rw["K"]), pend, mult).then_inc(*raises("dve_step"))
                    dve.wait_ge(*latest("dve_step"))
                    tt(c3(rw["R"]), c3(r_), rP[:, :, 1:], mult).then_inc(*raises("rw_gram_in"))
                    dve.wait_ge(*latest("rw_gram_in"))
                    dve.wait_ge(*filled(f"bon{j}"))
                    ps = bank(f"bon{j}")
                    tt(rw["bonus"], ps[:, :], v_, mult).then_inc(*empties(f"bon{j}"))
                    dve.wait_ge(*emptied(f"bon{j}"))
                    dve.wait_ge(S["hT_da"].h, DA_HEADS)

                    def q3(a):
                        return a.rearrange("p (i t) -> p i t", t=P)

                    def m3(c):
                        return K[:, c:c + P].unsqueeze(1).to_broadcast([P, NT, P])

                    for hh in range(2):
                        g = f"grABT{j}{hh}"
                        dve.wait_ge(*filled(g))
                        ps = bank(g)
                        tt(q3(mAB[:, hh, :]), q3(ps[:, :]), m3(C_SU), mult).then_inc(*raises("dve_step"))
                        dve.wait_ge(*latest("dve_step"))
                        tt(q3(TiT[:, hh, :]), q3(ps[:, :]), m3(C_L1U), mult).then_inc(*empties(g))
                        dve.wait_ge(*emptied(g))
                        tt(q3(TiT[:, hh, :]), q3(TiT[:, hh, :]), m3(C_ID), add).then_inc(*raises("rw_T"))
                        dve.wait_ge(*latest("rw_T"))
                        g = f"grAB{j}{hh}"
                        dve.wait_ge(*filled(g))
                        ps = bank(g)
                        tt(q3(Ti[:, hh, :]), q3(ps[:, :]), m3(C_L1L), mult).then_inc(*empties(g))
                        dve.wait_ge(*emptied(g))
                        tt(q3(Ti[:, hh, :]), q3(Ti[:, hh, :]), m3(C_ID), add).then_inc(*raises("rw_T"))
                        dve.wait_ge(*latest("rw_T"))
                        for nm, dst, mask in (("RBT", mRB, C_IU), ("RKT", mRK, C_IU), ("AKT", mAK, C_SU)):
                            g = f"gr{nm}{j}{hh}"
                            dve.wait_ge(*filled(g))
                            ps = bank(g)
                            tt(q3(dst[:, hh, :]), q3(ps[:, :]), m3(mask), mult).then_inc(*empties(g))
                            dve.wait_ge(*emptied(g))
                    for lv in range(len(LEVELS)):
                        for hh in range(2):
                            dve.wait_ge(*filled(f"dT{j}{lv}{hh}"))
                            pa = bank(f"dT{j}{lv}{hh}")
                            dve.wait_ge(*filled(f"dTT{j}{lv}{hh}"))
                            pb = bank(f"dTT{j}{lv}{hh}")
                            for i, (g, dst, ps) in enumerate(((f"dT{j}{lv}{hh}", Ti, pa), (f"dTT{j}{lv}{hh}", TiT, pb))):
                                V.copy_predicated(q3(dst[:, hh, :]), lev[:, lv, i, :].bitcast(u32).unsqueeze(1).to_broadcast([P, NT, P]), q3(ps[:, :])).then_inc(*empties(g))
                                dve.wait_ge(*emptied(g))
                    dve.wait_ge(*filled(f"Q{j}"))
                    ps = bank(f"Q{j}")
                    tt(rQ, ps[:, :], rw["R"], add).then_inc(*empties(f"Q{j}"))
                    dve.wait_ge(*emptied(f"Q{j}"))
                    tt(t0.rearrange("p (c k) -> p c k", c=NCH), K[:, C_EYE:C_EYE + CH].unsqueeze(1).to_broadcast([P, NCH, CH]), pend, mult).then_inc(*raises("dve_step"))
                    dve.wait_ge(*latest("dve_step"))
                    for par in range(2):
                        dve.wait_ge(*filled(f"GH{j}{par}"))
                        ps = bank(f"GH{j}{par}")

                        def par3(a):
                            return a.rearrange("p (i q k) -> p i q k", q=2, k=CH)[:, :, par, :]

                        tt(par3(rG), ps[:, 0:256].rearrange("p (i k) -> p i k", k=CH), par3(t0), add).then_inc(*raises("dve_step"))
                        dve.wait_ge(*latest("dve_step"))
                        V.tensor_copy(par3(rH), ps[:, 256:512].rearrange("p (i k) -> p i k", k=CH)).then_inc(*empties(f"GH{j}{par}"))
                        dve.wait_ge(*emptied(f"GH{j}{par}"))
                    V.tensor_copy(rS[:, CH:2 * CH], rH[:, 0:CH]).then_inc(*raises("rw_state"))
                    dve.wait_ge(*latest("rw_state"))
                    for c in range(1, NCH - 1):
                        for hh in range(2):
                            r = slice(64 * hh, 64 * hh + 64)
                            g = f"S{j}{c}{hh}"
                            dve.wait_ge(*filled(g))
                            ps = bank(g)
                            tt(rS[r, (c + 1) * CH:(c + 2) * CH], ps[r, 0:CH], rH[r, c * CH:(c + 1) * CH], add).then_inc(*empties(g))
                            dve.wait_ge(*emptied(g))
                    dve.wait_ge(*filled(f"ym{j}"))
                    ps = bank(f"ym{j}")
                    stt(rY, ps[:, :], -1.0 / CH, rY, mult, add).then_inc(*empties(f"ym{j}"))
                    dve.wait_ge(*emptied(f"ym{j}"))
                    dve.wait_ge(*emptied(f"yv{j}"))
                    tt(rY, rY, t1, mult).then_inc(*raises("dve_step"))
                    dve.wait_ge(*latest("dve_step"))
                    ts(rY, rY, c2("rw_lnx_g"), c2("rw_lnx_b"), mult, add).then_inc(*raises("dve_step"))
                    dve.wait_ge(*latest("dve_step"))
                    tt(rY, rY, rw["bonus"], add).then_inc(*raises("dve_step"))
                    dve.wait_ge(*latest("dve_step"))
                    tt(hT[:, 4 + j, :], rY, rw["g"], mult).then_inc(*raises("hT_rw"))
                    dve.wait_ge(*latest("hT_rw"))

                def layer_norm(n, t, names):
                    st = stat[:, t % 2, :]
                    for h in range(2):
                        if names[h]:
                            dve.wait_ge(*filled(names[h]))
                            ps = bank(names[h])
                            xx = x[:, t, h * 512:(h + 1) * 512]
                            stt(xx, xx, ALPHA, ps[:, :], mult, add).then_inc(*empties(names[h]))
                            dve.wait_ge(*emptied(names[h]))
                    bs = st[:, 12:24].rearrange("p (a b) -> p a b", b=6)
                    for h in range(2):
                        V.bn_stats(bs[:, h, :], x[:, t, h * 512:(h + 1) * 512]).then_inc(*raises("dve_step"))
                        dve.wait_ge(*latest("dve_step"))
                    V.bn_aggr(st[:, 0:2], st[:, 12:24]).then_inc(*raises("ln_var"))
                    dve.wait_ge(*latest("ln_var"))
                    dve.wait_ge(S["ln_rstd"].h, NT * n + t + 1)
                    ts(x[:, t, :], x[:, t, :], st[:, 0:1], st[:, 1:2], sub, mult).then_inc(*raises("ln_hat"))
                    dve.wait_ge(*latest("ln_hat"))

                for t in range(NT):
                    layer_norm(0, t, [f"wo{t}0", f"wo{t}1"])
                for n in range(MEM_HEADS * NT):
                    h, i = n // NT, n % NT
                    st = stat[:, n % 2, :]
                    dve.wait_ge(*filled(f"cs{h}{i}"))
                    ps = bank(f"cs{h}{i}")
                    V.reduce_max(st[:, 8:9], ps[:, 0:N_MEM], AX.X).then_inc(*raises("dve_step"))
                    dve.wait_ge(*latest("dve_step"))
                    ts(st[:, 9:10], st[:, 8:9], -1.0 / 16, None, mult).then_inc(*raises("ca_max"))
                    dve.wait_ge(*latest("ca_max"))
                    dve.wait_ge(*emptied(f"cs{h}{i}"))
                    V.reciprocal(st[:, 10:11], st[:, 10:11]).then_inc(*raises("dve_step"))
                    dve.wait_ge(*latest("dve_step"))
                    ts(p2[:, n % 2, :], p2[:, n % 2, :], st[:, 10:11], None, mult).then_inc(*raises("ca_p"))
                    dve.wait_ge(*latest("ca_p"))
                for t in range(NT):
                    layer_norm(1, t, [f"cw{t}0", f"cw{t}1"])
                for i in range(2):
                    V.memset(fa[i][:, 0:2], 0.0).then_inc(*raises("ffn_a"))
                    dve.wait_ge(*latest("ffn_a"))
                for i in range(FT):
                    a = fa[i % 2]

                    def w(k):
                        return col1[:, k * FT + i:k * FT + i + 1]

                    dve.wait_ge(*emptied(f"fa{i}"))
                    ts(fc, a[:, 2:T + 2], w(2), col1[:, 3 * FT + i:3 * FT + i + 1], mult, add).then_inc(*raises("dve_step"))
                    dve.wait_ge(*latest("dve_step"))
                    stt(fc, a[:, 1:T + 1], w(1), fc, mult, add).then_inc(*raises("dve_step"))
                    dve.wait_ge(*latest("dve_step"))
                    stt(fc, a[:, 0:T], w(0), fc, mult, add).then_inc(*raises("ffn_c"))
                    dve.wait_ge(*latest("ffn_c"))
                    dve.wait_ge(*filled(f"fg{i}"))
                    ps = bank(f"fg{i}")
                    dve.wait_ge(S["ffn_s"].h, i + 1)
                    tt(hid[:, i, :], ps[:, :], fc, mult).then_inc(*empties(f"fg{i}"))
                    dve.wait_ge(*emptied(f"fg{i}"))
                for t in range(NT):
                    dve.wait_ge(*filled(f"dn{t}0"))
                    ps = bank(f"dn{t}0")
                    xx = x[:, t, 0:512]
                    stt(xx, xx, ALPHA, ps[:, :], mult, add).then_inc(*empties(f"dn{t}0"))
                    dve.wait_ge(*emptied(f"dn{t}0"))
                for t in range(NT):
                    layer_norm(2, t, [None, f"dn{t}1"])

            layers(dve, "dve", prologue, body)

        @block.gpsimd
        def _(pool):
            G = nc.gpsimd

            def prologue():
                pass

            def body(l):
                for j in range(S5_TILES):
                    pool.wait_ge(*emptied(f"bu{j}1"))
                    pool.wait_ge(*emptied(f"bu{j}0"))
                    if j:
                        if j % 4 == 0:
                            pool.wait_ge(*filled(f"y{j // 4 - 1}"))
                        else:
                            pool.wait_ge(S["s5_y"].h, j - j // 4)
                    G.tensor_tensor(s_x[0], s_m[0], s_m[1], ALU.add).then_inc(*raises("s5_w"))
                    pool.wait_ge(*latest("s5_w"))
                    G.tensor_tensor(s_x[1], s_m[2], s_m[3], ALU.subtract).then_inc(*raises("s5_w"))
                    pool.wait_ge(*latest("s5_w"))
                    pool.wait_ge(S["s5_n"].h, 4 * j + 4)
                    G.tensor_tensor(s_x[0], s_m[0], s_m[1], ALU.subtract).then_inc(*raises("s5_x"))
                    pool.wait_ge(*latest("s5_x"))
                    G.tensor_tensor(s_x[1], s_m[2], s_m[3], ALU.add).then_inc(*raises("s5_x"))
                    pool.wait_ge(*latest("s5_x"))
                for n in range(3):
                    pool.wait_ge(S["rows_loaded"].h, 32 * (n + 1))
                    for t in range(NT):
                        pool.wait_ge(S["ln_hat"].h, NT * n + t + 1)
                        G.tensor_tensor(x[:, t, :], x[:, t, :], lnrow[:, 0, :], ALU.mult).then_inc(*raises("pool_step"))
                        pool.wait_ge(*latest("pool_step"))
                        G.tensor_tensor(x[:, t, :], x[:, t, :], lnrow[:, 1, :], ALU.add).then_inc(*raises("ln_out"))
                        pool.wait_ge(*latest("ln_out"))

            layers(pool, "pool", prologue, body)


_NAMES = ["x", "mem", "positions", "w_in", "da_lam_q1", "da_lam_k1", "da_lam_q2", "da_lam_k2", "da_subln_g",
          "rw_mu", "rw_w0", "rw_w2", "rw_a0", "rw_a2", "rw_g2", "rw_k_k", "rw_k_a", "rw_r_k", "rw_lnx_g", "rw_lnx_b",
          "s5_a_re", "s5_a_im", "s5_b_re", "s5_b_im", "s5_c_re", "s5_c_im", "s5_d", "s5_log_step", "s5_glu_w",
          "s5_glu_b", "s5_out_g", "w_out", "ln1_g", "ln1_b", "ca_wq", "ca_wkv", "ca_wo", "ln2_g", "ln2_b",
          "ffn_w_up", "ffn_conv_w", "ffn_conv_b", "ffn_w_down", "ln3_g", "ln3_b"]


def kernel(**inputs):
    import numpy as _np
    import concourse.bacc as _bacc
    from concourse import mybir as _mybir
    from concourse.bass_utils import run_bass_kernel_spmd as _run

    nc = _bacc.Bacc("TRN2", target_bir_lowering=False, num_devices=1)
    arrays = {name: _np.ascontiguousarray(inputs[name]) for name in _NAMES}
    arrays.update(constants())
    io = {}
    for name, a in arrays.items():
        io[name] = nc.dram_tensor(f"in_{name}", a.shape, _mybir.dt.from_np(a.dtype), kind="ExternalInput").ap()
    io["out"] = nc.dram_tensor("out_0", (1, T, D), _mybir.dt.float32, kind="ExternalOutput").ap()
    build(nc, io)
    r = _run(nc, [{f"in_{k}": v for k, v in arrays.items()}], core_ids=[0])
    return r.results[0]["out_0"]
```

```python
import math
from contextlib import ExitStack

import numpy as np

import concourse.bass as bass
from concourse import mybir

DEPTH, D, T = 2, 1024, 512
P = 128
KT, NT = D // P, T // P
DA_HEADS, DA_W = 4, 512
RW_W, RW_IN, RW_TILES = 256, 896, 7
S5_W, S5_GROUPS, S5_STATE, S5_CH = 256, 16, 64, 16
S5_TILES = S5_GROUPS * S5_STATE // P
IN_W = 3 * DA_W + RW_IN + S5_W
N_MEM, MT, MEM_HEADS = 256, 2, 4
D_FF = 2816
FT = D_FF // P
CH = 64
NCH = T // CH
ALPHA = (2.0 * DEPTH) ** 0.25
DECAY = math.exp(-0.5)
LN_EPS, RMS_EPS, LNX_EPS = 1e-5, 1e-6, 64e-5
NEG = -1e37
ROUND = 1.5 * 2.0 ** 23
ROUND13 = ROUND / 2.0 ** 13
INV_2PI = 1.0 / (2.0 * math.pi)
TWO_PI_SAFE = 6.283184
PI_SAFE = 3.1415925
SLOTS = 2
SLOT = 2048
ARENA = 24088

C_ID, C_SU, C_IU, C_L1U, C_L1L, C_ONE, C_BONE, C_ROT = (P * i for i in range(8))
C_EYE = 8 * P
C_S5M = C_EYE + CH
C_IOTA = C_S5M + 4 * P
C_NEG = C_IOTA + T
C_MROW = C_NEG + CH
C_FREQ = C_MROW + P
C_SC = C_FREQ + 1
SC = {"ln_eps": LN_EPS, "rms_eps": RMS_EPS, "lnx_eps": LNX_EPS, "half_pi": math.pi / 2, "zero": 0.0, "one": 1.0}
C_W = C_SC + len(SC)
LEVELS = [2, 4, 8, 16, 32]

S1 = {}
S2 = {}


def _rows(table, names):
    at = 0
    for name, n in names:
        table[name] = (at, n)
        at += n
    return at


S1_N = _rows(S1, [("ffn_conv_w", 3 * FT), ("ffn_conv_b", FT)])
S2_N = _rows(S2, [("rw_mu", 7), ("rw_w0", 2), ("rw_a0", 2), ("rw_k_k", 2), ("rw_k_a", 2), ("rw_r_k", 2),
                  ("rw_lnx_g", 2), ("rw_lnx_b", 2), ("s5_d", 2), ("s5_glu_b", 2), ("s5_out_g", 2),
                  ("da_subln_g", 1)])


def two_pi_parts():
    hi = np.float32(round(2 * math.pi * 2 ** 9) / 2 ** 9)
    mid = np.float32(round((2 * math.pi - float(hi)) * 2 ** 22) / 2 ** 22)
    lo = np.float32(2 * math.pi - float(hi) - float(mid))
    return float(hi), float(mid), float(lo)


def constants():
    c = np.zeros((P, C_W), np.float32)
    p, m = np.arange(P)[:, None], np.arange(P)[None, :]
    same = p // CH == m // CH
    c[:, C_ID:C_ID + P] = p == m
    c[:, C_SU:C_SU + P] = same & (p < m)
    c[:, C_IU:C_IU + P] = same & (p <= m)
    c[:, C_L1U:C_L1U + P] = (p // 2 == m // 2) & (p < m)
    c[:, C_L1L:C_L1L + P] = (p // 2 == m // 2) & (p > m)
    c[:, C_ONE:C_ONE + P] = 1
    c[:, C_BONE:C_BONE + P] = same
    c[:, C_ROT:C_ROT + P] = np.where((p == m + 32) & (m % 64 < 32), -1.0, np.where((p == m - 32) & (m % 64 >= 32), 1.0, 0.0))
    c[:, C_EYE:C_EYE + CH] = p % CH == np.arange(CH)[None, :]
    for j in range(4):
        c[:, C_S5M + j * P:C_S5M + (j + 1) * P] = m // S5_CH == 2 * j + p // S5_STATE
    c[:, C_IOTA:C_IOTA + T] = np.arange(T)[None, :]
    c[:, C_NEG:C_NEG + CH] = NEG
    c[:, C_MROW:C_MROW + P] = m < CH
    inv = np.float32(10000.0) ** (-np.arange(0, 64, 2, dtype=np.float32) / np.float32(64))
    c[:, C_FREQ] = inv.astype(np.float32)[np.arange(P) % 32]
    for i, v in enumerate(SC.values()):
        c[:, C_SC + i] = v
    lev = np.zeros((P, len(LEVELS), 2, P), np.float32)
    for i, b in enumerate(LEVELS):
        joined = (p // (2 * b) == m // (2 * b)) & (p // b != m // b)
        lev[:, i, 0] = joined & (p > m)
        lev[:, i, 1] = joined & (p < m)
    lam = np.zeros((DEPTH, 2), np.float32)
    for l in range(DEPTH):
        lam[l] = 0.8 - 0.6 * math.exp(-0.3 * l), 1.0 - (0.8 - 0.6 * math.exp(-0.3 * l))
    return {"const": c, "level_masks": lev, "lambda_inits": lam}


class Sem:

    def __init__(self, handle):
        self.h, self.n = handle, 0


def build(nc, io):
    f32, f32r, u32, i32 = mybir.dt.float32, mybir.dt.float32r, mybir.dt.uint32, mybir.dt.int32
    ALU, ACT, AX = mybir.AluOpType, mybir.ActivationFunctionType, mybir.AxisListType
    ctx = ExitStack()
    with ctx:
        def sb(name, shape, dt=f32):
            return ctx.enter_context(nc.sbuf_tensor(name, shape, dt))

        x = sb("x", [P, NT, D])
        xT = [sb(n, [P, KT, T], f32r) for n in ("xT_high", "xT_low")]
        hT = xT
        raw = sb("raw_weights", [P, SLOTS, SLOT])
        split = [sb(n, [P, SLOTS, SLOT], f32r) for n in ("weights_high", "weights_low")]
        ropeC, ropeS = sb("ropeC", [P, T]), sb("ropeS", [P, T])
        K = sb("consts", [P, C_W])
        col1, col2, col3 = sb("col1", [P, S1_N]), sb("col2", [P, S2_N]), sb("col3", [P, 24])
        stat = sb("stat", [P, NT, 40])
        lamc = sb("lamc", [P, 4])
        s5c = sb("s5c", [P, 24, S5_TILES])
        with nc.sbuf_tensor("arena", [P, ARENA], f32) as arena:
            pass
        arena_r = sb("arena_split", [P, ARENA], f32r)

        def view(at, *shape, of=arena):
            n = int(np.prod(shape))
            assert at + n <= ARENA, (at, n)
            v = of[:, at:at + n]
            if len(shape) == 2:
                v = v.rearrange("p (a b) -> p a b", b=shape[1])
            if len(shape) == 3:
                v = v.rearrange("p (a b c) -> p a b c", b=shape[1], c=shape[2])
            return v

        def split_view(at, *shape):
            return view(at, *shape, of=arena_r)

        def as32(v):
            return v.bitcast(f32)

        qT, kT, vtok = view(0, 4, T), view(2048, 4, T), view(4096, NT, DA_W)
        PR = view(6144, RW_TILES, T + 2)
        uT = view(9744, 2, T)
        lrw = view(10768, RW_W)
        bn = view(11024, 2, S5_TILES, S5_CH)
        cn = view(11280, 2, 2, P)
        WK = 11792
        gluw = view(WK, 2, S5_W)
        lev = view(11024, len(LEVELS), 2, P)
        lnrow1 = view(6144, 2, D)
        AP_ = view(WK + 512, 4, T)
        aT = view(WK + 2560, 4, T)
        oh, osq, orr = view(WK + 4608, T), view(WK + 5120, T), view(WK + 5632, T)
        S = WK + 6144
        cT = view(S, 4, P)
        bpad, bT, cpad = view(S + 512, 2, P), view(S + 768, 2, P), view(S + 1024, 2, P)
        s_cos = [view(S + 1280, T), view(WK + 2048, T)]
        s_sin = [view(S + 1792, T), view(S + 5376, T)]
        s_m = [view(S + 2304 + 512 * i, T) for i in range(4)]
        s_z = [view(S + 4352 + 512 * i, T) for i in range(2)]
        assert S + 5888 <= ARENA
        s_turn, s_round = view(WK + 512, T), view(WK + 1024, T)
        rope_a = view(WK + 1536, T)
        s_n = [view(WK + 2560 + 512 * i, T) for i in range(4)]
        yT, zT, s_r = view(WK + 4608, 2, T), view(WK + 2560, 2, T), view(WK + 512, 2, T)
        shifted = view(WK + 5632, T)
        b_parts = view(WK + 5632, 4, S5_CH)
        R = WK + 512
        rw = {n: view(R + 512 * i, T) for i, n in enumerate(
            ["LR", "a", "g", "t0", "iP", "kk", "kmod", "A", "B", "Bh", "K", "Kh", "R", "bonus", "t1"])}
        rP = view(R + 7680, NCH, CH + 1)
        vT_, bT_, kT_ = (view(R + 8200 + 512 * i, NT, P) for i in range(3))
        zA = view(R + 9736, 2, NT * P)
        uw = view(R + 10760, 2, NT * P)
        rZ = view(R + 512 * 7, 2, NT * P)
        rH, rS, rG, rQ = rw["K"], rw["iP"], rw["Bh"], rw["Kh"]
        rY = uT[:, 0, :]
        assert R + 11784 <= ARENA
        mAB, mRB, mRK, mAK, Ti, TiT = (view(1024 * i, 2, NT * P) for i in range(6))
        mK, mV, q2 = view(0, KT, N_MEM), view(2048, MT, D), view(4096, KT, T)
        memT = [split_view(at, KT, N_MEM) for at in (8192, 10240)]
        o2 = [split_view(at, KT, T) for at in (8192, 13824)]
        p2, pT2 = view(12288, 2, N_MEM), view(12800, MT, T)
        memtok, lnrow2 = view(17920, MT, D), view(22040, 2, D)
        hid = [split_view(at, FT, T) for at in (0, FT * T)]
        fa = view(2 * FT * T, T + 2)
        fc = [view(2 * FT * T + 514 + 512 * i, T) for i in range(2)]
        posr, posf, ang, tn, tr = (view(2048 + 512 * i, T) for i in range(5))
        sheet = view(0, 3, P)
        lamr = view(512, 6, 64)

        def const(name):
            i = C_SC + list(SC).index(name)
            return K[:, i:i + 1]

        ident, ones, bones, rot = (K[:, c:c + P] for c in (C_ID, C_ONE, C_BONE, C_ROT))

        banks = [ctx.enter_context(nc.psum_tensor(f"bank{i}", [P, 512], f32)) for i in range(8)]

        def sem(name):
            return Sem(ctx.enter_context(nc.semaphore(name)))

        quiet = sem("engines_quiet")
        go = {n: sem(f"go_{n}") for n in ("pe", "act", "dve", "pool")}
        out_done = sem("output_written")
        S = {}

        def ev(name):
            if name not in S:
                S[name] = sem(name)
            return S[name]

        for i in range(8):
            ev(f"bank{i}_filled"), ev(f"bank{i}_emptied")
        for i in range(SLOTS):
            ev(f"slot{i}_loaded")
        for name in ("act_step", "dve_step", "pool_step", "chunk_used", "small_loaded", "rows_loaded", "levels_loaded", "mem_loaded", "chunk_high", "chunk_low_pool", "chunk_low_dve",
                     "x_high", "mem_high", "o2_high", "hT_high", "s5_raw", "rw_raw", "da_raw", "hid_high", "hid_low",
                     "shift_done", "s5_tables", "s5_b", "s5_c", "s5_w", "s5_n", "s5_x", "s5_y", "s5_z", "s5_g",
                     "s5_sq", "hT_s5", "lr_ready", "rw_kk", "rw_sq", "rw_gram_in", "rw_T", "rw_state", "rw_ysq",
                     "rw_bonus", "hT_rw", "attn_max", "attn_p", "attn_rs", "hT_da", "rope_done", "ln_var", "ln_rstd",
                     "ln_hat", "ln_out_dve", "ln_out_pool", "ca_max", "ca_p", "ffn_a", "ffn_c", "ffn_s", "sheets", "lam_in", "lam_exp",
                     "lam_row", "s5_col_v", "s5_col_a"):
            ev(name)

        def new_segment():
            for one in S.values():
                one.n = 0

        def raises(name):
            S[name].n += 1
            return S[name].h, 1

        def latest(name):
            return S[name].h, S[name].n

        def bank(g):
            return banks[groups[g][0]]

        def fills(g):
            return S[f"bank{groups[g][0]}_filled"].h, 1

        def filled(g):
            return S[f"bank{groups[g][0]}_filled"].h, groups[g][1] + 1

        def empties(g):
            return S[f"bank{groups[g][0]}_emptied"].h, 1

        def emptied(g):
            return S[f"bank{groups[g][0]}_emptied"].h, groups[g][1] + 1

        def free_for(g):
            return S[f"bank{groups[g][0]}_emptied"].h, groups[g][1]

        def chan(w, c0, n=256):
            return ("chan", w, c0, n)

        def tok(w, k0, nk, n0):
            return ("tok", w, k0, nk, n0)

        RW0 = 3 * DA_W
        chunks = [chan("w_in", RW0 + RW_IN)] + [chan("w_in", RW0 + 256 * i) for i in range(3)] + [chan("w_in", RW0 + 768, 128)]
        chunks += [chan("w_in", 256 * i) for i in range(4)]
        chunks += [tok("w_in", 4 * i, 4, 2 * DA_W) for i in range(2)]
        first = {"w_out": len(chunks)}
        chunks += [tok("w_out", 4 * i, 4, 512 * h) for h in range(2) for i in range(2)]
        first["ca_wq"] = len(chunks)
        chunks += [chan("ca_wq", 256 * i) for i in range(4)]
        first["ca_wkv"] = len(chunks)
        chunks += [chan("ca_wkv", 256 * i) for i in range(4)]
        chunks += [tok("ca_wkv", 4 * i, 4, D + 512 * h) for h in range(2) for i in range(2)]
        first["ca_wo"] = len(chunks)
        chunks += [tok("ca_wo", 4 * i, 4, 512 * h) for h in range(2) for i in range(2)]
        first["ffn_up"] = len(chunks)
        for i in range(FT // 2):
            chunks += [chan("ffn_w_up", 256 * i), chan("ffn_w_up", D_FF + 256 * i)]
        first["ffn_down"] = len(chunks)
        chunks += [tok("ffn_w_down", 4 * i, min(4, FT - 4 * i), 512 * h) for h in range(2) for i in range(6)]

        def slot(of, c):
            v = of[:, c % SLOTS, :]
            kind = chunks[c]
            if kind[0] == "chan":
                return v[:, 0:8 * kind[3]].rearrange("p (k n) -> p k n", n=kind[3])
            return v[:, 0:kind[3] * 512].rearrange("p (k n) -> p k n", n=512)

        low_by = ["dve" if first["ca_wkv"] <= c < first["ca_wo"] or c >= first["ffn_up"] + 2 else "pool" for c in range(len(chunks))]

        def low_done(c):
            return S[f"chunk_low_{low_by[c]}"].h, low_by[:c + 1].count(low_by[c])

        lnrow3 = raw[:, len(chunks) % SLOTS, :].rearrange("p (a d) -> p a d", a=2)

        groups = {}
        used = {}
        block = ctx.enter_context(nc.Block())

        def layers(eng, name, prologue, body):
            def rest():
                eng.drain().then_inc(quiet.h, 1)
                eng.wait_ge(go[name].h, 1)
                eng.sem_clear(go[name].h)

            new_segment()
            prologue()
            rest()
            with eng.Fori(0, DEPTH) as l:
                new_segment()
                body(l)
                rest()

        @block.tensor
        def _(pe):
            state = {}

            def fresh():
                state.update(uses=[0] * 8, chunk=0)
                share_banks(turn=[0, 1, 2, 3, 4, 5, 6, 7])

            def share_banks(**pools):
                state["pools"] = pools

            def take_bank(g, kind="turn"):
                pool = state["pools"][kind]
                b = pool.pop(0)
                pool.append(b)
                assert g not in groups, g
                groups[g] = (b, state["uses"][b])
                state["uses"][b] += 1
                return banks[b]

            mm = nc.tensor.matmul
            ALL = slice(None)

            def next_chunk():
                c = state["chunk"]
                state["chunk"] += 1
                return c, (slot(split[0], c), slot(split[1], c))

            def product(ps, a, b, start, stop):
                for i, (pa, pb) in enumerate(((a[0], b[0]), (a[0], b[1]), (a[1], b[0]))):
                    ins = mm(ps, pa, pb, start=start and i == 0, stop=stop and i == 2)
                return ins

            def part(v, *at):
                return v[0][at], v[1][at]

            def used_with_group(c, g):
                used[c] = filled(g)

            def used_with_step(c):
                one = raises("chunk_used")
                used[c] = latest("chunk_used")
                return one

            def transposes(g, srcs):
                ps = take_bank(g)
                pe.wait_ge(*free_for(g))
                for i, s in enumerate(srcs):
                    ins = nc.tensor.transpose(ps[:, i * P:(i + 1) * P], s, ident)
                ins.then_inc(*fills(g))

            def to_channels(tag, t):
                for h in range(2):
                    transposes(f"{tag}{t}{h}", [x[:, t, (4 * h + i) * P:(4 * h + i + 1) * P] for i in range(4)])

            def project_channels(names, rhs, n=T):
                for _ in projection_steps(names, rhs, n):
                    pass

            def projection_steps(names, rhs, n=T):
                names = list(names)
                while names:
                    c, w = next_chunk()
                    pe.wait_ge(*low_done(c))
                    for j in range(chunks[c][3] // P):
                        g = names.pop(0)
                        ps = take_bank(g)
                        pe.wait_ge(*free_for(g))
                        for k in range(KT):
                            ins = product(ps[:, 0:n], part(w, ALL, k, slice(j * P, (j + 1) * P)), part(rhs, ALL, k), k == 0, k == KT - 1)
                        ins.then_inc(*fills(g))
                        if j == chunks[c][3] // P - 1:
                            used_with_group(c, g)
                        yield g

            def project_tokens(tag, lhs, nk, tiles=NT, halves=(0, 1)):
                for h in halves:
                    out = [take_bank(f"{tag}{t}{h}") for t in range(tiles)]
                    for t in range(tiles):
                        pe.wait_ge(*free_for(f"{tag}{t}{h}"))
                    k0 = 0
                    while k0 < nk:
                        c, w = next_chunk()
                        n = chunks[c][3]
                        pe.wait_ge(*low_done(c))
                        for t in range(tiles):
                            for k in range(n):
                                ins = product(out[t][:, :], part(lhs, ALL, k0 + k, slice(t * P, (t + 1) * P)), part(w, ALL, k),
                                              k0 + k == 0, k0 + k == nk - 1)
                            if k0 + n == nk:
                                ins.then_inc(*fills(f"{tag}{t}{h}"))
                        if k0 + n == nk:
                            used_with_group(c, f"{tag}{tiles - 1}{h}")
                        else:
                            ins.then_inc(*used_with_step(c))
                        k0 += n

            def prologue():
                fresh()

            def s5_inputs_T(j):
                pe.wait_ge(S["s5_b"].h, j + 1)
                ps = take_bank(f"bT{j}")
                pe.wait_ge(*free_for(f"bT{j}"))
                for i in range(2):
                    ins = nc.tensor.transpose(ps[:, i * P:(i + 1) * P], bpad[:, i, :], ident)
                ins.then_inc(*fills(f"bT{j}"))

            def s5_inputs(j):
                pe.wait_ge(*emptied(f"bT{j}"))
                for i in range(2):
                    ps = take_bank(f"bu{j}{i}", "s5_in")
                    pe.wait_ge(*free_for(f"bu{j}{i}"))
                    mm(ps[:, :], bT[:, i, :], uT[:, j // 4, :], start=True, stop=True).then_inc(*fills(f"bu{j}{i}"))

            def s5_out(j):
                ct, jj = j // 4, j % 4
                if jj == 0:
                    state["y"] = take_bank(f"y{ct}", "s5_y")
                    pe.wait_ge(*free_for(f"y{ct}"))
                pe.wait_ge(S["s5_x"].h, 2 * (j + 1))
                pe.wait_ge(S["s5_c"].h, j + 1)
                for i in range(2):
                    ins = mm(state["y"][:, :], cpad[:, i, :], s_n[2 * i], start=jj == 0 and i == 0, stop=jj == 3 and i == 1)
                if jj == 3:
                    ins.then_inc(*fills(f"y{ct}"))
                else:
                    ins.then_inc(S["s5_y"].h, 1)

            def s5_gate():
                pe.wait_ge(S["s5_z"].h, 2)
                for n in range(2):
                    ps = take_bank(f"glu{n}")
                    pe.wait_ge(*free_for(f"glu{n}"))
                    for k in range(2):
                        ins = mm(ps[:, :], gluw[:, k, n * P:(n + 1) * P], zT[:, k, :], start=k == 0, stop=k == 1)
                    ins.then_inc(*fills(f"glu{n}"))

            def s5_norm():
                pe.wait_ge(S["s5_sq"].h, 1)
                ps = take_bank("s5ss")
                pe.wait_ge(*free_for("s5ss"))
                for k in range(2):
                    ins = mm(ps[:, :], ones, s_r[:, k, :], start=k == 0, stop=k == 1)
                ins.then_inc(*fills("s5ss"))

            def mixer_projections():
                for _ in projection_steps([f"rw{i}" for i in range(RW_TILES)], xT):
                    yield
                for i, nm in enumerate(projection_steps([f"q{i}" for i in range(4)] + [f"k{i}" for i in range(4)], xT)):
                    if i:
                        rotate(i - 1)
                    yield
                cs = [next_chunk() for _ in range(2)]
                for t in range(NT):
                    g = f"v{t}"
                    ps = take_bank(g)
                    pe.wait_ge(*free_for(g))
                    for k in range(KT):
                        if t == 0 and k % 4 == 0:
                            pe.wait_ge(*low_done(cs[k // 4][0]))
                        ins = product(ps[:, :], part(xT, ALL, k, slice(t * P, (t + 1) * P)), part(cs[k // 4][1], ALL, k % 4), k == 0, k == KT - 1)
                    ins.then_inc(*fills(g))
                    if t == 0:
                        rotate(7)
                    if t == NT - 1:
                        for c, _ in cs:
                            used_with_group(c, g)
                    yield

            def rotate(i):
                pe.wait_ge(*emptied(f"{'qk'[i // 4]}{i % 4}"))
                ps = take_bank(f"rot{i}", "rot")
                pe.wait_ge(*free_for(f"rot{i}"))
                mm(ps[:, :], rot, (qT if i < 4 else kT)[:, i % 4, :], start=True, stop=True).then_inc(*fills(f"rot{i}"))

            def attention():
                todo = [(h, i) for h in range(DA_HEADS) for i in range(NT)]

                def scores(n):
                    h, i = todo[n]
                    for s in range(2):
                        g = f"sc{h}{i}{s}"
                        ps = take_bank(g)
                        pe.wait_ge(*free_for(g))
                        r = slice(64 * s, 64 * s + 64)
                        mm(ps[:, 0:(i + 1) * P], qT[r, h, i * P:(i + 1) * P], kT[r, h, 0:(i + 1) * P], start=True, stop=False)
                        ins = mm(ps[:, i * P + 64:(i + 1) * P], K[0:1, C_MROW:C_MROW + P], K[0:1, C_NEG:C_NEG + CH],
                                 start=False, stop=True)
                        ins.then_inc(*fills(g))

                def weights(n):
                    h, i = todo[n]
                    pe.wait_ge(S["attn_p"].h, n + 1)
                    transposes(f"aT{h}{i}", [AP_[:, 2 * (n % 2), b * P:(b + 1) * P] for b in range(i + 1)])
                    if i == NT - 1:
                        for ii in range(NT):
                            pe.wait_ge(*emptied(f"aT{h}{ii}"))
                        ps = take_bank(f"o{h}")
                        pe.wait_ge(*free_for(f"o{h}"))
                        for b in range(NT):
                            ins = mm(ps[:, b * P:T], vtok[:, b, h * P:(h + 1) * P], aT[:, b, b * P:T], start=b == 0, stop=b == NT - 1)
                        ins.then_inc(*fills(f"o{h}"))

                def norm(h):
                    pe.wait_ge(*emptied(f"o{h}"))
                    ps = take_bank(f"oss{h}")
                    pe.wait_ge(*free_for(f"oss{h}"))
                    mm(ps[:, :], ones, osq, start=True, stop=True).then_inc(*fills(f"oss{h}"))

                for n in range(len(todo) + 1):
                    if n < len(todo):
                        scores(n)
                    if n:
                        weights(n - 1)
                        if (n - 1) % NT == 1 and (n - 1) // NT:
                            norm((n - 1) // NT - 1)
                norm(DA_HEADS - 1)

            def rwkv(j):
                if j == 0:
                    pe.wait_ge(S["lr_ready"].h, 3)
                for nm, r in (("w", slice(0, 32)), ("a", slice(32, 64)), ("g", slice(64, 128))):
                    g = f"lr{nm}{j}"
                    ps = take_bank(g)
                    pe.wait_ge(*free_for(g))
                    mm(ps[:, :], lrw[r, j * P:(j + 1) * P], rw["LR"][r, :], start=True, stop=True).then_inc(*fills(g))
                pe.wait_ge(S["rw_sq"].h, 2 * j + 1)
                ps = take_bank(f"kss{j}")
                pe.wait_ge(*free_for(f"kss{j}"))
                mm(ps[:, :], bones, rw["t1"], start=True, stop=True).then_inc(*fills(f"kss{j}"))
                pe.wait_ge(S["rw_bonus"].h, j + 1)
                ps = take_bank(f"bon{j}")
                pe.wait_ge(*free_for(f"bon{j}"))
                mm(ps[:, :], bones, rw["bonus"], start=True, stop=True).then_inc(*fills(f"bon{j}"))
                pe.wait_ge(S["rw_gram_in"].h, j + 1)
                for nm, src in (("A", rw["A"]), ("v", PR[:, 4 + j, 2:]), ("Bh", rw["Bh"]), ("Kh", rw["Kh"])):
                    transposes(f"tk{nm}{j}", [src[:, i * P:(i + 1) * P] for i in range(NT)])
                if j == 0:
                    pe.wait_ge(S["hT_da"].h, DA_HEADS)
                for hh in range(2):
                    r = slice(64 * hh, 64 * hh + 64)
                    for nm, a, b in (("ABT", "B", "A"), ("AB", "A", "B"), ("RBT", "B", "R"), ("RKT", "K", "R"), ("AKT", "K", "A")):
                        g = f"gr{nm}{j}{hh}"
                        ps = take_bank(g)
                        pe.wait_ge(*free_for(g))
                        for i in range(NT):
                            c = slice(i * P, (i + 1) * P)
                            ins = mm(ps[:, c], rw[a][r, c], rw[b][r, c], start=True, stop=True)
                        ins.then_inc(*fills(g))
                for lv in range(len(LEVELS)):
                    for hh in range(2):
                        for nm in ("T", "TT"):
                            if lv:
                                pe.wait_ge(*emptied(f"d{nm}{j}{lv - 1}{hh}"))
                    if lv == 0:
                        pe.wait_ge(S["rw_T"].h, 4 * (j + 1))
                    for hh in range(2):
                        g = f"Z{j}{lv}{hh}"
                        ps = take_bank(g)
                        pe.wait_ge(*free_for(g))
                        for i in range(NT):
                            c = slice(i * P, (i + 1) * P)
                            ins = mm(ps[:, c], mAB[:, hh, c], Ti[:, hh, c], start=True, stop=True)
                        ins.then_inc(*fills(g))
                    for hh in range(2):
                        pe.wait_ge(*emptied(f"Z{j}{lv}{hh}"))
                        for nm, a, b in (("T", TiT, rZ), ("TT", rZ, TiT)):
                            g = f"d{nm}{j}{lv}{hh}"
                            ps = take_bank(g)
                            pe.wait_ge(*free_for(g))
                            for i in range(NT):
                                c = slice(i * P, (i + 1) * P)
                                ins = mm(ps[:, c], a[:, hh, c], b[:, hh, c], start=True, stop=True)
                            ins.then_inc(*fills(g))
                for hh in range(2):
                    for nm in ("RBT", "RKT", "AKT"):
                        pe.wait_ge(*emptied(f"gr{nm}{j}{hh}"))
                for nm in ("v", "Bh", "Kh"):
                    pe.wait_ge(*emptied(f"tk{nm}{j}"))
                for hh in range(2):
                    g = f"MV{j}{hh}"
                    ps = take_bank(g)
                    pe.wait_ge(*free_for(g))
                    for i in range(NT):
                        ins = mm(ps[:, i * CH:(i + 1) * CH], mAK[:, hh, i * P:(i + 1) * P], vT_[:, i, 64 * hh:64 * hh + 64],
                                 start=True, stop=True)
                    ins.then_inc(*fills(g))
                for hh in range(2):
                    pe.wait_ge(*emptied(f"dT{j}{len(LEVELS) - 1}{hh}"))
                    pe.wait_ge(*emptied(f"dTT{j}{len(LEVELS) - 1}{hh}"))
                for hh in range(2):
                    pe.wait_ge(*emptied(f"MV{j}{hh}"))
                    pe.wait_ge(*emptied(f"tkA{j}"))
                    g = f"UW{j}{hh}"
                    ps = take_bank(g)
                    pe.wait_ge(*free_for(g))
                    for i in range(NT):
                        c = slice(i * P, (i + 1) * P)
                        ins = mm(ps[:, c], TiT[:, hh, c], zA[:, hh, c], start=True, stop=True)
                    ins.then_inc(*fills(g))
                for hh in range(2):
                    pe.wait_ge(*emptied(f"UW{j}{hh}"))

                def U(hh, i, rows=slice(0, P)):
                    return uw[rows, hh, i * P:i * P + CH]

                def W(hh, i, rows=slice(0, P)):
                    return uw[rows, hh, i * P + CH:(i + 1) * P]

                ps = take_bank(f"Q{j}")
                pe.wait_ge(*free_for(f"Q{j}"))
                for hh in range(2):
                    for i in range(NT):
                        c = slice(i * P, (i + 1) * P)
                        ins = mm(ps[64 * hh:64 * hh + 64, c], W(hh, i), mRB[:, hh, c], start=True, stop=True)
                ins.then_inc(*fills(f"Q{j}"))
                for par in range(2):
                    rows = slice(64 * par, 64 * par + 64)
                    g = f"GH{j}{par}"
                    ps = take_bank(g)
                    pe.wait_ge(*free_for(g))
                    for hh in range(2):
                        out = slice(64 * hh, 64 * hh + 64)
                        hc = slice(64 * hh, 64 * hh + 64)
                        for i in range(NT):
                            mm(ps[out, i * CH:(i + 1) * CH], W(hh, i, rows), bT_[rows, i, hc], start=True, stop=True)
                        for i in range(NT):
                            c = slice(256 + i * CH, 256 + (i + 1) * CH)
                            mm(ps[out, c], bT_[rows, i, hc], U(hh, i, rows), start=True, stop=False)
                            ins = mm(ps[out, c], kT_[rows, i, hc], vT_[rows, i, hc], start=False, stop=True)
                    ins.then_inc(*fills(g))
                for par in range(2):
                    pe.wait_ge(*emptied(f"GH{j}{par}"))
                pe.wait_ge(S["rw_state"].h, j + 1)
                for c in range(1, NCH - 1):
                    for hh in range(2):
                        r = slice(64 * hh, 64 * hh + 64)
                        g = f"S{j}{c}{hh}"
                        ps = take_bank(g)
                        pe.wait_ge(*free_for(g))
                        mm(ps[r, 0:CH], rG[r, c * CH:(c + 1) * CH], rS[r, c * CH:(c + 1) * CH], start=True, stop=True).then_inc(*fills(g))
                    for hh in range(2):
                        pe.wait_ge(*emptied(f"S{j}{c}{hh}"))
                pe.wait_ge(*emptied(f"Q{j}"))
                for hh in range(2):
                    r = slice(64 * hh, 64 * hh + 64)
                    g = f"Y{j}{hh}"
                    ps = take_bank(g)
                    pe.wait_ge(*free_for(g))
                    for i in range(NT):
                        c = slice(i * P, (i + 1) * P)
                        mm(ps[r, c], U(hh, i), mRB[:, hh, c], start=i == 0, stop=False, skip_group_check=True)
                        mm(ps[r, c], vT_[:, i, r], mRK[:, hh, c], start=False, stop=False, skip_group_check=True)
                    for c in range(1, NCH):
                        cc = slice(c * CH, (c + 1) * CH)
                        ins = mm(ps[r, cc], rS[r, cc], rQ[r, cc], start=False, stop=c == NCH - 1, skip_group_check=True)
                    ins.then_inc(*fills(g))
                for hh in range(2):
                    pe.wait_ge(*emptied(f"Y{j}{hh}"))
                ps = take_bank(f"ym{j}")
                pe.wait_ge(*free_for(f"ym{j}"))
                mm(ps[:, :], bones, rY, start=True, stop=True).then_inc(*fills(f"ym{j}"))
                pe.wait_ge(S["rw_ysq"].h, j + 1)
                ps = take_bank(f"yv{j}")
                pe.wait_ge(*free_for(f"yv{j}"))
                mm(ps[:, :], bones, rw["t1"], start=True, stop=True).then_inc(*fills(f"yv{j}"))

            def cross():
                todo = [(h, i) for h in range(MEM_HEADS) for i in range(NT)]

                def scores(n):
                    h, i = todo[n]
                    g = f"cs{h}{i}"
                    ps = take_bank(g)
                    pe.wait_ge(*free_for(g))
                    for k in range(2):
                        ins = mm(ps[:, 0:N_MEM], q2[:, 2 * h + k, i * P:(i + 1) * P], mK[:, 2 * h + k, :], start=k == 0, stop=k == 1)
                    ins.then_inc(*fills(g))

                def weights(n):
                    h, i = todo[n]
                    pe.wait_ge(S["ca_p"].h, n + 1)
                    transposes(f"pT{h}{i}", [p2[:, n % 2, m * P:(m + 1) * P] for m in range(MT)])
                    if i == NT - 1:
                        for ii in range(NT):
                            pe.wait_ge(*emptied(f"pT{h}{ii}"))
                        for d in range(2):
                            g = f"co{h}{d}"
                            ps = take_bank(g)
                            pe.wait_ge(*free_for(g))
                            for m in range(MT):
                                ins = mm(ps[:, :], mV[:, m, (2 * h + d) * P:(2 * h + d + 1) * P], pT2[:, m, :], start=m == 0, stop=m == 1)
                            ins.then_inc(*fills(g))

                for n in range(len(todo) + 1):
                    if n < len(todo):
                        scores(n)
                    if n:
                        weights(n - 1)

            def body(l):
                fresh()
                for t in range(NT):
                    to_channels("x0", t)
                pe.wait_ge(S["sheets"].h, 1)
                for i, n in enumerate((S1_N, S2_N, 24)):
                    ps = take_bank(f"sheet{i}")
                    pe.wait_ge(*free_for(f"sheet{i}"))
                    nc.tensor.transpose(ps[:, 0:n], sheet[0:n, i, :], ident[0:n, 0:n]).then_inc(*fills(f"sheet{i}"))
                ps = take_bank("cT")
                pe.wait_ge(*free_for("cT"))
                for i in range(2):
                    for ct in range(2):
                        ins = nc.tensor.transpose(ps[:, (2 * i + ct) * P:(2 * i + ct + 1) * P], cn[:, i, ct, :], ident)
                ins.then_inc(*fills("cT"))
                pe.wait_ge(S["lam_row"].h, 1)
                ps = take_bank("lam")
                pe.wait_ge(*free_for("lam"))
                mm(ps[:, 0:2], ones[0:1, :], lamr[0:1, 4, 0:2], start=True, stop=True).then_inc(*fills("lam"))
                for t in range(NT):
                    for h in range(2):
                        pe.wait_ge(*emptied(f"x0{t}{h}"))
                for nm in ("sheet0", "sheet1", "sheet2", "lam"):
                    pe.wait_ge(*emptied(nm))
                share_banks(turn=[0, 1, 2], rot=[3, 7], s5_in=[4, 5], s5_y=[6])
                project_channels(["u0", "u1"], xT)
                steps = mixer_projections()
                pe.wait_ge(*emptied("u0"))
                pe.wait_ge(*emptied("u1"))
                s5_inputs_T(0)
                next(steps)
                s5_inputs(0)
                for j in range(S5_TILES):
                    next(steps)
                    if j + 1 < S5_TILES:
                        s5_inputs_T(j + 1)
                    if j:
                        s5_out(j - 1)
                    next(steps)
                    if j + 1 < S5_TILES:
                        s5_inputs(j + 1)
                s5_out(S5_TILES - 1)
                next(steps)
                s5_gate()
                next(steps)
                s5_norm()
                assert next(steps, "done") == "done"
                share_banks(turn=[0, 1, 2, 3, 4, 5, 6, 7])
                for t in range(NT):
                    pe.wait_ge(*emptied(f"v{t}"))
                pe.wait_ge(S["rope_done"].h, 8)
                attention()
                for j in range(2):
                    rwkv(j)
                pe.wait_ge(S["hT_s5"].h, 2)
                pe.wait_ge(S["hT_da"].h, DA_HEADS)
                pe.wait_ge(S["hT_rw"].h, 2)
                project_tokens("wo", hT, KT)
                for t in range(NT):
                    pe.wait_ge(S["ln_out_dve"].h, t + 1)
                    pe.wait_ge(S["ln_out_pool"].h, t + 1)
                    to_channels("x1", t)
                pe.wait_ge(S["mem_loaded"].h, 16)
                for m in range(MT):
                    for h in range(2):
                        transposes(f"mem{m}{h}", [memtok[:, m, (4 * h + i) * P:(4 * h + i + 1) * P] for i in range(4)])
                for t in range(NT):
                    for h in range(2):
                        pe.wait_ge(*emptied(f"x1{t}{h}"))
                project_channels([f"cq{i}" for i in range(KT)], xT)
                for m in range(MT):
                    for h in range(2):
                        pe.wait_ge(*emptied(f"mem{m}{h}"))
                project_channels([f"mk{i}" for i in range(KT)], memT, N_MEM)
                project_tokens("mv", memT, KT, tiles=MT)
                for i in range(KT):
                    pe.wait_ge(*emptied(f"cq{i}"))
                    pe.wait_ge(*emptied(f"mk{i}"))
                for m in range(MT):
                    pe.wait_ge(*emptied(f"mv{m}0"))
                    pe.wait_ge(*emptied(f"mv{m}1"))
                cross()
                for h in range(MEM_HEADS):
                    pe.wait_ge(*emptied(f"co{h}0"))
                    pe.wait_ge(*emptied(f"co{h}1"))
                project_tokens("cw", o2, KT)
                for t in range(NT):
                    pe.wait_ge(S["ln_out_dve"].h, NT + t + 1)
                    pe.wait_ge(S["ln_out_pool"].h, NT + t + 1)
                    to_channels("x2", t)
                for t in range(NT):
                    for h in range(2):
                        pe.wait_ge(*emptied(f"x2{t}{h}"))
                names = []
                for i in range(FT // 2):
                    names += [f"fa{2 * i}", f"fa{2 * i + 1}", f"fg{2 * i}", f"fg{2 * i + 1}"]
                project_channels(names, xT)
                pe.wait_ge(S["hid_low"].h, FT)
                project_tokens("dn", hid, FT)

            layers(pe, "pe", prologue, body)

        small = {}

        @block.sync
        def _(sp):
            def rest():
                sp.wait_ge(quiet.h, 4)
                sp.sem_clear(quiet.h)
                nums = sorted(s.h.num for s in S.values())
                assert nums == list(range(nums[0], nums[-1] + 1))
                sp.sem_clear(range(nums[0], nums[-1] + 1))
                for n in go:
                    sp.sem_inc(go[n].h, 1)

            def load(dst, src):
                sp.dma_start(dst, src).then_inc(S["small_loaded"].h, 16)
                S["small_loaded"].n += 16

            new_segment()
            load(K[:, :], io["const"])
            load(posr.bitcast(i32), io["positions"].to_broadcast([P, T]))
            for h in range(2):
                load(x[:, 2 * h:2 * h + 2, :], io["x"][0, 2 * h * P:(2 * h + 2) * P, :].rearrange("(t p) d -> p t d", p=P))
            rest()
            with sp.Fori(0, DEPTH) as l:
                new_segment()

                def layer_chunk(c):
                    kind = chunks[c]
                    w = io[kind[1]][l]
                    if kind[0] == "chan":
                        return w[:, kind[2]:kind[2] + kind[3]].rearrange("(k p) n -> p k n", p=P)
                    k0, nk, n0 = kind[2:]
                    return w[k0 * P:(k0 + nk) * P, n0:n0 + 512].rearrange("(k p) n -> p k n", p=P)

                def load_chunk(c):
                    if c >= SLOTS:
                        sp.wait_ge(*low_done(c - SLOTS))
                    sp.dma_start(slot(raw, c), layer_chunk(c)).then_inc(S[f"slot{c % SLOTS}_loaded"].h, 16)

                load(sheet[0:S1["ffn_conv_w"][1], 0, :], io["ffn_conv_w"][l].rearrange("j (c p) -> (j c) p", p=P))
                load(sheet[S1["ffn_conv_b"][0]:S1_N, 0, :], io["ffn_conv_b"][l].rearrange("(c p) -> c p", p=P))
                for name, (at, n) in S2.items():
                    src = io[name][l]
                    if name == "rw_r_k":
                        src = src.rearrange("(c a) d -> c (a d)", a=2)
                    else:
                        src = src.rearrange("(c p) -> c p", p=P)
                    load(sheet[at:at + n, 1, :], src)
                load(sheet[8:16, 2, :], io["s5_a_re"][l].rearrange("(j a) p -> j (a p)", a=2))
                load(sheet[16:24, 2, :], io["s5_a_im"][l].rearrange("(j a) p -> j (a p)", a=2))
                load(lamr[0:8, 5, 0:2], io["s5_log_step"][l].rearrange("(j a) -> j a", a=2))
                for i, name in enumerate(("da_lam_q1", "da_lam_k1", "da_lam_q2", "da_lam_k2")):
                    load(lamr[0:1, i, :], io[name][l].unsqueeze(0))
                load(lamr[0:1, 4, 2:4], io["lambda_inits"][l].unsqueeze(0))
                load_chunk(0)
                load_chunk(1)
                load(lrw[0:32, :], io["rw_w2"][l])
                load(lrw[32:64, :], io["rw_a2"][l])
                load(lrw[64:128, :], io["rw_g2"][l])
                for i, nm in enumerate(("re", "im")):
                    load(bn[:, i, :, :], io[f"s5_b_{nm}"][l].rearrange("(j a) p h -> (a p) j h", a=2))
                    for dup in range(2):
                        load(cn[:, i, :, dup * 64:dup * 64 + 64], io[f"s5_c_{nm}"][l].rearrange("(c g) h p -> (g h) c p", c=2))
                load(gluw, io["s5_glu_w"][l].rearrange("(k p) n -> p k n", p=P))
                small["layer"] = S["small_loaded"].n
                for c in range(2, len(chunks)):
                    load_chunk(c)
                sp.wait_ge(*low_done(len(chunks) - SLOTS))
                for i, nm in enumerate("gb"):
                    sp.dma_start(lnrow3[:, i, :], io[f"ln3_{nm}"][l].unsqueeze(0).to_broadcast([P, D])).then_inc(S["rows_loaded"].h, 16)
                rest()
            for h in range(2):
                sp.dma_start(io["out"][0, 2 * h * P:(2 * h + 2) * P, :].rearrange("(t p) d -> p t d", p=P),
                             x[:, 2 * h:2 * h + 2, :]).then_inc(out_done.h, 16)
            sp.wait_ge(out_done.h, 32)

        @block.scalar
        def _(act):
            A = nc.scalar.activation

            def prologue():
                act.wait_ge(S["s5_col_v"].h, 1)
                A(ropeS[:, :], tr, ACT.Sin).then_inc(*raises("act_step"))
                act.wait_ge(*latest("act_step"))
                A(tn, tr, ACT.Abs).then_inc(*raises("act_step"))
                act.wait_ge(*latest("act_step"))
                A(ropeC[:, :], tn, ACT.Sin, bias=const("half_pi"), scale=-1.0).then_inc(*raises("act_step"))
                act.wait_ge(*latest("act_step"))

            def body(l):

                def rows(n, dst):
                    for i, nm in enumerate("gb"):
                        act.dma_start(dst[:, i, :], io[f"ln{n}_{nm}"][l].unsqueeze(0).to_broadcast([P, D])).then_inc(S["rows_loaded"].h, 16)

                def chunk_high(c):
                    act.wait_ge(S[f"slot{c % SLOTS}_loaded"].h, 16 * (c // SLOTS + 1))
                    if c >= SLOTS:
                        act.wait_ge(*used[c - SLOTS])
                    A(slot(split[0], c), slot(raw, c), ACT.Copy).then_inc(*raises("chunk_high"))
                    act.wait_ge(*latest("chunk_high"))

                def part_high(name, src, k):
                    A(hT[0][:, k, :], src, ACT.Copy).then_inc(*raises(name))
                    act.wait_ge(*latest(name))

                def copy_out(g, dst, n=T):
                    act.wait_ge(*filled(g))
                    ps = bank(g)
                    A(dst, ps[:, 0:n], ACT.Copy).then_inc(*empties(g))
                    act.wait_ge(*emptied(g))

                def channels_out(tag, t):
                    for h in range(2):
                        g = f"{tag}{t}{h}"
                        act.wait_ge(*filled(g))
                        ps = bank(g)
                        A(xT[0][:, 4 * h:4 * h + 4, t * P:(t + 1) * P], ps[:, :].rearrange("p (k t) -> p k t", k=4), ACT.Copy).then_inc(*raises("x_high"))
                        act.wait_ge(*latest("x_high"))

                def layer_norm(n, t):
                    act.wait_ge(S["ln_var"].h, NT * n + t + 1)
                    v = stat[:, t, 1:2]
                    A(v, v, ACT.Ln, bias=const("ln_eps")).then_inc(*raises("act_step"))
                    act.wait_ge(*latest("act_step"))
                    A(v, v, ACT.Exp, scale=-0.5).then_inc(*raises("ln_rstd"))
                    act.wait_ge(*latest("ln_rstd"))

                for t in range(NT):
                    channels_out("x0", t)
                chunk_high(0)
                chunk_high(1)
                act.wait_ge(S["lam_in"].h, 1)
                A(lamr[0:1, 4, 4:6], lamr[0:1, 4, 6:8], ACT.Exp).then_inc(*raises("lam_exp"))
                act.wait_ge(*latest("lam_exp"))
                act.wait_ge(S["s5_col_v"].h, 1)
                A(s5c[:, 0, :], col3[:, 0:8], ACT.Exp).then_inc(*raises("s5_col_a"))
                act.wait_ge(*latest("s5_col_a"))
                act.wait_ge(S["s5_col_v"].h, 2)
                A(s5c[:, 3, :], s5c[:, 1, :], ACT.Exp).then_inc(*raises("s5_col_a"))
                act.wait_ge(*latest("s5_col_a"))
                A(s5c[:, 8, :], s5c[:, 5, :], ACT.Sin).then_inc(*raises("act_step"))
                act.wait_ge(*latest("act_step"))
                A(s5c[:, 9, :], s5c[:, 5, :], ACT.Abs).then_inc(*raises("act_step"))
                act.wait_ge(*latest("act_step"))
                A(s5c[:, 9, :], s5c[:, 9, :], ACT.Sin, bias=const("half_pi"), scale=-1.0).then_inc(*raises("s5_col_a"))
                act.wait_ge(*latest("s5_col_a"))
                act.wait_ge(*filled("cT"))
                ps = bank("cT")
                A(cT[:, 0:2, :], ps[:, 0:2 * P].rearrange("p (a b) -> p a b", a=2), ACT.Copy).then_inc(*raises("act_step"))
                act.wait_ge(*latest("act_step"))
                A(cT[:, 2:4, :], ps[:, 2 * P:].rearrange("p (a b) -> p a b", a=2), ACT.Copy, scale=-1.0).then_inc(*empties("cT"))
                act.wait_ge(*emptied("cT"))
                def s5_tables(j):
                    act.wait_ge(S["s5_tables"].h, j + 1)
                    if j >= 2:
                        act.wait_ge(S["s5_n"].h, 4 * (j - 1))
                    A(s_sin[j % 2], s_turn, ACT.Sin, scale=TWO_PI_SAFE).then_inc(*raises("act_step"))
                    act.wait_ge(*latest("act_step"))
                    A(s_round, s_turn, ACT.Abs).then_inc(*raises("act_step"))
                    act.wait_ge(*latest("act_step"))
                    A(s_cos[j % 2], s_round, ACT.Sin, bias=const("half_pi"), scale=-TWO_PI_SAFE).then_inc(*raises("s5_col_a"))
                    act.wait_ge(*latest("s5_col_a"))

                def s5_inputs_T(j):
                    act.wait_ge(*filled(f"bT{j}"))
                    ps = bank(f"bT{j}")
                    if j:
                        act.wait_ge(*filled(f"bu{j - 1}1"))
                    A(bT, ps[:, 0:2 * P].rearrange("p (a b) -> p a b", a=2), ACT.Copy).then_inc(*empties(f"bT{j}"))
                    act.wait_ge(*emptied(f"bT{j}"))

                copy_out("u0", uT[:, 0, :])
                copy_out("u1", uT[:, 1, :])
                results = [(f"rw{i}", PR[:, i, 2:T + 2]) for i in range(RW_TILES)]
                results += [(f"q{i}", qT[:, i, :]) for i in range(4)] + [(f"k{i}", kT[:, i, :]) for i in range(4)]
                results += [(f"v{t}", vtok[:, t, :]) for t in range(NT)]
                after = {1: 3, 3: 4, 5: 5, 6: 6, 8: 7, 10: 8, 12: 9, 14: 10}
                chunk_high(2)
                s5_tables(0)
                s5_inputs_T(0)
                copy_out(*results[0])
                for j in range(S5_TILES):
                    copy_out(*results[2 * j + 1])
                    if 2 * j + 1 in after:
                        chunk_high(after[2 * j + 1])
                    if j + 1 < S5_TILES:
                        s5_tables(j + 1)
                        s5_inputs_T(j + 1)
                    copy_out(*results[2 * j + 2])
                    if 2 * j + 2 in after:
                        chunk_high(after[2 * j + 2])
                act.wait_ge(*filled("y1"))
                for ct in range(2):
                    act.wait_ge(*emptied(f"y{ct}"))
                    A(zT[:, ct, :], yT[:, ct, :], ACT.Gelu_apprx_tanh).then_inc(*raises("s5_z"))
                    act.wait_ge(*latest("s5_z"))
                copy_out(*results[-2])
                for n in range(2):
                    act.wait_ge(*filled(f"glu{n}"))
                    ps = bank(f"glu{n}")
                    A(s_r[:, n, :], ps[:, :], ACT.Sigmoid, bias=col2[:, S2["s5_glu_b"][0] + n:S2["s5_glu_b"][0] + n + 1]).then_inc(*empties(f"glu{n}"))
                    act.wait_ge(*emptied(f"glu{n}"))
                act.wait_ge(S["s5_g"].h, 2)
                A(s_r, zT, ACT.Square).then_inc(*raises("s5_sq"))
                act.wait_ge(*latest("s5_sq"))
                copy_out(*results[-1])
                act.wait_ge(*filled("s5ss"))
                ps = bank("s5ss")
                A(yT[:, 0, :], ps[:, :], ACT.Ln, bias=const("rms_eps"), scale=1.0 / S5_W).then_inc(*raises("act_step"))
                act.wait_ge(*latest("act_step"))
                A(yT[:, 1, :], yT[:, 0, :], ACT.Exp, scale=-0.5).then_inc(*empties("s5ss"))
                act.wait_ge(*emptied("s5ss"))
                for ct in range(2):
                    act.wait_ge(S["s5_raw"].h, ct + 1)
                    part_high("hT_high", zT[:, ct, :], 6 + ct)
                act.wait_ge(S["s5_b"].h, S5_TILES)
                act.wait_ge(*filled("glu1"))
                act.dma_start(lev, io["level_masks"]).then_inc(S["levels_loaded"].h, 16)
                for c in range(first["w_out"], first["w_out"] + 2):
                    chunk_high(c)
                act.wait_ge(S["hT_s5"].h, 2)
                def attn_head_out(h):
                    act.wait_ge(*filled(f"o{h}"))
                    ps = bank(f"o{h}")
                    if h:
                        act.wait_ge(S["hT_da"].h, h)
                    A(oh, ps[:, :], ACT.Copy).then_inc(*raises("act_step"))
                    act.wait_ge(*latest("act_step"))
                    A(osq, ps[:, :], ACT.Square).then_inc(*empties(f"o{h}"))
                    act.wait_ge(*emptied(f"o{h}"))

                def attn_head_norm(h):
                    act.wait_ge(*filled(f"oss{h}"))
                    ps = bank(f"oss{h}")
                    A(orr, ps[:, :], ACT.Ln, bias=const("rms_eps"), scale=1.0 / P).then_inc(*empties(f"oss{h}"))
                    act.wait_ge(*emptied(f"oss{h}"))
                    A(orr, orr, ACT.Exp, scale=-0.5).then_inc(*raises("attn_rs"))
                    act.wait_ge(*latest("attn_rs"))

                def attn_head_high(h):
                    act.wait_ge(S["da_raw"].h, h + 1)
                    part_high("hT_high", oh, h)

                def attn_weights_out(n):
                    h, i = n // NT, n % NT
                    g = f"aT{h}{i}"
                    act.wait_ge(*filled(g))
                    ps = bank(g)
                    if h:
                        act.wait_ge(*filled(f"o{h - 1}"))
                    A(aT[:, 0:i + 1, i * P:(i + 1) * P], ps[:, 0:(i + 1) * P].rearrange("p (a b) -> p a b", a=i + 1), ACT.Copy).then_inc(*empties(g))
                    act.wait_ge(*emptied(g))

                for n in range(DA_HEADS * NT + 1):
                    h, i = n // NT, n % NT
                    if n < DA_HEADS * NT:
                        for s in range(2):
                            g = f"sc{h}{i}{s}"
                            act.wait_ge(*filled(g))
                            ps = bank(g)
                            act.wait_ge(S["attn_max"].h, 2 * n + s + 1)
                            if n >= 2:
                                act.wait_ge(*filled(f"aT{(n - 2) // NT}{(n - 2) % NT}"))
                            A(AP_[:, 2 * (n % 2) + s, 0:(i + 1) * P], ps[:, 0:(i + 1) * P], ACT.Exp,
                                   bias=stat[:, n % 2, 4 + s:5 + s], scale=0.125, accum_out=stat[:, n % 2, 6 + s:7 + s]).then_inc(*empties(g))
                            act.wait_ge(*emptied(g))
                    if n:
                        attn_weights_out(n - 1)
                        if (n - 1) % NT == NT - 1:
                            attn_head_out((n - 1) // NT)
                        if (n - 1) % NT == 1 and (n - 1) // NT:
                            attn_head_norm((n - 1) // NT - 1)
                        if (n - 1) % NT == 2 and (n - 1) // NT:
                            attn_head_high((n - 1) // NT - 1)
                attn_head_norm(DA_HEADS - 1)
                attn_head_high(DA_HEADS - 1)
                act.wait_ge(S["shift_done"].h, 7)
                LR = rw["LR"]
                A(LR[0:32, :], PR[0:32, 6, 2:], ACT.Tanh).then_inc(*raises("lr_ready"))
                act.wait_ge(*latest("lr_ready"))
                A(LR[32:64, :], PR[32:64, 6, 2:], ACT.Copy).then_inc(*raises("lr_ready"))
                act.wait_ge(*latest("lr_ready"))
                A(LR[64:128, :], PR[64:128, 6, 2:], ACT.Sigmoid).then_inc(*raises("lr_ready"))
                act.wait_ge(*latest("lr_ready"))
                for j in range(2):
                    def c2(name):
                        return col2[:, S2[name][0] + j:S2[name][0] + j + 1]

                    if j:
                        act.wait_ge(S["hT_rw"].h, 1)
                    act.wait_ge(S["rw_kk"].h, j + 1)
                    A(rw["t1"], rw["kk"], ACT.Square).then_inc(*raises("rw_sq"))
                    act.wait_ge(*latest("rw_sq"))
                    act.wait_ge(*filled(f"lrw{j}"))
                    ps = bank(f"lrw{j}")
                    A(rw["t0"], ps[:, :], ACT.Sigmoid, bias=c2("rw_w0")).then_inc(*raises("act_step"))
                    act.wait_ge(*latest("act_step"))
                    A(rw["t0"], rw["t0"], ACT.Exp, scale=-DECAY).then_inc(*empties(f"lrw{j}"))
                    act.wait_ge(*emptied(f"lrw{j}"))
                    act.wait_ge(*filled(f"lra{j}"))
                    ps = bank(f"lra{j}")
                    A(rw["a"], ps[:, :], ACT.Sigmoid, bias=c2("rw_a0")).then_inc(*empties(f"lra{j}"))
                    act.wait_ge(*emptied(f"lra{j}"))
                    act.wait_ge(*filled(f"lrg{j}"))
                    ps = bank(f"lrg{j}")
                    A(rw["g"], ps[:, :], ACT.Copy).then_inc(*empties(f"lrg{j}"))
                    act.wait_ge(*emptied(f"lrg{j}"))
                    act.wait_ge(*emptied(f"kss{j}"))
                    A(rw["t1"], rw["t1"], ACT.Sqrt).then_inc(*raises("rw_sq"))
                    act.wait_ge(*latest("rw_sq"))
                    act.wait_ge(*filled(f"tkA{j}"))
                    ps = bank(f"tkA{j}")
                    for i in range(2):
                        copy = A(zA.rearrange("p h (t c) -> p h t c", c=P)[:, i, :, CH:],
                                 ps[:, :].rearrange("p (t c) -> p t c", c=P)[:, :, i * CH:(i + 1) * CH], ACT.Copy)
                        if i:
                            copy.then_inc(*empties(f"tkA{j}"))
                            act.wait_ge(*emptied(f"tkA{j}"))
                        else:
                            copy.then_inc(*raises("act_step"))
                            act.wait_ge(*latest("act_step"))
                    for nm, dst in (("v", vT_), ("Bh", bT_), ("Kh", kT_)):
                        act.wait_ge(*filled(f"tk{nm}{j}"))
                        ps = bank(f"tk{nm}{j}")
                        A(dst, ps[:, :].rearrange("p (t c) -> p t c", c=P), ACT.Copy).then_inc(*empties(f"tk{nm}{j}"))
                        act.wait_ge(*emptied(f"tk{nm}{j}"))
                    for lv in range(len(LEVELS)):
                        for hh in range(2):
                            g = f"Z{j}{lv}{hh}"
                            act.wait_ge(*filled(g))
                            ps = bank(g)
                            A(rZ[:, hh, :], ps[:, :], ACT.Copy).then_inc(*empties(g))
                            act.wait_ge(*emptied(g))
                    for hh in range(2):
                        g = f"MV{j}{hh}"
                        act.wait_ge(*filled(g))
                        ps = bank(g)
                        A(zA.rearrange("p h (t c) -> p h t c", c=P)[:, hh, :, 0:CH], ps[:, 0:NT * CH].rearrange("p (t c) -> p t c", c=CH), ACT.Copy).then_inc(*empties(g))
                        act.wait_ge(*emptied(g))
                    for hh in range(2):
                        copy_out(f"UW{j}{hh}", uw[:, hh, :])
                    for hh in range(2):
                        r = slice(64 * hh, 64 * hh + 64)
                        g = f"Y{j}{hh}"
                        act.wait_ge(*filled(g))
                        ps = bank(g)
                        A(rY[r, :], ps[r, :], ACT.Copy).then_inc(*empties(g))
                        act.wait_ge(*emptied(g))
                    act.wait_ge(*emptied(f"ym{j}"))
                    A(rw["t1"], rY, ACT.Square).then_inc(*raises("rw_ysq"))
                    act.wait_ge(*latest("rw_ysq"))
                    act.wait_ge(*filled(f"yv{j}"))
                    ps = bank(f"yv{j}")
                    A(rw["t1"], ps[:, :], ACT.Ln, bias=const("lnx_eps"), scale=1.0 / CH).then_inc(*raises("act_step"))
                    act.wait_ge(*latest("act_step"))
                    A(rw["t1"], rw["t1"], ACT.Exp, scale=-0.5).then_inc(*empties(f"yv{j}"))
                    act.wait_ge(*emptied(f"yv{j}"))
                    act.wait_ge(S["rw_raw"].h, j + 1)
                    part_high("hT_high", rY, 4 + j)
                act.wait_ge(S["rw_gram_in"].h, 2)
                rows(1, lnrow1)
                act.wait_ge(S["hT_rw"].h, 2)
                act.dma_start(memtok, io["mem"][0].rearrange("(m p) d -> p m d", p=P)).then_inc(S["mem_loaded"].h, 16)
                c0 = first["ca_wq"]
                for c in range(first["w_out"] + 2, c0 + 1):
                    chunk_high(c)
                nc.scalar.preload_act_table_set("natural_log_exp_and_others")
                for t in range(NT):
                    layer_norm(0, t)
                    if t:
                        channels_out("x1", t - 1)
                channels_out("x1", NT - 1)
                chunk_high(c0 + 1)
                for m in range(MT):
                    for h in range(2):
                        act.wait_ge(*filled(f"mem{m}{h}"))
                        ps = bank(f"mem{m}{h}")
                        A(memT[0][:, 4 * h:4 * h + 4, m * P:(m + 1) * P], ps[:, :].rearrange("p (k t) -> p k t", k=4), ACT.Copy).then_inc(*raises("mem_high"))
                        act.wait_ge(*latest("mem_high"))
                act.wait_ge(S["ln_out_dve"].h, NT)
                act.wait_ge(S["ln_out_pool"].h, NT)
                rows(2, lnrow2)
                for i in range(KT):
                    copy_out(f"cq{i}", q2[:, i, :])
                    if i % 2:
                        chunk_high(c0 + 2 + i // 2)
                c0 = first["ca_wkv"]
                for i in range(KT):
                    copy_out(f"mk{i}", mK[:, i, :], N_MEM)
                    if i % 2:
                        chunk_high(c0 + 2 + i // 2)
                for h in range(2):
                    chunk_high(c0 + 6 + 2 * h)
                    for m in range(MT):
                        copy_out(f"mv{m}{h}", mV[:, m, h * 512:(h + 1) * 512])
                    chunk_high(c0 + 7 + 2 * h)
                for n in range(MEM_HEADS * NT + 1):
                    h, i = n // NT, n % NT
                    if n < MEM_HEADS * NT:
                        g = f"cs{h}{i}"
                        act.wait_ge(*filled(g))
                        ps = bank(g)
                        act.wait_ge(S["ca_max"].h, n + 1)
                        if n >= 2:
                            act.wait_ge(*filled(f"pT{(n - 2) // NT}{(n - 2) % NT}"))
                        A(p2[:, n % 2, :], ps[:, 0:N_MEM], ACT.Exp, bias=stat[:, n % 2, 9:10], scale=1.0 / 16,
                                  accum_out=stat[:, n % 2, 10:11]).then_inc(*empties(g))
                        act.wait_ge(*emptied(g))
                    if n:
                        hh, ii = (n - 1) // NT, (n - 1) % NT
                        g = f"pT{hh}{ii}"
                        act.wait_ge(*filled(g))
                        ps = bank(g)
                        if hh:
                            act.wait_ge(*filled(f"co{hh - 1}1"))
                        A(pT2[:, :, ii * P:(ii + 1) * P], ps[:, 0:2 * P].rearrange("p (a b) -> p a b", a=2), ACT.Copy).then_inc(*empties(g))
                        act.wait_ge(*emptied(g))
                        if ii == NT - 1:
                            for d in range(2):
                                act.wait_ge(*filled(f"co{hh}{d}"))
                                ps = bank(f"co{hh}{d}")
                                A(o2[0][:, 2 * hh + d, :], ps[:, :], ACT.Copy).then_inc(*raises("o2_high"))
                                act.wait_ge(*latest("o2_high"))
                c0 = first["ffn_up"]
                for c in range(first["ca_wo"] + 2, c0 + 1):
                    chunk_high(c)
                nc.scalar.preload_act_table_set("natural_log_exp_and_others")
                for t in range(NT):
                    layer_norm(1, t)
                    if t:
                        channels_out("x2", t - 1)
                channels_out("x2", NT - 1)
                chunk_high(c0 + 1)
                act.wait_ge(S["ffn_a"].h, 1)

                def gate_input(i):
                    act.wait_ge(*filled(f"fa{i}"))
                    ps = bank(f"fa{i}")
                    if i:
                        act.wait_ge(S["ffn_c"].h, i)
                    A(fa[:, 2:T + 2], ps[:, :], ACT.Copy).then_inc(*empties(f"fa{i}"))
                    act.wait_ge(*emptied(f"fa{i}"))

                def gate(i):
                    act.wait_ge(S["ffn_c"].h, i + 1)
                    A(fc[i % 2], fc[i % 2], ACT.Silu).then_inc(*raises("ffn_s"))
                    act.wait_ge(*latest("ffn_s"))

                def hidden_high(i):
                    act.wait_ge(*emptied(f"fg{i}"))
                    A(hid[0][:, i, :], fc[i % 2], ACT.Copy).then_inc(*raises("hid_high"))
                    act.wait_ge(*latest("hid_high"))

                for i in range(0, FT, 2):
                    gate_input(i)
                    gate(i)
                    gate_input(i + 1)
                    chunk_high(c0 + 2 + i)
                    gate(i + 1)
                    hidden_high(i)
                    hidden_high(i + 1)
                    chunk_high(c0 + 3 + i)
                for c in range(first["ffn_down"] + 2, len(chunks)):
                    chunk_high(c)
                nc.scalar.preload_act_table_set("natural_log_exp_and_others")
                for t in range(NT):
                    layer_norm(2, t)

            layers(act, "act", prologue, body)

        @block.vector
        def _(dve):
            V = nc.vector
            tt, ts, stt = V.tensor_tensor, V.tensor_scalar, V.scalar_tensor_tensor
            mult, add, sub = ALU.mult, ALU.add, ALU.subtract

            def reduce_angle(dst, src, n, last):
                ts(n, src, INV_2PI, ROUND, mult, add).then_inc(*raises("dve_step"))
                dve.wait_ge(*latest("dve_step"))
                ts(n, n, ROUND, None, sub).then_inc(*raises("dve_step"))
                dve.wait_ge(*latest("dve_step"))
                hi, mid, lo = two_pi_parts()
                stt(dst, n, -hi, src, mult, add).then_inc(*raises("dve_step"))
                dve.wait_ge(*latest("dve_step"))
                stt(dst, n, -mid, dst, mult, add).then_inc(*raises("dve_step"))
                dve.wait_ge(*latest("dve_step"))
                stt(dst, n, -lo, dst, mult, add).then_inc(*raises("dve_step"))
                dve.wait_ge(*latest("dve_step"))
                ts(dst, dst, PI_SAFE, -PI_SAFE, ALU.min, ALU.max).then_inc(*raises(last))
                dve.wait_ge(*latest(last))

            def chunk_low(c):
                dve.wait_ge(S["chunk_high"].h, c + 1)
                tt(slot(split[1], c), slot(raw, c), as32(slot(split[0], c)), sub).then_inc(*raises("chunk_low_dve"))
                dve.wait_ge(*latest("chunk_low_dve"))

            def channels_low(tag, t, turn):
                for h in range(2):
                    g = f"{tag}{t}{h}"
                    dve.wait_ge(S["x_high"].h, 2 * (NT * turn + t) + h + 1)
                    ps = bank(g)
                    at = (slice(None), slice(4 * h, 4 * h + 4), slice(t * P, (t + 1) * P))
                    tt(xT[1][at], ps[:, :].rearrange("p (k t) -> p k t", k=4), as32(xT[0][at]), sub).then_inc(*empties(g))
                    dve.wait_ge(*emptied(g))

            def prologue():
                dve.wait_ge(S["small_loaded"].h, 16 * 4)
                V.tensor_copy(posf, posr.bitcast(i32)).then_inc(*raises("dve_step"))
                dve.wait_ge(*latest("dve_step"))
                ts(ang, posf, K[:, C_FREQ:C_FREQ + 1], None, mult).then_inc(*raises("dve_step"))
                dve.wait_ge(*latest("dve_step"))
                reduce_angle(tr, ang, tn, "s5_col_v")

            def body(l):
                dve.wait_ge(S["small_loaded"].h, small["layer"])
                V.tensor_copy(sheet[0:8, 2, :].rearrange("p (a b) -> p a b", a=2), lamr[0:8, 5, 0:2].unsqueeze(2).to_broadcast([8, 2, 64])).then_inc(*raises("sheets"))
                dve.wait_ge(*latest("sheets"))
                for i in range(2):
                    tt(lamr[0:1, 2 * i, :], lamr[0:1, 2 * i, :], lamr[0:1, 2 * i + 1, :], mult).then_inc(*raises("dve_step"))
                    dve.wait_ge(*latest("dve_step"))
                    V.reduce_sum(lamr[0:1, 4, 6 + i:7 + i], lamr[0:1, 2 * i, :], AX.X).then_inc(*raises("lam_in" if i else "dve_step"))
                    dve.wait_ge(*latest("lam_in" if i else "dve_step"))
                for t in range(NT):
                    channels_low("x0", t, 0)
                dve.wait_ge(S["lam_exp"].h, 1)
                tt(lamr[0:1, 4, 0:1], lamr[0:1, 4, 5:6], lamr[0:1, 4, 4:5], sub).then_inc(*raises("dve_step"))
                dve.wait_ge(*latest("dve_step"))
                tt(lamr[0:1, 4, 0:1], lamr[0:1, 4, 0:1], lamr[0:1, 4, 2:3], sub).then_inc(*raises("dve_step"))
                dve.wait_ge(*latest("dve_step"))
                V.tensor_copy(lamr[0:1, 4, 1:2], lamr[0:1, 4, 3:4]).then_inc(*raises("lam_row"))
                dve.wait_ge(*latest("lam_row"))
                dve.wait_ge(*filled("sheet0"))
                ps = bank("sheet0")
                V.tensor_copy(col1[:, :], ps[:, 0:S1_N]).then_inc(*empties("sheet0"))
                dve.wait_ge(*emptied("sheet0"))
                dve.wait_ge(*filled("sheet1"))
                ps = bank("sheet1")
                V.tensor_copy(col2[:, :], ps[:, 0:S2_N]).then_inc(*empties("sheet1"))
                dve.wait_ge(*emptied("sheet1"))
                dve.wait_ge(*filled("sheet2"))
                ps = bank("sheet2")
                V.tensor_copy(col3[:, :], ps[:, 0:24]).then_inc(*empties("sheet2"))
                dve.wait_ge(*emptied("sheet2"))
                dve.wait_ge(*filled("lam"))
                ps = bank("lam")
                V.tensor_copy(lamc[:, 0:2], ps[:, 0:2]).then_inc(*empties("lam"))
                dve.wait_ge(*emptied("lam"))
                g0 = S2["da_subln_g"][0]
                tt(lamc[:, 2:3], col2[:, g0:g0 + 1], lamc[:, 1:2], mult).then_inc(*raises("dve_step"))
                dve.wait_ge(*latest("dve_step"))
                s = [s5c[:, i, :] for i in range(24)]
                are, aim = col3[:, 8:16], col3[:, 16:24]
                V.memset(stat[:, 0, 38:39], 0.0).then_inc(*raises("s5_col_v"))
                dve.wait_ge(*latest("s5_col_v"))
                dve.wait_ge(S["s5_col_a"].h, 1)
                tt(s[1], s[0], are, mult).then_inc(*raises("dve_step"))
                dve.wait_ge(*latest("dve_step"))
                tt(s[2], s[0], aim, mult).then_inc(*raises("dve_step"))
                dve.wait_ge(*latest("dve_step"))
                reduce_angle(s[5], s[2], s[4], "s5_col_v")
                ts(s[6], s[5], INV_2PI, None, mult).then_inc(*raises("dve_step"))
                dve.wait_ge(*latest("dve_step"))
                ts(s[7], s[6], ROUND13, ROUND13, add, sub).then_inc(*raises("dve_step"))
                dve.wait_ge(*latest("dve_step"))
                tt(s[6], s[6], s[7], sub).then_inc(*raises("dve_step"))
                dve.wait_ge(*latest("dve_step"))
                dve.wait_ge(S["s5_col_a"].h, 3)
                rho, sn, cs = s[3], s[8], s[9]
                tt(s[10], rho, cs, mult).then_inc(*raises("dve_step"))
                dve.wait_ge(*latest("dve_step"))
                ts(s[10], s[10], -1.0, None, add).then_inc(*raises("dve_step"))
                dve.wait_ge(*latest("dve_step"))
                tt(s[11], rho, sn, mult).then_inc(*raises("dve_step"))
                dve.wait_ge(*latest("dve_step"))
                tt(s[12], are, are, mult).then_inc(*raises("dve_step"))
                dve.wait_ge(*latest("dve_step"))
                tt(s[13], aim, aim, mult).then_inc(*raises("dve_step"))
                dve.wait_ge(*latest("dve_step"))
                tt(s[12], s[12], s[13], add).then_inc(*raises("dve_step"))
                dve.wait_ge(*latest("dve_step"))
                V.reciprocal(s[12], s[12]).then_inc(*raises("dve_step"))
                dve.wait_ge(*latest("dve_step"))
                tt(s[13], s[10], are, mult).then_inc(*raises("dve_step"))
                dve.wait_ge(*latest("dve_step"))
                tt(s[14], s[11], aim, mult).then_inc(*raises("dve_step"))
                dve.wait_ge(*latest("dve_step"))
                tt(s[13], s[13], s[14], add).then_inc(*raises("dve_step"))
                dve.wait_ge(*latest("dve_step"))
                tt(s[13], s[13], s[12], mult).then_inc(*raises("dve_step"))
                dve.wait_ge(*latest("dve_step"))
                tt(s[14], s[11], are, mult).then_inc(*raises("dve_step"))
                dve.wait_ge(*latest("dve_step"))
                tt(s[15], s[10], aim, mult).then_inc(*raises("dve_step"))
                dve.wait_ge(*latest("dve_step"))
                tt(s[14], s[14], s[15], sub).then_inc(*raises("dve_step"))
                dve.wait_ge(*latest("dve_step"))
                tt(s[14], s[14], s[12], mult).then_inc(*raises("dve_step"))
                dve.wait_ge(*latest("dve_step"))
                dve.wait_ge(*emptied("cT"))
                V.memset(PR[:, :, 0:2], 0.0).then_inc(*raises("dve_step"))
                dve.wait_ge(*latest("dve_step"))

                def token_shift(i):
                    dve.wait_ge(*emptied(f"rw{i}"))
                    tt(shifted, PR[:, i, 1:T + 1], PR[:, i, 2:T + 2], sub).then_inc(*raises("dve_step"))
                    dve.wait_ge(*latest("dve_step"))
                    stt(PR[:, i, 2:T + 2], shifted, col2[:, i:i + 1], PR[:, i, 2:T + 2], mult, add).then_inc(*raises("shift_done"))
                    dve.wait_ge(*latest("shift_done"))

                def rotary(i):
                    straight = (qT if i < 4 else kT)[:, i % 4, :]
                    dve.wait_ge(*filled(f"rot{i}"))
                    ps = bank(f"rot{i}")
                    tt(rope_a, ps[:, :], ropeS[:, :], mult).then_inc(*empties(f"rot{i}"))
                    dve.wait_ge(*emptied(f"rot{i}"))
                    tt(straight, straight, ropeC[:, :], mult).then_inc(*raises("dve_step"))
                    dve.wait_ge(*latest("dve_step"))
                    tt(straight, straight, rope_a, add).then_inc(*raises("rope_done"))
                    dve.wait_ge(*latest("rope_done"))

                iota = K[:, C_IOTA:C_IOTA + T]

                def s5_mask(j):
                    return K[:, C_S5M + j % 4 * P:C_S5M + (j % 4 + 1) * P]

                def s5_turns(j):
                    q, m = s_turn, s_round
                    ts(q, iota, s5c[:, 7, j:j + 1], None, mult).then_inc(*raises("dve_step"))
                    dve.wait_ge(*latest("dve_step"))
                    ts(m, q, ROUND, ROUND, add, sub).then_inc(*raises("dve_step"))
                    dve.wait_ge(*latest("dve_step"))
                    tt(q, q, m, sub).then_inc(*raises("dve_step"))
                    dve.wait_ge(*latest("dve_step"))
                    stt(q, iota, s5c[:, 6, j:j + 1], q, mult, add).then_inc(*raises("dve_step"))
                    dve.wait_ge(*latest("dve_step"))
                    ts(m, q, ROUND, ROUND, add, sub).then_inc(*raises("dve_step"))
                    dve.wait_ge(*latest("dve_step"))
                    tt(q, q, m, sub).then_inc(*raises("s5_tables"))
                    dve.wait_ge(*latest("s5_tables"))

                def s5_padded_b(j):
                    gr, gi = s5c[:, 13, j:j + 1], s5c[:, 14, j:j + 1]
                    br, bi = bn[:, 0, j, :], bn[:, 1, j, :]
                    ts(b_parts[:, 0, :], bi, gi, None, mult).then_inc(*raises("dve_step"))
                    dve.wait_ge(*latest("dve_step"))
                    ts(b_parts[:, 1, :], bi, gr, None, mult).then_inc(*raises("dve_step"))
                    dve.wait_ge(*latest("dve_step"))
                    stt(b_parts[:, 2, :], br, gr, b_parts[:, 0, :], mult, sub).then_inc(*raises("dve_step"))
                    dve.wait_ge(*latest("dve_step"))
                    stt(b_parts[:, 3, :], br, gi, b_parts[:, 1, :], mult, add).then_inc(*raises("dve_step"))
                    dve.wait_ge(*latest("dve_step"))
                    if j:
                        dve.wait_ge(*filled(f"bT{j - 1}"))
                    for i in range(2):
                        tt(bpad[:, i, :].rearrange("p (g h) -> p g h", h=16), b_parts[:, 2 + i, :].unsqueeze(1).to_broadcast([P, 8, 16]),
                                s5_mask(j).rearrange("p (g h) -> p g h", h=16), mult).then_inc(*raises("s5_b" if i else "dve_step"))
                        dve.wait_ge(*latest("s5_b" if i else "dve_step"))

                def s5_skip(ct):
                    dve.wait_ge(*filled(f"y{ct}"))
                    ps = bank(f"y{ct}")
                    stt(yT[:, ct, :], uT[:, ct, :], col2[:, S2["s5_d"][0] + ct:S2["s5_d"][0] + ct + 1], ps[:, :], mult, add).then_inc(*empties(f"y{ct}"))
                    dve.wait_ge(*emptied(f"y{ct}"))

                s5_turns(0)
                s5_padded_b(0)
                for j in range(S5_TILES):
                    ct = j // 4
                    cos, sin = s_cos[j % 2], s_sin[j % 2]
                    dve.wait_ge(S["s5_col_a"].h, 4 + j)
                    dve.wait_ge(*filled(f"bu{j}0"))
                    pr = bank(f"bu{j}0")
                    dve.wait_ge(*filled(f"bu{j}1"))
                    pi = bank(f"bu{j}1")
                    tt(s_m[0], pr[:, :], cos, mult).then_inc(*raises("dve_step"))
                    dve.wait_ge(*latest("dve_step"))
                    tt(s_m[1], pi[:, :], sin, mult).then_inc(*raises("dve_step"))
                    dve.wait_ge(*latest("dve_step"))
                    tt(s_m[2], pi[:, :], cos, mult).then_inc(*empties(f"bu{j}1"))
                    dve.wait_ge(*emptied(f"bu{j}1"))
                    tt(s_m[3], pr[:, :], sin, mult).then_inc(*empties(f"bu{j}0"))
                    dve.wait_ge(*emptied(f"bu{j}0"))
                    if j + 1 < S5_TILES:
                        s5_turns(j + 1)
                        s5_padded_b(j + 1)
                    for i in range(2 * j, min(2 * j + 2, RW_TILES)):
                        token_shift(i)
                    if j >= 4:
                        rotary(2 * j - 8)
                        if j < 7:
                            rotary(2 * j - 7)
                    dve.wait_ge(S["s5_w"].h, 2 * j + 2)
                    for i in range(2):
                        V.tensor_tensor_scan(s_z[i], s5c[:, 3, j:j + 1].to_broadcast([P, T]), s_m[2 * i], 0.0, mult, add).then_inc(*raises("dve_step"))
                        dve.wait_ge(*latest("dve_step"))
                    if j:
                        if j % 4 == 0:
                            dve.wait_ge(*filled(f"y{ct - 1}"))
                        else:
                            dve.wait_ge(S["s5_y"].h, j - ct)
                    tt(s_n[0], s_z[0], cos, mult).then_inc(*raises("s5_n"))
                    dve.wait_ge(*latest("s5_n"))
                    tt(s_n[1], s_z[1], sin, mult).then_inc(*raises("s5_n"))
                    dve.wait_ge(*latest("s5_n"))
                    tt(s_n[2], s_z[0], sin, mult).then_inc(*raises("s5_n"))
                    dve.wait_ge(*latest("s5_n"))
                    tt(s_n[3], s_z[1], cos, mult).then_inc(*raises("s5_n"))
                    dve.wait_ge(*latest("s5_n"))
                    for i in range(2):
                        tt(cpad[:, i, :], cT[:, 2 * i + ct, :], s5_mask(j), mult).then_inc(*raises("s5_c" if i else "dve_step"))
                        dve.wait_ge(*latest("s5_c" if i else "dve_step"))
                    if j == 4:
                        s5_skip(0)
                rotary(7)
                s5_skip(1)
                dve.wait_ge(*filled("glu1"))
                for n in range(2):
                    dve.wait_ge(*emptied(f"glu{n}"))
                    tt(zT[:, n, :], zT[:, n, :], s_r[:, n, :], mult).then_inc(*raises("s5_g"))
                    dve.wait_ge(*latest("s5_g"))
                dve.wait_ge(*emptied("s5ss"))
                for ct in range(2):
                    g0 = S2["s5_out_g"][0] + ct
                    stt(zT[:, ct, :], zT[:, ct, :], col2[:, g0:g0 + 1], yT[:, 1, :], mult, mult).then_inc(*raises("s5_raw"))
                    dve.wait_ge(*latest("s5_raw"))
                def head_out(h):
                    dve.wait_ge(S["attn_rs"].h, h + 1)
                    stt(oh, oh, lamc[:, 2:3], orr, mult, mult).then_inc(*raises("da_raw"))
                    dve.wait_ge(*latest("da_raw"))

                for n in range(DA_HEADS * NT):
                    h, i = n // NT, n % NT
                    st = stat[:, n % 2, :]
                    w = (i + 1) * P
                    for b in range(2):
                        dve.wait_ge(*filled(f"sc{h}{i}{b}"))
                        ps = bank(f"sc{h}{i}{b}")
                        V.reduce_max(st[:, 8 + b:9 + b], ps[:, 0:w], AX.X).then_inc(*raises("dve_step"))
                        dve.wait_ge(*latest("dve_step"))
                        ts(st[:, 4 + b:5 + b], st[:, 8 + b:9 + b], -0.125, None, mult).then_inc(*raises("attn_max"))
                        dve.wait_ge(*latest("attn_max"))
                    dve.wait_ge(*emptied(f"sc{h}{i}0"))
                    dve.wait_ge(*emptied(f"sc{h}{i}1"))
                    V.reciprocal(st[:, 6:8], st[:, 6:8]).then_inc(*raises("dve_step"))
                    dve.wait_ge(*latest("dve_step"))
                    tt(st[:, 7:8], st[:, 7:8], lamc[:, 0:1], mult).then_inc(*raises("dve_step"))
                    dve.wait_ge(*latest("dve_step"))
                    p0, p1 = AP_[:, 2 * (n % 2), 0:w], AP_[:, 2 * (n % 2) + 1, 0:w]
                    ts(p1, p1, st[:, 7:8], None, mult).then_inc(*raises("dve_step"))
                    dve.wait_ge(*latest("dve_step"))
                    stt(p0, p0, st[:, 6:7], p1, mult, add).then_inc(*raises("attn_p"))
                    dve.wait_ge(*latest("attn_p"))
                    if n % NT == 2 and h:
                        head_out(h - 1)
                head_out(DA_HEADS - 1)
                for j in range(2):
                    def c2(name):
                        return col2[:, S2[name][0] + j:S2[name][0] + j + 1]

                    if j == 0:
                        dve.wait_ge(S["lr_ready"].h, 3)
                        dve.wait_ge(S["hT_da"].h, DA_HEADS)
                    r_, k_, v_ = PR[:, j, 2:], PR[:, 2 + j, 2:], PR[:, 4 + j, 2:]
                    t0, t1 = rw["t0"], rw["t1"]
                    ts(rw["kk"], k_, c2("rw_k_k"), None, mult).then_inc(*raises("rw_kk"))
                    dve.wait_ge(*latest("rw_kk"))
                    dve.wait_ge(*filled(f"kss{j}"))
                    ps = bank(f"kss{j}")
                    ts(t1, ps[:, :], 1e-24, None, ALU.max).then_inc(*empties(f"kss{j}"))
                    dve.wait_ge(*emptied(f"kss{j}"))
                    dve.wait_ge(*emptied(f"lrw{j}"))
                    V.memset(rP[:, :, 0:1], 1.0).then_inc(*raises("dve_step"))
                    dve.wait_ge(*latest("dve_step"))
                    zero = const("zero").to_broadcast([P, CH])
                    for c in range(NCH):
                        V.tensor_tensor_scan(rP[:, c, 1:], t0[:, c * CH:(c + 1) * CH], zero, 1.0, mult, add).then_inc(*raises("dve_step"))
                        dve.wait_ge(*latest("dve_step"))
                    ip3 = rw["iP"].rearrange("p (c t) -> p c t", c=NCH)
                    V.reciprocal(ip3, rP[:, :, 1:]).then_inc(*raises("dve_step"))
                    dve.wait_ge(*latest("dve_step"))
                    dve.wait_ge(*emptied(f"lra{j}"))
                    ts(t0, rw["a"], -1.0, c2("rw_k_a"), add, mult).then_inc(*raises("dve_step"))
                    dve.wait_ge(*latest("dve_step"))
                    stt(rw["kmod"], t0, 1.0, k_, add, mult).then_inc(*raises("dve_step"))
                    dve.wait_ge(*latest("dve_step"))
                    tt(t0, r_, rw["kmod"], mult).then_inc(*raises("dve_step"))
                    dve.wait_ge(*latest("dve_step"))
                    ts(rw["bonus"], t0, c2("rw_r_k"), None, mult).then_inc(*raises("rw_bonus"))
                    dve.wait_ge(*latest("rw_bonus"))
                    dve.wait_ge(S["rw_sq"].h, 2 * j + 2)
                    V.reciprocal(t1, t1).then_inc(*raises("dve_step"))
                    dve.wait_ge(*latest("dve_step"))
                    tt(rw["kk"], rw["kk"], t1, mult).then_inc(*raises("dve_step"))
                    dve.wait_ge(*latest("dve_step"))

                    def c3(a):
                        return a.rearrange("p (c t) -> p c t", c=NCH)

                    pend = rP[:, :, CH:CH + 1].to_broadcast([P, NCH, CH])
                    stt(c3(rw["A"]), c3(rw["kk"]), -1.0, rP[:, :, 0:CH], mult, mult).then_inc(*raises("dve_step"))
                    dve.wait_ge(*latest("dve_step"))
                    tt(t0, rw["kk"], rw["a"], mult).then_inc(*raises("dve_step"))
                    dve.wait_ge(*latest("dve_step"))
                    tt(rw["B"], t0, rw["iP"], mult).then_inc(*raises("dve_step"))
                    dve.wait_ge(*latest("dve_step"))
                    tt(c3(rw["Bh"]), c3(rw["B"]), pend, mult).then_inc(*raises("dve_step"))
                    dve.wait_ge(*latest("dve_step"))
                    tt(rw["K"], rw["kmod"], rw["iP"], mult).then_inc(*raises("dve_step"))
                    dve.wait_ge(*latest("dve_step"))
                    tt(c3(rw["Kh"]), c3(rw["K"]), pend, mult).then_inc(*raises("dve_step"))
                    dve.wait_ge(*latest("dve_step"))
                    tt(c3(rw["R"]), c3(r_), rP[:, :, 1:], mult).then_inc(*raises("rw_gram_in"))
                    dve.wait_ge(*latest("rw_gram_in"))
                    dve.wait_ge(*filled(f"bon{j}"))
                    ps = bank(f"bon{j}")
                    tt(rw["bonus"], ps[:, :], v_, mult).then_inc(*empties(f"bon{j}"))
                    dve.wait_ge(*emptied(f"bon{j}"))
                    dve.wait_ge(S["hT_da"].h, DA_HEADS)

                    def q3(a):
                        return a.rearrange("p (i t) -> p i t", t=P)

                    def m3(c):
                        return K[:, c:c + P].unsqueeze(1).to_broadcast([P, NT, P])

                    for hh in range(2):
                        g = f"grABT{j}{hh}"
                        dve.wait_ge(*filled(g))
                        ps = bank(g)
                        tt(q3(mAB[:, hh, :]), q3(ps[:, :]), m3(C_SU), mult).then_inc(*raises("dve_step"))
                        dve.wait_ge(*latest("dve_step"))
                        tt(q3(TiT[:, hh, :]), q3(ps[:, :]), m3(C_L1U), mult).then_inc(*empties(g))
                        dve.wait_ge(*emptied(g))
                        tt(q3(TiT[:, hh, :]), q3(TiT[:, hh, :]), m3(C_ID), add).then_inc(*raises("rw_T"))
                        dve.wait_ge(*latest("rw_T"))
                        g = f"grAB{j}{hh}"
                        dve.wait_ge(*filled(g))
                        ps = bank(g)
                        tt(q3(Ti[:, hh, :]), q3(ps[:, :]), m3(C_L1L), mult).then_inc(*empties(g))
                        dve.wait_ge(*emptied(g))
                        tt(q3(Ti[:, hh, :]), q3(Ti[:, hh, :]), m3(C_ID), add).then_inc(*raises("rw_T"))
                        dve.wait_ge(*latest("rw_T"))
                        for nm, dst, mask in (("RBT", mRB, C_IU), ("RKT", mRK, C_IU), ("AKT", mAK, C_SU)):
                            g = f"gr{nm}{j}{hh}"
                            dve.wait_ge(*filled(g))
                            ps = bank(g)
                            tt(q3(dst[:, hh, :]), q3(ps[:, :]), m3(mask), mult).then_inc(*empties(g))
                            dve.wait_ge(*emptied(g))
                    dve.wait_ge(S["levels_loaded"].h, 16)
                    for lv in range(len(LEVELS)):
                        for hh in range(2):
                            dve.wait_ge(*filled(f"dT{j}{lv}{hh}"))
                            pa = bank(f"dT{j}{lv}{hh}")
                            dve.wait_ge(*filled(f"dTT{j}{lv}{hh}"))
                            pb = bank(f"dTT{j}{lv}{hh}")
                            for i, (g, dst, ps) in enumerate(((f"dT{j}{lv}{hh}", Ti, pa), (f"dTT{j}{lv}{hh}", TiT, pb))):
                                V.copy_predicated(q3(dst[:, hh, :]), lev[:, lv, i, :].bitcast(u32).unsqueeze(1).to_broadcast([P, NT, P]), q3(ps[:, :])).then_inc(*empties(g))
                                dve.wait_ge(*emptied(g))
                    dve.wait_ge(*filled(f"Q{j}"))
                    ps = bank(f"Q{j}")
                    tt(rQ, ps[:, :], rw["R"], add).then_inc(*empties(f"Q{j}"))
                    dve.wait_ge(*emptied(f"Q{j}"))
                    tt(t0.rearrange("p (c k) -> p c k", c=NCH), K[:, C_EYE:C_EYE + CH].unsqueeze(1).to_broadcast([P, NCH, CH]), pend, mult).then_inc(*raises("dve_step"))
                    dve.wait_ge(*latest("dve_step"))
                    for par in range(2):
                        dve.wait_ge(*filled(f"GH{j}{par}"))
                        ps = bank(f"GH{j}{par}")

                        def par3(a):
                            return a.rearrange("p (i q k) -> p i q k", q=2, k=CH)[:, :, par, :]

                        tt(par3(rG), ps[:, 0:256].rearrange("p (i k) -> p i k", k=CH), par3(t0), add).then_inc(*raises("dve_step"))
                        dve.wait_ge(*latest("dve_step"))
                        V.tensor_copy(par3(rH), ps[:, 256:512].rearrange("p (i k) -> p i k", k=CH)).then_inc(*empties(f"GH{j}{par}"))
                        dve.wait_ge(*emptied(f"GH{j}{par}"))
                    V.tensor_copy(rS[:, CH:2 * CH], rH[:, 0:CH]).then_inc(*raises("rw_state"))
                    dve.wait_ge(*latest("rw_state"))
                    for c in range(1, NCH - 1):
                        for hh in range(2):
                            r = slice(64 * hh, 64 * hh + 64)
                            g = f"S{j}{c}{hh}"
                            dve.wait_ge(*filled(g))
                            ps = bank(g)
                            tt(rS[r, (c + 1) * CH:(c + 2) * CH], ps[r, 0:CH], rH[r, c * CH:(c + 1) * CH], add).then_inc(*empties(g))
                            dve.wait_ge(*emptied(g))
                    dve.wait_ge(*filled(f"ym{j}"))
                    ps = bank(f"ym{j}")
                    stt(rY, ps[:, :], -1.0 / CH, rY, mult, add).then_inc(*empties(f"ym{j}"))
                    dve.wait_ge(*emptied(f"ym{j}"))
                    dve.wait_ge(*emptied(f"yv{j}"))
                    tt(rY, rY, t1, mult).then_inc(*raises("dve_step"))
                    dve.wait_ge(*latest("dve_step"))
                    ts(rY, rY, c2("rw_lnx_g"), c2("rw_lnx_b"), mult, add).then_inc(*raises("dve_step"))
                    dve.wait_ge(*latest("dve_step"))
                    tt(rY, rY, rw["bonus"], add).then_inc(*raises("dve_step"))
                    dve.wait_ge(*latest("dve_step"))
                    tt(rY, rY, rw["g"], mult).then_inc(*raises("rw_raw"))
                    dve.wait_ge(*latest("rw_raw"))

                def add_half(tag, t, h):
                    dve.wait_ge(*filled(f"{tag}{t}{h}"))
                    ps = bank(f"{tag}{t}{h}")
                    xx = x[:, t, h * 512:(h + 1) * 512]
                    stt(xx, xx, ALPHA, ps[:, :], mult, add).then_inc(*empties(f"{tag}{t}{h}"))
                    dve.wait_ge(*emptied(f"{tag}{t}{h}"))
                    V.bn_stats(stat[:, t, 12 + 6 * h:18 + 6 * h], xx).then_inc(*raises("dve_step"))
                    dve.wait_ge(*latest("dve_step"))

                def layer_norm(n, t, tag, gain):
                    st = stat[:, t, :]
                    add_half(tag, t, 1)
                    V.bn_aggr(st[:, 0:2], st[:, 12:24]).then_inc(*raises("ln_var"))
                    dve.wait_ge(*latest("ln_var"))
                    dve.wait_ge(S["ln_rstd"].h, NT * n + t + 1)
                    ts(x[:, t, :], x[:, t, :], st[:, 0:1], st[:, 1:2], sub, mult).then_inc(*raises("ln_hat"))
                    dve.wait_ge(*latest("ln_hat"))
                    if t == 0:
                        dve.wait_ge(S["rows_loaded"].h, 32 * (n + 1))
                    half = slice(0, 512)
                    tt(x[:, t, half], x[:, t, half], gain[:, 0, half], mult).then_inc(*raises("dve_step"))
                    dve.wait_ge(*latest("dve_step"))
                    tt(x[:, t, half], x[:, t, half], gain[:, 1, half], add).then_inc(*raises("ln_out_dve"))
                    dve.wait_ge(*latest("ln_out_dve"))

                for t in range(NT):
                    add_half("wo", t, 0)
                for t in range(NT):
                    layer_norm(0, t, "wo", lnrow1)
                    if t:
                        channels_low("x1", t - 1, 1)
                channels_low("x1", NT - 1, 1)
                for m in range(MT):
                    for h in range(2):
                        dve.wait_ge(S["mem_high"].h, 2 * m + h + 1)
                        ps = bank(f"mem{m}{h}")
                        at = (slice(None), slice(4 * h, 4 * h + 4), slice(m * P, (m + 1) * P))
                        tt(memT[1][at], ps[:, :].rearrange("p (k t) -> p k t", k=4), as32(memT[0][at]), sub).then_inc(*empties(f"mem{m}{h}"))
                        dve.wait_ge(*emptied(f"mem{m}{h}"))
                for c in range(first["ca_wkv"], first["ca_wo"]):
                    chunk_low(c)

                def cross_out(h):
                    for d in range(2):
                        dve.wait_ge(S["o2_high"].h, 2 * h + d + 1)
                        ps = bank(f"co{h}{d}")
                        tt(o2[1][:, 2 * h + d, :], ps[:, :], as32(o2[0][:, 2 * h + d, :]), sub).then_inc(*empties(f"co{h}{d}"))
                        dve.wait_ge(*emptied(f"co{h}{d}"))

                for n in range(MEM_HEADS * NT):
                    h, i = n // NT, n % NT
                    st = stat[:, n % 2, :]
                    dve.wait_ge(*filled(f"cs{h}{i}"))
                    ps = bank(f"cs{h}{i}")
                    V.reduce_max(st[:, 8:9], ps[:, 0:N_MEM], AX.X).then_inc(*raises("dve_step"))
                    dve.wait_ge(*latest("dve_step"))
                    ts(st[:, 9:10], st[:, 8:9], -1.0 / 16, None, mult).then_inc(*raises("ca_max"))
                    dve.wait_ge(*latest("ca_max"))
                    dve.wait_ge(*emptied(f"cs{h}{i}"))
                    V.reciprocal(st[:, 10:11], st[:, 10:11]).then_inc(*raises("dve_step"))
                    dve.wait_ge(*latest("dve_step"))
                    ts(p2[:, n % 2, :], p2[:, n % 2, :], st[:, 10:11], None, mult).then_inc(*raises("ca_p"))
                    dve.wait_ge(*latest("ca_p"))
                    if i == 2 and h:
                        cross_out(h - 1)
                cross_out(MEM_HEADS - 1)
                for t in range(NT):
                    add_half("cw", t, 0)
                for t in range(NT):
                    layer_norm(1, t, "cw", lnrow2)
                    if t:
                        channels_low("x2", t - 1, 2)
                channels_low("x2", NT - 1, 2)
                V.memset(fa[:, 0:2], 0.0).then_inc(*raises("ffn_a"))
                dve.wait_ge(*latest("ffn_a"))

                def convolution(i):
                    def w(k):
                        return col1[:, k * FT + i:k * FT + i + 1]

                    c = fc[i % 2]
                    if i >= 2:
                        dve.wait_ge(S["hid_low"].h, i - 1)
                    dve.wait_ge(*emptied(f"fa{i}"))
                    ts(c, fa[:, 2:T + 2], w(2), col1[:, 3 * FT + i:3 * FT + i + 1], mult, add).then_inc(*raises("dve_step"))
                    dve.wait_ge(*latest("dve_step"))
                    stt(c, fa[:, 1:T + 1], w(1), c, mult, add).then_inc(*raises("dve_step"))
                    dve.wait_ge(*latest("dve_step"))
                    stt(c, fa[:, 0:T], w(0), c, mult, add).then_inc(*raises("ffn_c"))
                    dve.wait_ge(*latest("ffn_c"))

                def gated(i):
                    dve.wait_ge(*filled(f"fg{i}"))
                    ps = bank(f"fg{i}")
                    dve.wait_ge(S["ffn_s"].h, i + 1)
                    tt(fc[i % 2], ps[:, :], fc[i % 2], mult).then_inc(*empties(f"fg{i}"))
                    dve.wait_ge(*emptied(f"fg{i}"))

                c0 = first["ffn_up"]
                for i in range(0, FT, 2):
                    convolution(i)
                    convolution(i + 1)
                    chunk_low(c0 + 2 + i)
                    gated(i)
                    gated(i + 1)
                    chunk_low(c0 + 3 + i)
                c0 = first["ffn_down"]
                for c in range(c0 + 2, c0 + 8):
                    chunk_low(c)
                for t in range(NT):
                    add_half("dn", t, 0)
                for c in range(c0 + 8, len(chunks)):
                    chunk_low(c)
                for t in range(NT):
                    layer_norm(2, t, "dn", lnrow3)

            layers(dve, "dve", prologue, body)

        @block.gpsimd
        def _(pool):
            G = nc.gpsimd

            def chunk_low(c):
                pool.wait_ge(S["chunk_high"].h, c + 1)
                G.tensor_tensor(slot(split[1], c), slot(raw, c), as32(slot(split[0], c)), ALU.subtract).then_inc(*raises("chunk_low_pool"))
                pool.wait_ge(*latest("chunk_low_pool"))

            def part_low(name, src, k):
                hT_parts.append(k)
                pool.wait_ge(S["hT_high"].h, len(hT_parts))
                G.tensor_tensor(hT[1][:, k, :], src, as32(hT[0][:, k, :]), ALU.subtract).then_inc(*raises(name))
                pool.wait_ge(*latest(name))

            def prologue():
                pass

            hT_parts = []

            def body(l):
                hT_parts.clear()
                for c in range(3):
                    chunk_low(c)
                lows = {0: [3], 1: [4], 2: [5], 3: [6], 4: [7], 5: [8], 6: [9], 7: [10]}
                for j in range(S5_TILES):
                    pool.wait_ge(*emptied(f"bu{j}1"))
                    pool.wait_ge(*emptied(f"bu{j}0"))
                    G.tensor_tensor(s_m[0], s_m[0], s_m[1], ALU.add).then_inc(*raises("s5_w"))
                    pool.wait_ge(*latest("s5_w"))
                    G.tensor_tensor(s_m[2], s_m[2], s_m[3], ALU.subtract).then_inc(*raises("s5_w"))
                    pool.wait_ge(*latest("s5_w"))
                    for c in lows[j]:
                        chunk_low(c)
                    pool.wait_ge(S["s5_n"].h, 4 * j + 4)
                    G.tensor_tensor(s_n[0], s_n[0], s_n[1], ALU.subtract).then_inc(*raises("s5_x"))
                    pool.wait_ge(*latest("s5_x"))
                    G.tensor_tensor(s_n[2], s_n[2], s_n[3], ALU.add).then_inc(*raises("s5_x"))
                    pool.wait_ge(*latest("s5_x"))
                for ct in range(2):
                    part_low("hT_s5", zT[:, ct, :], 6 + ct)
                for c in range(first["w_out"], first["w_out"] + 2):
                    chunk_low(c)
                for h in range(DA_HEADS):
                    part_low("hT_da", oh, h)
                for j in range(2):
                    part_low("hT_rw", rY, 4 + j)

                def layer_norm(n, gain):
                    pool.wait_ge(S["rows_loaded"].h, 32 * (n + 1))
                    half = slice(512, D)
                    for t in range(NT):
                        pool.wait_ge(S["ln_hat"].h, NT * n + t + 1)
                        G.tensor_tensor(x[:, t, half], x[:, t, half], gain[:, 0, half], ALU.mult).then_inc(*raises("pool_step"))
                        pool.wait_ge(*latest("pool_step"))
                        G.tensor_tensor(x[:, t, half], x[:, t, half], gain[:, 1, half], ALU.add).then_inc(*raises("ln_out_pool"))
                        pool.wait_ge(*latest("ln_out_pool"))

                for c in range(first["w_out"] + 2, first["ca_wq"] + 1):
                    chunk_low(c)
                layer_norm(0, lnrow1)
                for c in range(first["ca_wq"] + 1, first["ca_wkv"]):
                    chunk_low(c)
                for c in range(first["ca_wo"], first["ffn_up"] + 1):
                    chunk_low(c)
                layer_norm(1, lnrow2)
                chunk_low(first["ffn_up"] + 1)
                for i in range(FT):
                    pool.wait_ge(S["hid_high"].h, i + 1)
                    G.tensor_tensor(hid[1][:, i, :], fc[i % 2], as32(hid[0][:, i, :]), ALU.subtract).then_inc(*raises("hid_low"))
                    pool.wait_ge(*latest("hid_low"))
                layer_norm(2, lnrow3)

            layers(pool, "pool", prologue, body)


_NAMES = ["x", "mem", "positions", "w_in", "da_lam_q1", "da_lam_k1", "da_lam_q2", "da_lam_k2", "da_subln_g",
          "rw_mu", "rw_w0", "rw_w2", "rw_a0", "rw_a2", "rw_g2", "rw_k_k", "rw_k_a", "rw_r_k", "rw_lnx_g", "rw_lnx_b",
          "s5_a_re", "s5_a_im", "s5_b_re", "s5_b_im", "s5_c_re", "s5_c_im", "s5_d", "s5_log_step", "s5_glu_w",
          "s5_glu_b", "s5_out_g", "w_out", "ln1_g", "ln1_b", "ca_wq", "ca_wkv", "ca_wo", "ln2_g", "ln2_b",
          "ffn_w_up", "ffn_conv_w", "ffn_conv_b", "ffn_w_down", "ln3_g", "ln3_b"]


def kernel(**inputs):
    import numpy as _np
    import concourse.bacc as _bacc
    from concourse import mybir as _mybir
    from concourse.bass_utils import run_bass_kernel_spmd as _run

    nc = _bacc.Bacc("TRN2", target_bir_lowering=False, num_devices=1)
    arrays = {name: _np.ascontiguousarray(inputs[name]) for name in _NAMES}
    arrays.update(constants())
    io = {}
    for name, a in arrays.items():
        io[name] = nc.dram_tensor(f"in_{name}", a.shape, _mybir.dt.from_np(a.dtype), kind="ExternalInput").ap()
    io["out"] = nc.dram_tensor("out_0", (1, T, D), _mybir.dt.float32, kind="ExternalOutput").ap()
    build(nc, io)
    r = _run(nc, [{f"in_{k}": v for k, v in arrays.items()}], core_ids=[0])
    return r.results[0]["out_0"]
```

```python
import math
from contextlib import ExitStack

import numpy as np

import concourse.bass as bass
from concourse import mybir

DEPTH, D, T = 2, 1024, 512
P = 128
KT, NT = D // P, T // P
DA_HEADS, DA_W = 4, 512
RW_W, RW_IN, RW_TILES = 256, 896, 7
S5_W, S5_GROUPS, S5_STATE, S5_CH = 256, 16, 64, 16
S5_TILES = S5_GROUPS * S5_STATE // P
IN_W = 3 * DA_W + RW_IN + S5_W
N_MEM, MT, MEM_HEADS = 256, 2, 4
D_FF = 2816
FT = D_FF // P
CH = 64
NCH = T // CH
ALPHA = (2.0 * DEPTH) ** 0.25
DECAY = math.exp(-0.5)
LN_EPS, RMS_EPS, LNX_EPS = 1e-5, 1e-6, 64e-5
NEG = -1e37
ROUND = 1.5 * 2.0 ** 23
ROUND13 = ROUND / 2.0 ** 13
INV_2PI = 1.0 / (2.0 * math.pi)
TWO_PI_SAFE = 6.283184
PI_SAFE = 3.1415925
SLOTS = 2
SLOT = 2048
LN_SHARE = (576, 512, 640)
ARENA = 24088

C_ID, C_SU, C_IU, C_L1U, C_L1L, C_ONE, C_BONE, C_ROT = (P * i for i in range(8))
C_EYE = 8 * P
C_S5M = C_EYE + CH
C_IOTA = C_S5M + 4 * P
C_NEG = C_IOTA + T
C_MROW = C_NEG + CH
C_FREQ = C_MROW + P
C_SC = C_FREQ + 1
SC = {"ln_eps": LN_EPS, "rms_eps": RMS_EPS, "lnx_eps": LNX_EPS, "half_pi": math.pi / 2, "zero": 0.0, "one": 1.0}
C_W = C_SC + len(SC)
LEVELS = [2, 4, 8, 16, 32]

S1 = {}
S2 = {}


def _rows(table, names):
    at = 0
    for name, n in names:
        table[name] = (at, n)
        at += n
    return at


S1_N = _rows(S1, [("ffn_conv_w", 3 * FT), ("ffn_conv_b", FT)])
S2_N = _rows(S2, [("rw_mu", 7), ("rw_w0", 2), ("rw_a0", 2), ("rw_k_k", 2), ("rw_k_a", 2), ("rw_r_k", 2),
                  ("rw_lnx_g", 2), ("rw_lnx_b", 2), ("s5_d", 2), ("s5_glu_b", 2), ("s5_out_g", 2),
                  ("da_subln_g", 1)])


def two_pi_parts():
    hi = np.float32(round(2 * math.pi * 2 ** 9) / 2 ** 9)
    mid = np.float32(round((2 * math.pi - float(hi)) * 2 ** 22) / 2 ** 22)
    lo = np.float32(2 * math.pi - float(hi) - float(mid))
    return float(hi), float(mid), float(lo)


def constants():
    c = np.zeros((P, C_W), np.float32)
    p, m = np.arange(P)[:, None], np.arange(P)[None, :]
    same = p // CH == m // CH
    c[:, C_ID:C_ID + P] = p == m
    c[:, C_SU:C_SU + P] = same & (p < m)
    c[:, C_IU:C_IU + P] = same & (p <= m)
    c[:, C_L1U:C_L1U + P] = (p // 2 == m // 2) & (p < m)
    c[:, C_L1L:C_L1L + P] = (p // 2 == m // 2) & (p > m)
    c[:, C_ONE:C_ONE + P] = 1
    c[:, C_BONE:C_BONE + P] = same
    c[:, C_ROT:C_ROT + P] = np.where((p == m + 32) & (m % 64 < 32), -1.0, np.where((p == m - 32) & (m % 64 >= 32), 1.0, 0.0))
    c[:, C_EYE:C_EYE + CH] = p % CH == np.arange(CH)[None, :]
    for j in range(4):
        c[:, C_S5M + j * P:C_S5M + (j + 1) * P] = m // S5_CH == 2 * j + p // S5_STATE
    c[:, C_IOTA:C_IOTA + T] = np.arange(T)[None, :]
    c[:, C_NEG:C_NEG + CH] = NEG
    c[:, C_MROW:C_MROW + P] = m < CH
    inv = np.float32(10000.0) ** (-np.arange(0, 64, 2, dtype=np.float32) / np.float32(64))
    c[:, C_FREQ] = inv.astype(np.float32)[np.arange(P) % 32]
    for i, v in enumerate(SC.values()):
        c[:, C_SC + i] = v
    lev = np.zeros((P, len(LEVELS), 2, P), np.float32)
    for i, b in enumerate(LEVELS):
        joined = (p // (2 * b) == m // (2 * b)) & (p // b != m // b)
        lev[:, i, 0] = joined & (p > m)
        lev[:, i, 1] = joined & (p < m)
    lam = np.zeros((DEPTH, 2), np.float32)
    for l in range(DEPTH):
        lam[l] = 0.8 - 0.6 * math.exp(-0.3 * l), 1.0 - (0.8 - 0.6 * math.exp(-0.3 * l))
    return {"const": c, "level_masks": lev, "lambda_inits": lam}


class Sem:

    def __init__(self, handle):
        self.h, self.n = handle, 0


def build(nc, io):
    f32, f32r, u32, i32 = mybir.dt.float32, mybir.dt.float32r, mybir.dt.uint32, mybir.dt.int32
    ALU, ACT, AX = mybir.AluOpType, mybir.ActivationFunctionType, mybir.AxisListType
    ctx = ExitStack()
    with ctx:
        def sb(name, shape, dt=f32):
            return ctx.enter_context(nc.sbuf_tensor(name, shape, dt))

        x = sb("x", [P, NT, D])
        xT = [sb(n, [P, KT, T], f32r) for n in ("xT_high", "xT_low")]
        hT = xT
        raw = sb("raw_weights", [P, SLOTS, SLOT])
        split = [sb(n, [P, SLOTS, SLOT], f32r) for n in ("weights_high", "weights_low")]
        ropeC, ropeS = sb("ropeC", [P, T]), sb("ropeS", [P, T])
        K = sb("consts", [P, C_W])
        col1, col2, col3 = sb("col1", [P, S1_N]), sb("col2", [P, S2_N]), sb("col3", [P, 24])
        stat = sb("stat", [P, NT, 40])
        lamc = sb("lamc", [P, 4])
        s5c = sb("s5c", [P, 24, S5_TILES])
        with nc.sbuf_tensor("arena", [P, ARENA], f32) as arena:
            pass
        arena_r = sb("arena_split", [P, ARENA], f32r)

        def view(at, *shape, of=arena):
            n = int(np.prod(shape))
            assert at + n <= ARENA, (at, n)
            v = of[:, at:at + n]
            if len(shape) == 2:
                v = v.rearrange("p (a b) -> p a b", b=shape[1])
            if len(shape) == 3:
                v = v.rearrange("p (a b c) -> p a b c", b=shape[1], c=shape[2])
            return v

        def split_view(at, *shape):
            return view(at, *shape, of=arena_r)

        def as32(v):
            return v.bitcast(f32)

        qT, kT, vtok = view(0, 4, T), view(2048, 4, T), view(4096, NT, DA_W)
        PR = view(6144, RW_TILES, T + 2)
        uT = view(9744, 2, T)
        lrw = view(10768, RW_W)
        bn = view(11024, 2, S5_TILES, S5_CH)
        cn = view(11280, 2, 2, P)
        WK = 11792
        gluw = view(WK, 2, S5_W)
        lev = view(11024, len(LEVELS), 2, P)
        lnrow1 = view(6144, 2, D)
        AP_ = view(WK + 512, 4, T)
        aT = view(WK + 2560, 4, T)
        oh, osq, orr = view(WK + 4608, T), view(WK + 5120, T), view(WK + 5632, T)
        S = WK + 6144
        cT = view(S, 4, P)
        bpad, bT, cpad = view(S + 512, 2, P), view(S + 768, 2, P), view(S + 1024, 2, P)
        s_cos = [view(S + 1280, T), view(WK + 2048, T)]
        s_sin = [view(S + 1792, T), view(S + 5376, T)]
        s_m = [view(S + 2304 + 512 * i, T) for i in range(4)]
        s_z = [view(S + 4352 + 512 * i, T) for i in range(2)]
        assert S + 5888 <= ARENA
        s_turn, s_round = view(WK + 512, T), view(WK + 1024, T)
        rope_a = view(WK + 1536, T)
        s_n = [view(WK + 2560 + 512 * i, T) for i in range(4)]
        yT, zT, s_r = view(WK + 4608, 2, T), view(WK + 2560, 2, T), view(WK + 512, 2, T)
        shifted = view(WK + 5632, T)
        b_parts = view(WK + 5632, 4, S5_CH)
        R = WK + 512
        rw = {n: view(R + 512 * i, T) for i, n in enumerate(
            ["-", "a", "g", "t0", "iP", "kk", "kmod", "A", "B", "Bh", "K", "Kh", "R", "bonus", "t1"])}
        rP = view(R + 7680, NCH, CH + 1)
        vT_, bT_, kT_ = (view(R + 8200 + 512 * i, NT, P) for i in range(3))
        zA = view(R + 9736, 2, NT * P)
        uw = view(R + 10760, 2, NT * P)
        rZ = view(R + 512 * 5, 2, NT * P)
        rH, rS, rG, rQ = rw["K"], rw["iP"], rw["Bh"], rw["Kh"]
        rY, LR = uT[:, 0, :], uT[:, 1, :]
        assert R + 11784 <= ARENA
        mAB, mRB, mRK, mAK, Ti, TiT = (view(1024 * i, 2, NT * P) for i in range(6))
        mK, mV, q2 = view(0, KT, N_MEM), view(2048, MT, D), view(4096, KT, T)
        memT = [split_view(at, KT, N_MEM) for at in (13840, 15888)]
        o2 = [split_view(at, KT, T) for at in (17936, 8192)]
        p2, pT2 = view(12288, 2, N_MEM), view(12800, MT, T)
        memtok, lnrow2 = view(22040, MT, D), view(22040, 2, D)
        hid = [split_view(at, FT, T) for at in (0, FT * T)]
        fa = view(2 * FT * T, T + 2)
        fc = [view(2 * FT * T + 514 + 512 * i, T) for i in range(2)]
        posr, posf, ang, tn, tr = (view(2048 + 512 * i, T) for i in range(5))
        sheet = view(0, 3, P)
        lamr = view(512, 6, 64)

        def const(name):
            i = C_SC + list(SC).index(name)
            return K[:, i:i + 1]

        ident, ones, bones, rot = (K[:, c:c + P] for c in (C_ID, C_ONE, C_BONE, C_ROT))

        banks = [ctx.enter_context(nc.psum_tensor(f"bank{i}", [P, 512], f32)) for i in range(8)]

        def sem(name):
            return Sem(ctx.enter_context(nc.semaphore(name)))

        quiet = sem("engines_quiet")
        go = {n: sem(f"go_{n}") for n in ("pe", "act", "dve", "pool")}
        out_done = sem("output_written")
        S = {}

        def ev(name):
            if name not in S:
                S[name] = sem(name)
            return S[name]

        for i in range(8):
            ev(f"bank{i}_filled"), ev(f"bank{i}_emptied")
        for i in range(SLOTS):
            ev(f"slot{i}_loaded")
        for name in ("act_step", "dve_step", "pool_step", "chunk_used", "small_loaded", "s5_loaded", "s5_b_loaded", "rows_loaded", "levels_loaded", "mem_loaded", "chunk_high", "chunk_low_pool", "chunk_low_dve",
                     "x_high", "mem_high", "o2_high", "hT_high", "s5_raw", "rw_raw", "da_raw", "hid_high", "hid_low",
                     "shift_done", "s5_tables", "s5_b", "s5_c", "s5_w", "s5_n", "s5_x", "s5_y", "s5_z", "s5_g",
                     "s5_sq", "hT_s5", "lr_ready", "rw_kk", "rw_sq", "rw_gram_in", "rw_T", "rw_state", "rw_ysq",
                     "rw_cum", "rw_decay", "rw_kmod", "rw_rk", "rw_r", "rw_hat", "rw_bonus", "hT_rw", "attn_max", "attn_p", "attn_rs", "hT_da", "rope_done", "ln_var",
                     "ln_hat", "ln_out_dve", "ln_out_pool", "ca_max", "ca_p", "ffn_a", "ffn_c", "ffn_s", "sheets", "lam_in", "lam_exp",
                     "lam_row", "s5_col_v", "s5_col_a"):
            ev(name)

        def new_segment():
            for one in S.values():
                one.n = 0

        def raises(name):
            S[name].n += 1
            return S[name].h, 1

        def latest(name):
            return S[name].h, S[name].n

        def bank(g):
            return banks[groups[g][0]]

        def fills(g):
            return S[f"bank{groups[g][0]}_filled"].h, 1

        def filled(g):
            return S[f"bank{groups[g][0]}_filled"].h, groups[g][1] + 1

        def empties(g):
            return S[f"bank{groups[g][0]}_emptied"].h, 1

        def emptied(g):
            return S[f"bank{groups[g][0]}_emptied"].h, groups[g][1] + 1

        def free_for(g):
            return S[f"bank{groups[g][0]}_emptied"].h, groups[g][1]

        def chan(w, c0, n=256):
            return ("chan", w, c0, n)

        def tok(w, k0, nk, n0, n=512):
            return ("tok", w, k0, nk, n0, n)

        RW0 = 3 * DA_W
        chunks = [chan("w_in", RW0 + RW_IN)] + [chan("w_in", RW0 + 256 * i) for i in range(3)] + [chan("w_in", RW0 + 768, 128)]
        chunks += [chan("w_in", 256 * i) for i in range(4)]
        chunks += [tok("w_in", 4 * i, 4, 2 * DA_W) for i in range(2)]
        first = {"w_out": len(chunks)}
        for h in range(2):
            chunks += [tok("w_out", 0, 4, 512 * h), tok("w_out", 6, 2, 512 * h)]
        chunks += [tok("w_out", 4, 2, 0, D)]
        chunks += [chan("ca_wkv", 256 * i) for i in range(2)]
        first["ca_wq"] = len(chunks)
        chunks += [chan("ca_wq", 256 * i) for i in range(4)]
        first["ca_wkv"] = len(chunks)
        chunks += [chan("ca_wkv", 256 * i) for i in range(2, 4)]
        chunks += [tok("ca_wkv", 4 * i, 4, D + 512 * h) for h in range(2) for i in range(2)]
        first["ca_wo"] = len(chunks)
        chunks += [tok("ca_wo", 4 * i, 4, 512 * h) for h in range(2) for i in range(2)]
        first["ffn_up"] = len(chunks)
        for i in range(FT // 2):
            chunks += [chan("ffn_w_up", 256 * i), chan("ffn_w_up", D_FF + 256 * i)]
        first["ffn_down"] = len(chunks)
        chunks += [tok("ffn_w_down", 4 * i, min(4, FT - 4 * i), 512 * h) for h in range(2) for i in range(6)]

        def slot(of, c):
            v = of[:, c % SLOTS, :]
            kind = chunks[c]
            if kind[0] == "chan":
                return v[:, 0:8 * kind[3]].rearrange("p (k n) -> p k n", n=kind[3])
            return v[:, 0:kind[3] * kind[5]].rearrange("p (k n) -> p k n", n=kind[5])

        low_by = ["dve" if first["ca_wkv"] <= c < first["ca_wkv"] + 4 or c >= first["ffn_up"] + 2 or c == 0 else "pool" for c in range(len(chunks))]

        def low_done(c):
            return S[f"chunk_low_{low_by[c]}"].h, low_by[:c + 1].count(low_by[c])

        lnrow3 = raw[:, len(chunks) % SLOTS, :].rearrange("p (a d) -> p a d", a=2)

        groups = {}
        used = {}
        block = ctx.enter_context(nc.Block())

        def layers(eng, name, prologue, body):
            def rest():
                eng.drain().then_inc(quiet.h, 1)
                eng.wait_ge(go[name].h, 1)
                eng.sem_clear(go[name].h)

            new_segment()
            prologue()
            rest()
            with eng.Fori(0, DEPTH) as l:
                new_segment()
                body(l)
                rest()

        @block.tensor
        def _(pe):
            state = {}

            def fresh():
                state.update(uses=[0] * 8, chunk=0)
                share_banks(turn=[0, 1, 2, 3, 4, 5, 6, 7])

            def share_banks(**pools):
                state["pools"] = pools

            def take_bank(g, kind="turn"):
                pool = state["pools"][kind]
                b = pool.pop(0)
                pool.append(b)
                assert g not in groups, g
                groups[g] = (b, state["uses"][b])
                state["uses"][b] += 1
                return banks[b]

            mm = nc.tensor.matmul
            ALL = slice(None)

            def next_chunk():
                c = state["chunk"]
                state["chunk"] += 1
                return c, (slot(split[0], c), slot(split[1], c))

            def product(ps, a, b, start, stop):
                for i, (pa, pb) in enumerate(((a[0], b[0]), (a[0], b[1]), (a[1], b[0]))):
                    ins = mm(ps, pa, pb, start=start and i == 0, stop=stop and i == 2)
                return ins

            def part(v, *at):
                return v[0][at], v[1][at]

            def used_with_group(c, g):
                used[c] = filled(g)

            def used_with_step(c):
                one = raises("chunk_used")
                used[c] = latest("chunk_used")
                return one

            def transposes(g, srcs):
                ps = take_bank(g)
                pe.wait_ge(*free_for(g))
                for i, s in enumerate(srcs):
                    ins = nc.tensor.transpose(ps[:, i * P:(i + 1) * P], s, ident)
                ins.then_inc(*fills(g))

            def to_channels(tag, t):
                for h in range(2):
                    transposes(f"{tag}{t}{h}", [x[:, t, (4 * h + i) * P:(4 * h + i + 1) * P] for i in range(4)])

            def project_channels(names, rhs, n=T):
                for _ in projection_steps(names, rhs, n):
                    pass

            def projection_steps(names, rhs, n=T):
                names = list(names)
                while names:
                    c, w = next_chunk()
                    pe.wait_ge(*low_done(c))
                    for j in range(chunks[c][3] // P):
                        g = names.pop(0)
                        ps = take_bank(g)
                        pe.wait_ge(*free_for(g))
                        for k in range(KT):
                            ins = product(ps[:, 0:n], part(w, ALL, k, slice(j * P, (j + 1) * P)), part(rhs, ALL, k), k == 0, k == KT - 1)
                        ins.then_inc(*fills(g))
                        if j == chunks[c][3] // P - 1:
                            used_with_group(c, g)
                        yield g

            def project_tokens(tag, lhs, nk, tiles=NT, halves=(0, 1)):
                for h in halves:
                    out = [take_bank(f"{tag}{t}{h}") for t in range(tiles)]
                    for t in range(tiles):
                        pe.wait_ge(*free_for(f"{tag}{t}{h}"))
                    k0 = 0
                    while k0 < nk:
                        c, w = next_chunk()
                        n = chunks[c][3]
                        pe.wait_ge(*low_done(c))
                        for t in range(tiles):
                            for k in range(n):
                                ins = product(out[t][:, :], part(lhs, ALL, k0 + k, slice(t * P, (t + 1) * P)), part(w, ALL, k),
                                              k0 + k == 0, k0 + k == nk - 1)
                            if k0 + n == nk:
                                ins.then_inc(*fills(f"{tag}{t}{h}"))
                        if k0 + n == nk:
                            used_with_group(c, f"{tag}{tiles - 1}{h}")
                        else:
                            ins.then_inc(*used_with_step(c))
                        k0 += n

            def prologue():
                fresh()

            def s5_inputs_T(j):
                pe.wait_ge(S["s5_b"].h, j + 1)
                ps = take_bank(f"bT{j}")
                pe.wait_ge(*free_for(f"bT{j}"))
                for i in range(2):
                    ins = nc.tensor.transpose(ps[:, i * P:(i + 1) * P], bpad[:, i, :], ident)
                ins.then_inc(*fills(f"bT{j}"))

            def s5_inputs(j):
                pe.wait_ge(*emptied(f"bT{j}"))
                for i in range(2):
                    ps = take_bank(f"bu{j}{i}", "s5_in")
                    pe.wait_ge(*free_for(f"bu{j}{i}"))
                    mm(ps[:, :], bT[:, i, :], uT[:, j // 4, :], start=True, stop=True).then_inc(*fills(f"bu{j}{i}"))

            def s5_out(j):
                ct, jj = j // 4, j % 4
                if jj == 0:
                    state["y"] = take_bank(f"y{ct}", "s5_y")
                    pe.wait_ge(*free_for(f"y{ct}"))
                pe.wait_ge(S["s5_x"].h, 2 * (j + 1))
                pe.wait_ge(S["s5_c"].h, j + 1)
                for i in range(2):
                    ins = mm(state["y"][:, :], cpad[:, i, :], s_n[2 * i], start=jj == 0 and i == 0, stop=jj == 3 and i == 1)
                if jj == 3:
                    ins.then_inc(*fills(f"y{ct}"))
                else:
                    ins.then_inc(S["s5_y"].h, 1)

            def s5_gate():
                pe.wait_ge(S["s5_z"].h, 2)
                for n in range(2):
                    ps = take_bank(f"glu{n}")
                    pe.wait_ge(*free_for(f"glu{n}"))
                    for k in range(2):
                        ins = mm(ps[:, :], gluw[:, k, n * P:(n + 1) * P], zT[:, k, :], start=k == 0, stop=k == 1)
                    ins.then_inc(*fills(f"glu{n}"))

            def s5_norm():
                pe.wait_ge(S["s5_sq"].h, 1)
                ps = take_bank("s5ss")
                pe.wait_ge(*free_for("s5ss"))
                for k in range(2):
                    ins = mm(ps[:, :], ones, s_r[:, k, :], start=k == 0, stop=k == 1)
                ins.then_inc(*fills("s5ss"))

            def mixer_projections():
                for _ in projection_steps([f"rw{i}" for i in range(RW_TILES)], xT):
                    yield
                for i, nm in enumerate(projection_steps([f"q{i}" for i in range(4)] + [f"k{i}" for i in range(4)], xT)):
                    if i:
                        rotate(i - 1)
                    yield
                cs = [next_chunk() for _ in range(2)]
                vs = {}

                def v_half(t, half):
                    g = f"v{t}"
                    if half == 0:
                        vs[t] = take_bank(g)
                        pe.wait_ge(*free_for(g))
                    for k in range(4):
                        ins = product(vs[t][:, :], part(xT, ALL, 4 * half + k, slice(t * P, (t + 1) * P)), part(cs[half][1], ALL, k),
                                      half == 0 and k == 0, half == 1 and k == 3)
                    if half:
                        ins.then_inc(*fills(g))
                    if t == NT - 1:
                        used_with_group(cs[half][0], g)

                rotate(7)
                for ready in (((0, 0), (1, 0), (2, 0)), ((0, 1), (1, 1)), ((2, 1), (3, 0)), ((3, 1),)):
                    for t, half in ready:
                        if t == 0:
                            pe.wait_ge(*low_done(cs[half][0]))
                        v_half(t, half)
                    yield

            def rotate(i):
                pe.wait_ge(*emptied(f"{'qk'[i // 4]}{i % 4}"))
                ps = take_bank(f"rot{i}", "rot")
                pe.wait_ge(*free_for(f"rot{i}"))
                mm(ps[:, :], rot, (qT if i < 4 else kT)[:, i % 4, :], start=True, stop=True).then_inc(*fills(f"rot{i}"))

            def attention():
                todo = [(h, i) for h in range(DA_HEADS) for i in range(NT)]

                def scores(n):
                    h, i = todo[n]
                    for s in range(2):
                        g = f"sc{h}{i}{s}"
                        ps = take_bank(g)
                        pe.wait_ge(*free_for(g))
                        r = slice(64 * s, 64 * s + 64)
                        mm(ps[:, 0:(i + 1) * P], qT[r, h, i * P:(i + 1) * P], kT[r, h, 0:(i + 1) * P], start=True, stop=False)
                        ins = mm(ps[:, i * P + 64:(i + 1) * P], K[0:1, C_MROW:C_MROW + P], K[0:1, C_NEG:C_NEG + CH],
                                 start=False, stop=True)
                        ins.then_inc(*fills(g))

                def weights(n):
                    h, i = todo[n]
                    pe.wait_ge(S["attn_p"].h, n + 1)
                    transposes(f"aT{h}{i}", [AP_[:, 2 * (n % 2), b * P:(b + 1) * P] for b in range(i + 1)])

                def output(h):
                    for ii in range(NT):
                        pe.wait_ge(*emptied(f"aT{h}{ii}"))
                    ps = take_bank(f"o{h}")
                    pe.wait_ge(*free_for(f"o{h}"))
                    for b in range(NT):
                        ins = mm(ps[:, b * P:T], vtok[:, b, h * P:(h + 1) * P], aT[:, b, b * P:T], start=b == 0, stop=b == NT - 1)
                    ins.then_inc(*fills(f"o{h}"))

                def norm(h):
                    pe.wait_ge(*emptied(f"o{h}"))
                    ps = take_bank(f"oss{h}")
                    pe.wait_ge(*free_for(f"oss{h}"))
                    mm(ps[:, :], ones, osq, start=True, stop=True).then_inc(*fills(f"oss{h}"))

                scores(0)
                scores(1)
                for n in range(len(todo)):
                    if n + 2 < len(todo):
                        scores(n + 2)
                    if n % NT == 0 and n:
                        output(n // NT - 1)
                    weights(n)
                    if n % NT == 2 and n // NT:
                        norm(n // NT - 1)
                output(DA_HEADS - 1)
                norm(DA_HEADS - 1)

            def early_output(h):
                cs = [next_chunk() for _ in range(2)]
                rows = [0, 1, 2, 3, 6, 7]
                for t in range(NT):
                    g = f"wp{t}{h}"
                    ps = take_bank(g, "between")
                    pe.wait_ge(*free_for(g))
                    for i, k in enumerate(rows):
                        if t == 0 and i % 4 == 0:
                            pe.wait_ge(*low_done(cs[i // 4][0]))
                        ins = product(ps[:, :], part(hT, ALL, k, slice(t * P, (t + 1) * P)), part(cs[i // 4][1], ALL, i % 4), i == 0, i == 5)
                        if i == 5:
                            ins.then_inc(*fills(g))
                            if t == NT - 1:
                                for c, _ in cs:
                                    used_with_group(c, g)
                        yield

            def rwkv(j):
                between = early_output(j)

                def fill_in(n):
                    for _ in range(n):
                        next(between)

                if j == 0:
                    pe.wait_ge(S["lr_ready"].h, 3)
                for nm, r in (("w", slice(0, 32)), ("a", slice(32, 64)), ("g", slice(64, 128))):
                    g = f"lr{nm}{j}"
                    ps = take_bank(g)
                    pe.wait_ge(*free_for(g))
                    mm(ps[:, :], lrw[r, j * P:(j + 1) * P], LR[r, :], start=True, stop=True).then_inc(*fills(g))
                fill_in(5)
                pe.wait_ge(S["rw_sq"].h, 2 * j + 1)
                ps = take_bank(f"kss{j}")
                pe.wait_ge(*free_for(f"kss{j}"))
                mm(ps[:, :], bones, rw["t1"], start=True, stop=True).then_inc(*fills(f"kss{j}"))
                fill_in(5)
                pe.wait_ge(S["rw_gram_in"].h, j + 1)

                def grams(nm, hh):
                    a, b = {"ABT": "BA", "AB": "AB", "RBT": "BR", "RKT": "KR", "AKT": "KA"}[nm]
                    r = slice(64 * hh, 64 * hh + 64)
                    g = f"gr{nm}{j}{hh}"
                    ps = take_bank(g)
                    pe.wait_ge(*free_for(g))
                    for i in range(NT):
                        c = slice(i * P, (i + 1) * P)
                        ins = mm(ps[:, c], rw[a][r, c], rw[b][r, c], start=True, stop=True)
                    ins.then_inc(*fills(g))

                def to_tokens(nm):
                    src = {"A": rw["A"], "v": PR[:, 4 + j, 2:], "Bh": rw["Bh"], "Kh": rw["Kh"]}[nm]
                    transposes(f"tk{nm}{j}", [src[:, i * P:(i + 1) * P] for i in range(NT)])

                for hh in range(2):
                    grams("ABT", hh)
                    grams("AB", hh)
                pe.wait_ge(S["rw_bonus"].h, j + 1)
                ps = take_bank(f"bon{j}")
                pe.wait_ge(*free_for(f"bon{j}"))
                mm(ps[:, :], bones, rw["bonus"], start=True, stop=True).then_inc(*fills(f"bon{j}"))
                last = len(LEVELS) - 1
                for lv in range(len(LEVELS)):
                    for hh in range(2):
                        for nm in ("T", "TT"):
                            if lv:
                                pe.wait_ge(*emptied(f"d{nm}{j}{lv - 1}{hh}"))
                    if lv == 0:
                        pe.wait_ge(S["rw_T"].h, 4 * (j + 1))
                    for hh in range(2):
                        g = f"Z{j}{lv}{hh}"
                        ps = take_bank(g)
                        pe.wait_ge(*free_for(g))
                        for i in range(NT):
                            c = slice(i * P, (i + 1) * P)
                            ins = mm(ps[:, c], mAB[:, hh, c], Ti[:, hh, c], start=True, stop=True)
                        ins.then_inc(*fills(g))
                    for hh in range(2):
                        pe.wait_ge(*emptied(f"Z{j}{lv}{hh}"))
                        for nm, a, b in (("T", TiT, rZ), ("TT", rZ, TiT))[lv == last:]:
                            g = f"d{nm}{j}{lv}{hh}"
                            ps = take_bank(g)
                            pe.wait_ge(*free_for(g))
                            for i in range(NT):
                                c = slice(i * P, (i + 1) * P)
                                ins = mm(ps[:, c], a[:, hh, c], b[:, hh, c], start=True, stop=True)
                            ins.then_inc(*fills(g))
                    if lv == 0:
                        pe.wait_ge(S["rw_r"].h, j + 1)
                    if lv < 3:
                        for nm, hh in (("RBT", 0), ("RKT", 0), ("AKT", 0), ("RBT", 1), ("RKT", 1), ("AKT", 1))[2 * lv:2 * lv + 2]:
                            grams(nm, hh)
                    if lv == 2:
                        pe.wait_ge(S["rw_hat"].h, j + 1)
                    if lv < 4:
                        to_tokens(("A", "v", "Bh", "Kh")[lv])
                    fill_in((0, 0, 0, 2, 3)[lv])
                for hh in range(2):
                    for nm in ("RBT", "RKT", "AKT"):
                        pe.wait_ge(*emptied(f"gr{nm}{j}{hh}"))
                for nm in ("v", "Bh", "Kh"):
                    pe.wait_ge(*emptied(f"tk{nm}{j}"))
                for hh in range(2):
                    g = f"MV{j}{hh}"
                    ps = take_bank(g)
                    pe.wait_ge(*free_for(g))
                    for i in range(NT):
                        ins = mm(ps[:, i * CH:(i + 1) * CH], mAK[:, hh, i * P:(i + 1) * P], vT_[:, i, 64 * hh:64 * hh + 64],
                                 start=True, stop=True)
                    ins.then_inc(*fills(g))
                for hh in range(2):
                    pe.wait_ge(*emptied(f"dTT{j}{len(LEVELS) - 1}{hh}"))
                for hh in range(2):
                    pe.wait_ge(*emptied(f"MV{j}{hh}"))
                    pe.wait_ge(*emptied(f"tkA{j}"))
                    g = f"UW{j}{hh}"
                    ps = take_bank(g)
                    pe.wait_ge(*free_for(g))
                    for i in range(NT):
                        c = slice(i * P, (i + 1) * P)
                        ins = mm(ps[:, c], TiT[:, hh, c], zA[:, hh, c], start=True, stop=True)
                    ins.then_inc(*fills(g))
                fill_in(2)
                for hh in range(2):
                    pe.wait_ge(*emptied(f"UW{j}{hh}"))

                def U(hh, i, rows=slice(0, P)):
                    return uw[rows, hh, i * P:i * P + CH]

                def W(hh, i, rows=slice(0, P)):
                    return uw[rows, hh, i * P + CH:(i + 1) * P]

                ps = take_bank(f"Q{j}")
                pe.wait_ge(*free_for(f"Q{j}"))
                for hh in range(2):
                    for i in range(NT):
                        c = slice(i * P, (i + 1) * P)
                        ins = mm(ps[64 * hh:64 * hh + 64, c], W(hh, i), mRB[:, hh, c], start=True, stop=True)
                ins.then_inc(*fills(f"Q{j}"))
                for par in range(2):
                    rows = slice(64 * par, 64 * par + 64)
                    g = f"GH{j}{par}"
                    ps = take_bank(g)
                    pe.wait_ge(*free_for(g))
                    for hh in range(2):
                        out = slice(64 * hh, 64 * hh + 64)
                        hc = slice(64 * hh, 64 * hh + 64)
                        for i in range(NT):
                            mm(ps[out, i * CH:(i + 1) * CH], W(hh, i, rows), bT_[rows, i, hc], start=True, stop=True)
                        for i in range(NT):
                            c = slice(256 + i * CH, 256 + (i + 1) * CH)
                            mm(ps[out, c], bT_[rows, i, hc], U(hh, i, rows), start=True, stop=False)
                            ins = mm(ps[out, c], kT_[rows, i, hc], vT_[rows, i, hc], start=False, stop=True)
                    ins.then_inc(*fills(g))
                fill_in(2)
                for par in range(2):
                    pe.wait_ge(*emptied(f"GH{j}{par}"))
                pe.wait_ge(S["rw_state"].h, j + 1)
                for c in range(1, NCH - 1):
                    for hh in range(2):
                        r = slice(64 * hh, 64 * hh + 64)
                        g = f"S{j}{c}{hh}"
                        ps = take_bank(g)
                        pe.wait_ge(*free_for(g))
                        mm(ps[r, 0:CH], rG[r, c * CH:(c + 1) * CH], rS[r, c * CH:(c + 1) * CH], start=True, stop=True).then_inc(*fills(g))
                    fill_in(c < 6)
                    for hh in range(2):
                        pe.wait_ge(*emptied(f"S{j}{c}{hh}"))
                pe.wait_ge(*emptied(f"Q{j}"))
                for hh in range(2):
                    r = slice(64 * hh, 64 * hh + 64)
                    g = f"Y{j}{hh}"
                    ps = take_bank(g)
                    pe.wait_ge(*free_for(g))
                    for i in range(NT):
                        c = slice(i * P, (i + 1) * P)
                        mm(ps[r, c], U(hh, i), mRB[:, hh, c], start=i == 0, stop=False, skip_group_check=True)
                        mm(ps[r, c], vT_[:, i, r], mRK[:, hh, c], start=False, stop=False, skip_group_check=True)
                    for c in range(1, NCH):
                        cc = slice(c * CH, (c + 1) * CH)
                        ins = mm(ps[r, cc], rS[r, cc], rQ[r, cc], start=False, stop=c == NCH - 1, skip_group_check=True)
                    ins.then_inc(*fills(g))
                for hh in range(2):
                    pe.wait_ge(*emptied(f"Y{j}{hh}"))
                ps = take_bank(f"ym{j}")
                pe.wait_ge(*free_for(f"ym{j}"))
                mm(ps[:, :], bones, rY, start=True, stop=True).then_inc(*fills(f"ym{j}"))
                pe.wait_ge(S["rw_ysq"].h, j + 1)
                ps = take_bank(f"yv{j}")
                pe.wait_ge(*free_for(f"yv{j}"))
                mm(ps[:, :], bones, rw["t1"], start=True, stop=True).then_inc(*fills(f"yv{j}"))

            def memory_values():
                for h in range(2):
                    out = [take_bank(f"mv{m}{h}", "between") for m in range(MT)]
                    for m in range(MT):
                        pe.wait_ge(*free_for(f"mv{m}{h}"))
                    for half in range(2):
                        c, w = next_chunk()
                        pe.wait_ge(*low_done(c))
                        for m in range(MT):
                            for k in range(4):
                                kk = 4 * half + k
                                ins = product(out[m][:, :], part(memT, ALL, kk, slice(m * P, (m + 1) * P)), part(w, ALL, k), kk == 0, kk == KT - 1)
                                if kk == KT - 1:
                                    ins.then_inc(*fills(f"mv{m}{h}"))
                                    if m == MT - 1:
                                        used_with_group(c, f"mv{m}{h}")
                                elif m == MT - 1 and k == 3:
                                    ins.then_inc(*used_with_step(c))
                                yield

            def cross():
                values = memory_values()
                todo = [(h, i) for h in range(MEM_HEADS) for i in range(NT)]

                def scores(n):
                    h, i = todo[n]
                    g = f"cs{h}{i}"
                    ps = take_bank(g)
                    pe.wait_ge(*free_for(g))
                    for k in range(2):
                        ins = mm(ps[:, 0:N_MEM], q2[:, 2 * h + k, i * P:(i + 1) * P], mK[:, 2 * h + k, :], start=k == 0, stop=k == 1)
                    ins.then_inc(*fills(g))

                def weights(n):
                    h, i = todo[n]
                    pe.wait_ge(S["ca_p"].h, n + 1)
                    transposes(f"pT{h}{i}", [p2[:, n % 2, m * P:(m + 1) * P] for m in range(MT)])
                    if i == NT - 1:
                        for ii in range(NT):
                            pe.wait_ge(*emptied(f"pT{h}{ii}"))
                        for m in range(MT):
                            pe.wait_ge(*emptied(f"mv{m}{h // 2}"))
                        for d in range(2):
                            g = f"co{h}{d}"
                            ps = take_bank(g)
                            pe.wait_ge(*free_for(g))
                            for m in range(MT):
                                ins = mm(ps[:, :], mV[:, m, (2 * h + d) * P:(2 * h + d + 1) * P], pT2[:, m, :], start=m == 0, stop=m == 1)
                            ins.then_inc(*fills(g))

                scores(0)
                scores(1)
                for n in range(len(todo)):
                    if n + 2 < len(todo):
                        scores(n + 2)
                    for _ in range(4 if n < 8 else 0):
                        next(values)
                    weights(n)

            def body(l):
                fresh()
                for t in range(NT):
                    to_channels("x0", t)
                def sheet_columns(i):
                    n = (S1_N, S2_N, 24)[i]
                    ps = take_bank(f"sheet{i}")
                    pe.wait_ge(*free_for(f"sheet{i}"))
                    nc.tensor.transpose(ps[:, 0:n], sheet[0:n, i, :], ident[0:n, 0:n]).then_inc(*fills(f"sheet{i}"))

                pe.wait_ge(S["sheets"].h, 1)
                sheet_columns(2)
                for t in range(NT):
                    for h in range(2):
                        pe.wait_ge(*emptied(f"x0{t}{h}"))
                share_banks(turn=[0, 1, 2], rot=[3, 7], s5_in=[4, 5], s5_y=[6])
                project_channels(["u0", "u1"], xT)
                steps = mixer_projections()
                pe.wait_ge(*emptied("u0"))
                pe.wait_ge(*emptied("u1"))
                s5_inputs_T(0)
                next(steps)
                s5_inputs(0)
                pe.wait_ge(S["sheets"].h, 2)
                sheet_columns(0)
                sheet_columns(1)
                ps = take_bank("cT")
                pe.wait_ge(*free_for("cT"))
                for i in range(2):
                    for ct in range(2):
                        ins = nc.tensor.transpose(ps[:, (2 * i + ct) * P:(2 * i + ct + 1) * P], cn[:, i, ct, :], ident)
                ins.then_inc(*fills("cT"))
                for j in range(S5_TILES):
                    if j == 1:
                        pe.wait_ge(S["lam_row"].h, 1)
                        ps = take_bank("lam", "rot")
                        pe.wait_ge(*free_for("lam"))
                        mm(ps[:, 0:2], ones[0:1, :], lamr[0:1, 4, 0:2], start=True, stop=True).then_inc(*fills("lam"))
                    if j == 2:
                        for nm in ("sheet0", "sheet1", "sheet2", "lam"):
                            pe.wait_ge(*emptied(nm))
                    next(steps)
                    if j + 1 < S5_TILES:
                        s5_inputs_T(j + 1)
                    if j:
                        s5_out(j - 1)
                    next(steps)
                    if j + 1 < S5_TILES:
                        s5_inputs(j + 1)
                s5_out(S5_TILES - 1)
                next(steps)
                s5_gate()
                next(steps)
                s5_norm()
                assert next(steps, "done") == "done"
                share_banks(turn=[0, 1, 2, 3, 4, 5, 6, 7])
                for t in range(NT):
                    pe.wait_ge(*emptied(f"v{t}"))
                pe.wait_ge(S["rope_done"].h, 8)
                attention()
                pe.wait_ge(S["hT_s5"].h, 2)
                pe.wait_ge(S["hT_da"].h, DA_HEADS)
                share_banks(turn=[0, 1, 2, 3, 4, 5], between=[6, 7])
                for j in range(2):
                    rwkv(j)
                pe.wait_ge(S["mem_loaded"].h, 16)
                for m in range(MT):
                    for h in range(2):
                        transposes(f"mem{m}{h}", [memtok[:, m, (4 * h + i) * P:(4 * h + i + 1) * P] for i in range(4)])
                share_banks(turn=[0, 1, 2, 3, 4, 5, 6, 7])
                c, w = next_chunk()
                pe.wait_ge(*low_done(c))
                pe.wait_ge(S["hT_rw"].h, 2)
                for t in range(NT):
                    for h in range(2):
                        g = f"wo{t}{h}"
                        ps = take_bank(g)
                        pe.wait_ge(*free_for(g))
                        for k in range(2):
                            ins = product(ps[:, :], part(hT, ALL, 4 + k, slice(t * P, (t + 1) * P)),
                                          part(w, ALL, k, slice(512 * h, 512 * h + 512)), k == 0, k == 1)
                        ins.then_inc(*fills(g))
                used_with_group(c, g)
                for m in range(MT):
                    for h in range(2):
                        pe.wait_ge(*emptied(f"mem{m}{h}"))
                project_channels([f"mk{i}" for i in range(4)], memT, N_MEM)
                for t in range(NT):
                    pe.wait_ge(S["ln_out_dve"].h, t + 1)
                    pe.wait_ge(S["ln_out_pool"].h, t + 1)
                    to_channels("x1", t)
                for t in range(NT):
                    for h in range(2):
                        pe.wait_ge(*emptied(f"x1{t}{h}"))
                project_channels([f"cq{i}" for i in range(KT)], xT)
                project_channels([f"mk{i}" for i in range(4, KT)], memT, N_MEM)
                for i in range(KT):
                    pe.wait_ge(*emptied(f"cq{i}"))
                    pe.wait_ge(*emptied(f"mk{i}"))
                share_banks(turn=[0, 1, 2, 3, 4, 5], between=[6, 7])
                cross()
                share_banks(turn=[0, 1, 2, 3, 4, 5, 6, 7])
                for h in range(MEM_HEADS):
                    pe.wait_ge(*emptied(f"co{h}0"))
                    pe.wait_ge(*emptied(f"co{h}1"))
                project_tokens("cw", o2, KT)
                for t in range(NT):
                    pe.wait_ge(S["ln_out_dve"].h, NT + t + 1)
                    pe.wait_ge(S["ln_out_pool"].h, NT + t + 1)
                    to_channels("x2", t)
                for t in range(NT):
                    for h in range(2):
                        pe.wait_ge(*emptied(f"x2{t}{h}"))
                names = []
                for i in range(FT // 2):
                    names += [f"fa{2 * i}", f"fa{2 * i + 1}", f"fg{2 * i}", f"fg{2 * i + 1}"]
                project_channels(names, xT)
                pe.wait_ge(S["hid_low"].h, FT)
                project_tokens("dn", hid, FT)

            layers(pe, "pe", prologue, body)

        small = {}

        @block.sync
        def _(sp):
            def rest():
                sp.wait_ge(quiet.h, 4)
                sp.sem_clear(quiet.h)
                nums = sorted(s.h.num for s in S.values())
                assert nums == list(range(nums[0], nums[-1] + 1))
                sp.sem_clear(range(nums[0], nums[-1] + 1))
                for n in go:
                    sp.sem_inc(go[n].h, 1)

            def load(dst, src):
                sp.dma_start(dst, src).then_inc(S["small_loaded"].h, 16)
                S["small_loaded"].n += 16

            new_segment()
            load(K[:, :], io["const"])
            load(posr.bitcast(i32), io["positions"].to_broadcast([P, T]))
            for h in range(2):
                load(x[:, 2 * h:2 * h + 2, :], io["x"][0, 2 * h * P:(2 * h + 2) * P, :].rearrange("(t p) d -> p t d", p=P))
            rest()
            with sp.Fori(0, DEPTH) as l:
                new_segment()

                def layer_chunk(c):
                    kind = chunks[c]
                    w = io[kind[1]][l]
                    if kind[0] == "chan":
                        return w[:, kind[2]:kind[2] + kind[3]].rearrange("(k p) n -> p k n", p=P)
                    k0, nk, n0, n = kind[2:]
                    return w[k0 * P:(k0 + nk) * P, n0:n0 + n].rearrange("(k p) n -> p k n", p=P)

                def load_chunk(c):
                    if c >= SLOTS:
                        sp.wait_ge(*low_done(c - SLOTS))
                    sp.dma_start(slot(raw, c), layer_chunk(c)).then_inc(S[f"slot{c % SLOTS}_loaded"].h, 16)

                early = [(sheet[8:16, 2, :], io["s5_a_re"][l].rearrange("(j a) p -> j (a p)", a=2)),
                         (sheet[16:24, 2, :], io["s5_a_im"][l].rearrange("(j a) p -> j (a p)", a=2)),
                         (lamr[0:8, 5, 0:2], io["s5_log_step"][l].rearrange("(j a) -> j a", a=2))]
                early += [(bn[:, i, :, :], io[f"s5_b_{nm}"][l].rearrange("(j a) p h -> (a p) j h", a=2)) for i, nm in enumerate(("re", "im"))]
                for i, (dst, src) in enumerate(early):
                    sp.dma_start(dst, src).then_inc(S["s5_loaded" if i < 3 else "s5_b_loaded"].h, 16)
                    if i == 2:
                        load_chunk(0)
                load_chunk(1)
                for name, (at, n) in S2.items():
                    src = io[name][l]
                    if name == "rw_r_k":
                        src = src.rearrange("(c a) d -> c (a d)", a=2)
                    else:
                        src = src.rearrange("(c p) -> c p", p=P)
                    load(sheet[at:at + n, 1, :], src)
                for i, nm in enumerate(("re", "im")):
                    for dup in range(2):
                        load(cn[:, i, :, dup * 64:dup * 64 + 64], io[f"s5_c_{nm}"][l].rearrange("(c g) h p -> (g h) c p", c=2))
                load(sheet[0:S1["ffn_conv_w"][1], 0, :], io["ffn_conv_w"][l].rearrange("j (c p) -> (j c) p", p=P))
                load(sheet[S1["ffn_conv_b"][0]:S1_N, 0, :], io["ffn_conv_b"][l].rearrange("(c p) -> c p", p=P))
                for i, name in enumerate(("da_lam_q1", "da_lam_k1", "da_lam_q2", "da_lam_k2")):
                    load(lamr[0:1, i, :], io[name][l].unsqueeze(0))
                load(lamr[0:1, 4, 2:4], io["lambda_inits"][l].unsqueeze(0))
                load(lrw[0:32, :], io["rw_w2"][l])
                load(lrw[32:64, :], io["rw_a2"][l])
                load(lrw[64:128, :], io["rw_g2"][l])
                load(gluw, io["s5_glu_w"][l].rearrange("(k p) n -> p k n", p=P))
                small["layer"] = S["small_loaded"].n
                for c in range(2, len(chunks)):
                    load_chunk(c)
                sp.wait_ge(*low_done(len(chunks) - SLOTS))
                for i, nm in enumerate("gb"):
                    sp.dma_start(lnrow3[:, i, :], io[f"ln3_{nm}"][l].unsqueeze(0).to_broadcast([P, D])).then_inc(S["rows_loaded"].h, 16)
                rest()
            for h in range(2):
                sp.dma_start(io["out"][0, 2 * h * P:(2 * h + 2) * P, :].rearrange("(t p) d -> p t d", p=P),
                             x[:, 2 * h:2 * h + 2, :]).then_inc(out_done.h, 16)
            sp.wait_ge(out_done.h, 32)

        @block.scalar
        def _(act):
            A = nc.scalar.activation

            def prologue():
                act.wait_ge(S["s5_col_v"].h, 1)
                A(ropeS[:, :], tr, ACT.Sin).then_inc(*raises("act_step"))
                act.wait_ge(*latest("act_step"))
                A(tn, tr, ACT.Abs).then_inc(*raises("act_step"))
                act.wait_ge(*latest("act_step"))
                A(ropeC[:, :], tn, ACT.Sin, bias=const("half_pi"), scale=-1.0).then_inc(*raises("act_step"))
                act.wait_ge(*latest("act_step"))

            def body(l):

                def rows(n, dst):
                    for i, nm in enumerate("gb"):
                        act.dma_start(dst[:, i, :], io[f"ln{n}_{nm}"][l].unsqueeze(0).to_broadcast([P, D])).then_inc(S["rows_loaded"].h, 16)

                def chunk_high(c):
                    act.wait_ge(S[f"slot{c % SLOTS}_loaded"].h, 16 * (c // SLOTS + 1))
                    if c >= SLOTS:
                        act.wait_ge(*used[c - SLOTS])
                    A(slot(split[0], c), slot(raw, c), ACT.Copy).then_inc(*raises("chunk_high"))
                    act.wait_ge(*latest("chunk_high"))

                def part_high(name, src, k):
                    A(hT[0][:, k, :], src, ACT.Copy).then_inc(*raises(name))
                    act.wait_ge(*latest(name))

                def copy_out(g, dst, n=T):
                    act.wait_ge(*filled(g))
                    ps = bank(g)
                    A(dst, ps[:, 0:n], ACT.Copy).then_inc(*empties(g))
                    act.wait_ge(*emptied(g))

                def channels_out(tag, t):
                    for h in range(2):
                        g = f"{tag}{t}{h}"
                        act.wait_ge(*filled(g))
                        ps = bank(g)
                        A(xT[0][:, 4 * h:4 * h + 4, t * P:(t + 1) * P], ps[:, :].rearrange("p (k t) -> p k t", k=4), ACT.Copy).then_inc(*raises("x_high"))
                        act.wait_ge(*latest("x_high"))

                def layer_norm(n, t):
                    act.wait_ge(S["ln_var"].h, NT * n + t + 1)
                    v = stat[:, t, 1:2]
                    A(v, v, ACT.Ln, bias=const("ln_eps")).then_inc(*raises("act_step"))
                    act.wait_ge(*latest("act_step"))
                    A(v, v, ACT.Exp, scale=-0.5).then_inc(*raises("act_step"))
                    act.wait_ge(*latest("act_step"))
                    shift = stat[:, t, 2:3]
                    A(shift, shift, ACT.Identity, scale=v).then_inc(*raises("act_step"))
                    act.wait_ge(*latest("act_step"))
                    A(x[:, t, :], x[:, t, :], ACT.Identity, bias=shift, scale=v).then_inc(*raises("ln_hat"))
                    act.wait_ge(*latest("ln_hat"))

                for t in range(NT):
                    channels_out("x0", t)
                chunk_high(0)
                act.wait_ge(S["s5_col_v"].h, 1)
                A(s5c[:, 0, :], col3[:, 0:8], ACT.Exp).then_inc(*raises("s5_col_a"))
                act.wait_ge(*latest("s5_col_a"))
                act.wait_ge(S["s5_col_v"].h, 2)
                A(s5c[:, 3, :], s5c[:, 1, :], ACT.Exp).then_inc(*raises("s5_col_a"))
                act.wait_ge(*latest("s5_col_a"))
                A(s5c[:, 8, :], s5c[:, 5, :], ACT.Sin).then_inc(*raises("act_step"))
                act.wait_ge(*latest("act_step"))
                A(s5c[:, 9, :], s5c[:, 5, :], ACT.Abs).then_inc(*raises("act_step"))
                act.wait_ge(*latest("act_step"))
                A(s5c[:, 9, :], s5c[:, 9, :], ACT.Sin, bias=const("half_pi"), scale=-1.0).then_inc(*raises("s5_col_a"))
                act.wait_ge(*latest("s5_col_a"))
                def s5_tables(j):
                    act.wait_ge(S["s5_tables"].h, j + 1)
                    if j >= 2:
                        act.wait_ge(S["s5_n"].h, 4 * (j - 1))
                    A(s_sin[j % 2], s_turn, ACT.Sin, scale=TWO_PI_SAFE).then_inc(*raises("act_step"))
                    act.wait_ge(*latest("act_step"))
                    A(s_round, s_turn, ACT.Abs).then_inc(*raises("act_step"))
                    act.wait_ge(*latest("act_step"))
                    A(s_cos[j % 2], s_round, ACT.Sin, bias=const("half_pi"), scale=-TWO_PI_SAFE).then_inc(*raises("s5_col_a"))
                    act.wait_ge(*latest("s5_col_a"))

                def s5_inputs_T(j):
                    act.wait_ge(*filled(f"bT{j}"))
                    ps = bank(f"bT{j}")
                    if j:
                        act.wait_ge(*filled(f"bu{j - 1}1"))
                    A(bT, ps[:, 0:2 * P].rearrange("p (a b) -> p a b", a=2), ACT.Copy).then_inc(*empties(f"bT{j}"))
                    act.wait_ge(*emptied(f"bT{j}"))

                chunk_high(1)
                copy_out("u0", uT[:, 0, :])
                results = [(f"rw{i}", PR[:, i, 2:T + 2]) for i in range(RW_TILES)]
                results += [(f"q{i}", qT[:, i, :]) for i in range(4)] + [(f"k{i}", kT[:, i, :]) for i in range(4)]
                results += [(f"v{t}", vtok[:, t, :]) for t in range(NT)]
                after = {1: 3, 3: 4, 5: 5, 6: 6, 8: 7, 10: 8, 12: 9, 14: 10}
                s5_tables(0)
                copy_out("u1", uT[:, 1, :])
                chunk_high(2)
                s5_inputs_T(0)
                s5_tables(1)
                copy_out(*results[0])
                act.wait_ge(S["lam_in"].h, 1)
                A(lamr[0:1, 4, 4:6], lamr[0:1, 4, 6:8], ACT.Exp).then_inc(*raises("lam_exp"))
                act.wait_ge(*latest("lam_exp"))
                act.wait_ge(*filled("cT"))
                ps = bank("cT")
                A(cT[:, 0:2, :], ps[:, 0:2 * P].rearrange("p (a b) -> p a b", a=2), ACT.Copy).then_inc(*raises("act_step"))
                act.wait_ge(*latest("act_step"))
                A(cT[:, 2:4, :], ps[:, 2 * P:].rearrange("p (a b) -> p a b", a=2), ACT.Copy, scale=-1.0).then_inc(*empties("cT"))
                act.wait_ge(*emptied("cT"))
                for j in range(S5_TILES):
                    copy_out(*results[2 * j + 1])
                    if j + 1 < S5_TILES:
                        s5_inputs_T(j + 1)
                    if 2 * j + 1 in after:
                        chunk_high(after[2 * j + 1])
                    if 1 < j + 1 < S5_TILES:
                        s5_tables(j + 1)
                    copy_out(*results[2 * j + 2])
                    if 2 * j + 2 in after:
                        chunk_high(after[2 * j + 2])
                act.wait_ge(*filled("y1"))
                for ct in range(2):
                    act.wait_ge(*emptied(f"y{ct}"))
                    A(zT[:, ct, :], yT[:, ct, :], ACT.Gelu_apprx_tanh).then_inc(*raises("s5_z"))
                    act.wait_ge(*latest("s5_z"))
                copy_out(*results[-2])
                for n in range(2):
                    act.wait_ge(*filled(f"glu{n}"))
                    ps = bank(f"glu{n}")
                    A(s_r[:, n, :], ps[:, :], ACT.Sigmoid, bias=col2[:, S2["s5_glu_b"][0] + n:S2["s5_glu_b"][0] + n + 1]).then_inc(*empties(f"glu{n}"))
                    act.wait_ge(*emptied(f"glu{n}"))
                act.wait_ge(S["shift_done"].h, 7)
                A(LR[0:32, :], PR[0:32, 6, 2:], ACT.Tanh).then_inc(*raises("lr_ready"))
                act.wait_ge(*latest("lr_ready"))
                A(LR[32:64, :], PR[32:64, 6, 2:], ACT.Copy).then_inc(*raises("lr_ready"))
                act.wait_ge(*latest("lr_ready"))
                A(LR[64:128, :], PR[64:128, 6, 2:], ACT.Sigmoid).then_inc(*raises("lr_ready"))
                act.wait_ge(*latest("lr_ready"))
                act.wait_ge(S["s5_g"].h, 2)
                A(s_r, zT, ACT.Square).then_inc(*raises("s5_sq"))
                act.wait_ge(*latest("s5_sq"))
                copy_out(*results[-1])
                nc.scalar.preload_act_table_set("natural_log_exp_and_others")
                act.wait_ge(*filled("s5ss"))
                ps = bank("s5ss")
                A(yT[:, 0, :], ps[:, :], ACT.Ln, bias=const("rms_eps"), scale=1.0 / S5_W).then_inc(*raises("act_step"))
                act.wait_ge(*latest("act_step"))
                A(yT[:, 1, :], yT[:, 0, :], ACT.Exp, scale=-0.5).then_inc(*empties("s5ss"))
                act.wait_ge(*emptied("s5ss"))
                for ct in range(2):
                    act.wait_ge(S["s5_raw"].h, ct + 1)
                    part_high("hT_high", zT[:, ct, :], 6 + ct)
                act.wait_ge(S["s5_b"].h, S5_TILES)
                act.wait_ge(*filled("glu1"))
                act.dma_start(lev, io["level_masks"]).then_inc(S["levels_loaded"].h, 16)
                for c in range(first["w_out"], first["w_out"] + 2):
                    chunk_high(c)
                act.wait_ge(S["hT_s5"].h, 2)
                def attn_head_out(h):
                    act.wait_ge(*filled(f"o{h}"))
                    ps = bank(f"o{h}")
                    if h:
                        act.wait_ge(S["hT_da"].h, h)
                    A(oh, ps[:, :], ACT.Copy).then_inc(*raises("act_step"))
                    act.wait_ge(*latest("act_step"))
                    A(osq, ps[:, :], ACT.Square).then_inc(*empties(f"o{h}"))
                    act.wait_ge(*emptied(f"o{h}"))

                def attn_head_norm(h):
                    act.wait_ge(*filled(f"oss{h}"))
                    ps = bank(f"oss{h}")
                    A(orr, ps[:, :], ACT.Ln, bias=const("rms_eps"), scale=1.0 / P).then_inc(*empties(f"oss{h}"))
                    act.wait_ge(*emptied(f"oss{h}"))
                    A(orr, orr, ACT.Exp, scale=-0.5).then_inc(*raises("attn_rs"))
                    act.wait_ge(*latest("attn_rs"))

                def attn_head_high(h):
                    act.wait_ge(S["da_raw"].h, h + 1)
                    part_high("hT_high", oh, h)

                def attn_weights_out(n):
                    h, i = n // NT, n % NT
                    g = f"aT{h}{i}"
                    act.wait_ge(*filled(g))
                    ps = bank(g)
                    if h:
                        act.wait_ge(*filled(f"o{h - 1}"))
                    A(aT[:, 0:i + 1, i * P:(i + 1) * P], ps[:, 0:(i + 1) * P].rearrange("p (a b) -> p a b", a=i + 1), ACT.Copy).then_inc(*empties(g))
                    act.wait_ge(*emptied(g))

                for n in range(DA_HEADS * NT + 1):
                    h, i = n // NT, n % NT
                    if n < DA_HEADS * NT:
                        for s in range(2):
                            g = f"sc{h}{i}{s}"
                            act.wait_ge(*filled(g))
                            ps = bank(g)
                            act.wait_ge(S["attn_max"].h, n + 1)
                            if n >= 2:
                                act.wait_ge(*filled(f"aT{(n - 2) // NT}{(n - 2) % NT}"))
                            A(AP_[:, 2 * (n % 2) + s, 0:(i + 1) * P], ps[:, 0:(i + 1) * P], ACT.Exp,
                                   bias=stat[:, n % 2, 4 + s:5 + s], scale=0.125, accum_out=stat[:, n % 2, 6 + s:7 + s]).then_inc(*empties(g))
                            act.wait_ge(*emptied(g))
                    if n:
                        attn_weights_out(n - 1)
                        if (n - 1) // NT:
                            if (n - 1) % NT == 0:
                                attn_head_out((n - 1) // NT - 1)
                            if (n - 1) % NT == 2:
                                attn_head_norm((n - 1) // NT - 1)
                            if (n - 1) % NT == 3:
                                attn_head_high((n - 1) // NT - 1)
                attn_head_out(DA_HEADS - 1)
                attn_head_norm(DA_HEADS - 1)
                attn_head_high(DA_HEADS - 1)
                for j in range(2):
                    def c2(name):
                        return col2[:, S2[name][0] + j:S2[name][0] + j + 1]

                    if j:
                        act.wait_ge(S["hT_rw"].h, 1)
                    act.wait_ge(S["rw_kk"].h, j + 1)
                    A(rw["t1"], rw["kk"], ACT.Square).then_inc(*raises("rw_sq"))
                    act.wait_ge(*latest("rw_sq"))
                    act.wait_ge(*filled(f"lrw{j}"))
                    ps = bank(f"lrw{j}")
                    A(rw["t0"], ps[:, :], ACT.Sigmoid, bias=c2("rw_w0")).then_inc(*empties(f"lrw{j}"))
                    act.wait_ge(*emptied(f"lrw{j}"))
                    act.wait_ge(*filled(f"lra{j}"))
                    ps = bank(f"lra{j}")
                    A(rw["a"], ps[:, :], ACT.Sigmoid, bias=c2("rw_a0")).then_inc(*empties(f"lra{j}"))
                    act.wait_ge(*emptied(f"lra{j}"))
                    act.wait_ge(*filled(f"lrg{j}"))
                    ps = bank(f"lrg{j}")
                    A(rw["g"], ps[:, :], ACT.Copy).then_inc(*empties(f"lrg{j}"))
                    act.wait_ge(*emptied(f"lrg{j}"))
                    nc.scalar.preload_act_table_set("natural_log_exp_and_others")
                    act.wait_ge(S["rw_cum"].h, j + 1)
                    A(rw["iP"].rearrange("p (c t) -> p c t", c=NCH), rP[:, :, 1:], ACT.Exp, scale=DECAY).then_inc(*raises("act_step"))
                    act.wait_ge(*latest("act_step"))
                    A(rP[:, :, 1:], rP[:, :, 1:], ACT.Exp, scale=-DECAY).then_inc(*raises("rw_decay"))
                    act.wait_ge(*latest("rw_decay"))
                    act.wait_ge(*emptied(f"kss{j}"))
                    A(rw["t1"], rw["t1"], ACT.Ln).then_inc(*raises("act_step"))
                    act.wait_ge(*latest("act_step"))
                    A(rw["t1"], rw["t1"], ACT.Exp, scale=-0.5).then_inc(*raises("rw_sq"))
                    act.wait_ge(*latest("rw_sq"))

                    def to_tokens(nm):
                        act.wait_ge(*filled(f"tk{nm}{j}"))
                        ps = bank(f"tk{nm}{j}")
                        if nm == "A":
                            for i in range(2):
                                copy = A(zA.rearrange("p h (t c) -> p h t c", c=P)[:, i, :, CH:],
                                         ps[:, :].rearrange("p (t c) -> p t c", c=P)[:, :, i * CH:(i + 1) * CH], ACT.Copy)
                                if i:
                                    copy.then_inc(*empties(f"tkA{j}"))
                                    act.wait_ge(*emptied(f"tkA{j}"))
                                else:
                                    copy.then_inc(*raises("act_step"))
                                    act.wait_ge(*latest("act_step"))
                        else:
                            A({"v": vT_, "Bh": bT_, "Kh": kT_}[nm], ps[:, :].rearrange("p (t c) -> p t c", c=P), ACT.Copy).then_inc(*empties(f"tk{nm}{j}"))
                            act.wait_ge(*emptied(f"tk{nm}{j}"))

                    for lv in range(len(LEVELS)):
                        for hh in range(2):
                            g = f"Z{j}{lv}{hh}"
                            act.wait_ge(*filled(g))
                            ps = bank(g)
                            A(rZ[:, hh, :], ps[:, :], ACT.Copy).then_inc(*empties(g))
                            act.wait_ge(*emptied(g))
                        if lv < 4:
                            to_tokens(("A", "v", "Bh", "Kh")[lv])
                    for hh in range(2):
                        g = f"MV{j}{hh}"
                        act.wait_ge(*filled(g))
                        ps = bank(g)
                        A(zA.rearrange("p h (t c) -> p h t c", c=P)[:, hh, :, 0:CH], ps[:, 0:NT * CH].rearrange("p (t c) -> p t c", c=CH), ACT.Copy).then_inc(*empties(g))
                        act.wait_ge(*emptied(g))
                    for hh in range(2):
                        copy_out(f"UW{j}{hh}", uw[:, hh, :])
                    for hh in range(2):
                        r = slice(64 * hh, 64 * hh + 64)
                        g = f"Y{j}{hh}"
                        act.wait_ge(*filled(g))
                        ps = bank(g)
                        A(rY[r, :], ps[r, :], ACT.Copy).then_inc(*empties(g))
                        act.wait_ge(*emptied(g))
                    if j:
                        act.dma_start(memtok, io["mem"][0].rearrange("(m p) d -> p m d", p=P)).then_inc(S["mem_loaded"].h, 16)
                    act.wait_ge(*emptied(f"ym{j}"))
                    A(rw["t1"], rY, ACT.Square).then_inc(*raises("rw_ysq"))
                    act.wait_ge(*latest("rw_ysq"))
                    for c in range(first["w_out"] + 2 + 2 * j, first["w_out"] + 4 + 2 * j):
                        chunk_high(c)
                    act.wait_ge(*filled(f"yv{j}"))
                    ps = bank(f"yv{j}")
                    A(rw["t1"], ps[:, :], ACT.Ln, bias=const("lnx_eps"), scale=1.0 / CH).then_inc(*raises("act_step"))
                    act.wait_ge(*latest("act_step"))
                    A(rw["t1"], rw["t1"], ACT.Exp, scale=-0.5).then_inc(*empties(f"yv{j}"))
                    act.wait_ge(*emptied(f"yv{j}"))
                    act.wait_ge(S["rw_raw"].h, j + 1)
                    part_high("hT_high", rY, 4 + j)
                act.wait_ge(S["rw_gram_in"].h, 2)
                act.wait_ge(S["rw_r"].h, 2)
                rows(1, lnrow1)
                act.wait_ge(S["hT_rw"].h, 2)
                for m in range(MT):
                    for h in range(2):
                        act.wait_ge(*filled(f"mem{m}{h}"))
                        ps = bank(f"mem{m}{h}")
                        A(memT[0][:, 4 * h:4 * h + 4, m * P:(m + 1) * P], ps[:, :].rearrange("p (k t) -> p k t", k=4), ACT.Copy).then_inc(*raises("mem_high"))
                        act.wait_ge(*latest("mem_high"))
                c0 = first["ca_wq"]
                nc.scalar.preload_act_table_set("natural_log_exp_and_others")
                for t in range(NT):
                    layer_norm(0, t)
                    if t == 1:
                        chunk_high(c0 - 1)
                for i in range(4):
                    copy_out(f"mk{i}", mK[:, i, :], N_MEM)
                    if i % 2:
                        chunk_high(c0 + i // 2)
                for t in range(NT):
                    channels_out("x1", t)
                act.wait_ge(S["ln_out_dve"].h, NT)
                act.wait_ge(S["ln_out_pool"].h, NT)
                rows(2, lnrow2)
                for i in range(KT):
                    copy_out(f"cq{i}", q2[:, i, :])
                    if i % 2:
                        chunk_high(c0 + 2 + i // 2)
                c0 = first["ca_wkv"]
                for i in range(4, KT):
                    copy_out(f"mk{i}", mK[:, i, :], N_MEM)
                    if i % 2:
                        chunk_high(c0 + i // 2)
                for n in range(MEM_HEADS * NT + 1):
                    h, i = n // NT, n % NT
                    if n < MEM_HEADS * NT:
                        g = f"cs{h}{i}"
                        act.wait_ge(*filled(g))
                        ps = bank(g)
                        act.wait_ge(S["ca_max"].h, n + 1)
                        if n >= 2:
                            act.wait_ge(*filled(f"pT{(n - 2) // NT}{(n - 2) % NT}"))
                        A(p2[:, n % 2, :], ps[:, 0:N_MEM], ACT.Exp, bias=stat[:, n % 2, 9:10], scale=1.0 / 16,
                                  accum_out=stat[:, n % 2, 10:11]).then_inc(*empties(g))
                        act.wait_ge(*emptied(g))
                    if n in (4, 8):
                        for m in range(MT):
                            copy_out(f"mv{m}{n // 4 - 1}", mV[:, m, (n // 4 - 1) * 512:n // 4 * 512])
                    if n in (2, 4, 6, 8):
                        chunk_high(c0 + 3 + n // 2)
                    if n:
                        hh, ii = (n - 1) // NT, (n - 1) % NT
                        g = f"pT{hh}{ii}"
                        act.wait_ge(*filled(g))
                        ps = bank(g)
                        if hh:
                            act.wait_ge(*filled(f"co{hh - 1}1"))
                        A(pT2[:, :, ii * P:(ii + 1) * P], ps[:, 0:2 * P].rearrange("p (a b) -> p a b", a=2), ACT.Copy).then_inc(*empties(g))
                        act.wait_ge(*emptied(g))
                        if ii == NT - 1:
                            for d in range(2):
                                act.wait_ge(*filled(f"co{hh}{d}"))
                                ps = bank(f"co{hh}{d}")
                                A(o2[0][:, 2 * hh + d, :], ps[:, :], ACT.Copy).then_inc(*raises("o2_high"))
                                act.wait_ge(*latest("o2_high"))
                c0 = first["ffn_up"]
                for c in range(first["ca_wo"] + 2, c0 + 1):
                    chunk_high(c)
                nc.scalar.preload_act_table_set("natural_log_exp_and_others")
                for t in range(NT):
                    layer_norm(1, t)
                    if t:
                        channels_out("x2", t - 1)
                channels_out("x2", NT - 1)
                chunk_high(c0 + 1)
                act.wait_ge(S["ffn_a"].h, 1)

                def gate_input(i):
                    act.wait_ge(*filled(f"fa{i}"))
                    ps = bank(f"fa{i}")
                    if i:
                        act.wait_ge(S["ffn_c"].h, i)
                    A(fa[:, 2:T + 2], ps[:, :], ACT.Copy).then_inc(*empties(f"fa{i}"))
                    act.wait_ge(*emptied(f"fa{i}"))

                def gate(i):
                    act.wait_ge(S["ffn_c"].h, i + 1)
                    A(fc[i % 2], fc[i % 2], ACT.Silu).then_inc(*raises("ffn_s"))
                    act.wait_ge(*latest("ffn_s"))

                def hidden_high(i):
                    act.wait_ge(*emptied(f"fg{i}"))
                    A(hid[0][:, i, :], fc[i % 2], ACT.Copy).then_inc(*raises("hid_high"))
                    act.wait_ge(*latest("hid_high"))

                for i in range(0, FT, 2):
                    gate_input(i)
                    gate(i)
                    gate_input(i + 1)
                    chunk_high(c0 + 2 + i)
                    gate(i + 1)
                    hidden_high(i)
                    hidden_high(i + 1)
                    chunk_high(c0 + 3 + i)
                for c in range(first["ffn_down"] + 2, len(chunks)):
                    chunk_high(c)
                nc.scalar.preload_act_table_set("natural_log_exp_and_others")
                for t in range(NT):
                    layer_norm(2, t)

            layers(act, "act", prologue, body)

        @block.vector
        def _(dve):
            V = nc.vector
            tt, ts, stt = V.tensor_tensor, V.tensor_scalar, V.scalar_tensor_tensor
            mult, add, sub = ALU.mult, ALU.add, ALU.subtract

            def reduce_angle(dst, src, n, last):
                ts(n, src, INV_2PI, ROUND, mult, add).then_inc(*raises("dve_step"))
                dve.wait_ge(*latest("dve_step"))
                ts(n, n, ROUND, None, sub).then_inc(*raises("dve_step"))
                dve.wait_ge(*latest("dve_step"))
                hi, mid, lo = two_pi_parts()
                stt(dst, n, -hi, src, mult, add).then_inc(*raises("dve_step"))
                dve.wait_ge(*latest("dve_step"))
                stt(dst, n, -mid, dst, mult, add).then_inc(*raises("dve_step"))
                dve.wait_ge(*latest("dve_step"))
                stt(dst, n, -lo, dst, mult, add).then_inc(*raises("dve_step"))
                dve.wait_ge(*latest("dve_step"))
                ts(dst, dst, PI_SAFE, -PI_SAFE, ALU.min, ALU.max).then_inc(*raises(last))
                dve.wait_ge(*latest(last))

            def chunk_low(c):
                dve.wait_ge(S["chunk_high"].h, c + 1)
                tt(slot(split[1], c), slot(raw, c), as32(slot(split[0], c)), sub).then_inc(*raises("chunk_low_dve"))
                dve.wait_ge(*latest("chunk_low_dve"))

            def channels_low(tag, t, turn):
                for h in range(2):
                    g = f"{tag}{t}{h}"
                    dve.wait_ge(S["x_high"].h, 2 * (NT * turn + t) + h + 1)
                    ps = bank(g)
                    at = (slice(None), slice(4 * h, 4 * h + 4), slice(t * P, (t + 1) * P))
                    tt(xT[1][at], ps[:, :].rearrange("p (k t) -> p k t", k=4), as32(xT[0][at]), sub).then_inc(*empties(g))
                    dve.wait_ge(*emptied(g))

            def prologue():
                dve.wait_ge(S["small_loaded"].h, 16 * 4)
                V.tensor_copy(posf, posr.bitcast(i32)).then_inc(*raises("dve_step"))
                dve.wait_ge(*latest("dve_step"))
                ts(ang, posf, K[:, C_FREQ:C_FREQ + 1], None, mult).then_inc(*raises("dve_step"))
                dve.wait_ge(*latest("dve_step"))
                reduce_angle(tr, ang, tn, "s5_col_v")

            def body(l):
                dve.wait_ge(S["s5_loaded"].h, 48)
                V.tensor_copy(sheet[0:8, 2, :].rearrange("p (a b) -> p a b", a=2), lamr[0:8, 5, 0:2].unsqueeze(2).to_broadcast([8, 2, 64])).then_inc(*raises("sheets"))
                dve.wait_ge(*latest("sheets"))
                for t in range(NT):
                    channels_low("x0", t, 0)
                chunk_low(0)
                dve.wait_ge(*filled("sheet2"))
                ps = bank("sheet2")
                V.tensor_copy(col3[:, :], ps[:, 0:24]).then_inc(*empties("sheet2"))
                dve.wait_ge(*emptied("sheet2"))
                s = [s5c[:, i, :] for i in range(24)]
                are, aim = col3[:, 8:16], col3[:, 16:24]
                V.memset(stat[:, 0, 38:39], 0.0).then_inc(*raises("s5_col_v"))
                dve.wait_ge(*latest("s5_col_v"))
                dve.wait_ge(S["s5_col_a"].h, 1)
                tt(s[1], s[0], are, mult).then_inc(*raises("dve_step"))
                dve.wait_ge(*latest("dve_step"))
                tt(s[2], s[0], aim, mult).then_inc(*raises("dve_step"))
                dve.wait_ge(*latest("dve_step"))
                reduce_angle(s[5], s[2], s[4], "s5_col_v")
                ts(s[6], s[5], INV_2PI, None, mult).then_inc(*raises("dve_step"))
                dve.wait_ge(*latest("dve_step"))
                ts(s[7], s[6], ROUND13, ROUND13, add, sub).then_inc(*raises("dve_step"))
                dve.wait_ge(*latest("dve_step"))
                tt(s[6], s[6], s[7], sub).then_inc(*raises("dve_step"))
                dve.wait_ge(*latest("dve_step"))
                dve.wait_ge(S["s5_col_a"].h, 3)
                rho, sn, cs = s[3], s[8], s[9]
                tt(s[10], rho, cs, mult).then_inc(*raises("dve_step"))
                dve.wait_ge(*latest("dve_step"))
                ts(s[10], s[10], -1.0, None, add).then_inc(*raises("dve_step"))
                dve.wait_ge(*latest("dve_step"))
                tt(s[11], rho, sn, mult).then_inc(*raises("dve_step"))
                dve.wait_ge(*latest("dve_step"))
                tt(s[12], are, are, mult).then_inc(*raises("dve_step"))
                dve.wait_ge(*latest("dve_step"))
                tt(s[13], aim, aim, mult).then_inc(*raises("dve_step"))
                dve.wait_ge(*latest("dve_step"))
                tt(s[12], s[12], s[13], add).then_inc(*raises("dve_step"))
                dve.wait_ge(*latest("dve_step"))
                V.reciprocal(s[12], s[12]).then_inc(*raises("dve_step"))
                dve.wait_ge(*latest("dve_step"))
                tt(s[13], s[10], are, mult).then_inc(*raises("dve_step"))
                dve.wait_ge(*latest("dve_step"))
                tt(s[14], s[11], aim, mult).then_inc(*raises("dve_step"))
                dve.wait_ge(*latest("dve_step"))
                tt(s[13], s[13], s[14], add).then_inc(*raises("dve_step"))
                dve.wait_ge(*latest("dve_step"))
                tt(s[13], s[13], s[12], mult).then_inc(*raises("dve_step"))
                dve.wait_ge(*latest("dve_step"))
                tt(s[14], s[11], are, mult).then_inc(*raises("dve_step"))
                dve.wait_ge(*latest("dve_step"))
                tt(s[15], s[10], aim, mult).then_inc(*raises("dve_step"))
                dve.wait_ge(*latest("dve_step"))
                tt(s[14], s[14], s[15], sub).then_inc(*raises("dve_step"))
                dve.wait_ge(*latest("dve_step"))
                tt(s[14], s[14], s[12], mult).then_inc(*raises("dve_step"))
                dve.wait_ge(*latest("dve_step"))
                V.memset(PR[:, :, 0:2], 0.0).then_inc(*raises("dve_step"))
                dve.wait_ge(*latest("dve_step"))

                def token_shift(i):
                    dve.wait_ge(*emptied(f"rw{i}"))
                    tt(shifted, PR[:, i, 1:T + 1], PR[:, i, 2:T + 2], sub).then_inc(*raises("dve_step"))
                    dve.wait_ge(*latest("dve_step"))
                    stt(PR[:, i, 2:T + 2], shifted, col2[:, i:i + 1], PR[:, i, 2:T + 2], mult, add).then_inc(*raises("shift_done"))
                    dve.wait_ge(*latest("shift_done"))

                def rotary(i):
                    straight = (qT if i < 4 else kT)[:, i % 4, :]
                    dve.wait_ge(*filled(f"rot{i}"))
                    ps = bank(f"rot{i}")
                    tt(rope_a, ps[:, :], ropeS[:, :], mult).then_inc(*empties(f"rot{i}"))
                    dve.wait_ge(*emptied(f"rot{i}"))
                    tt(straight, straight, ropeC[:, :], mult).then_inc(*raises("dve_step"))
                    dve.wait_ge(*latest("dve_step"))
                    tt(straight, straight, rope_a, add).then_inc(*raises("rope_done"))
                    dve.wait_ge(*latest("rope_done"))

                iota = K[:, C_IOTA:C_IOTA + T]

                def s5_mask(j):
                    return K[:, C_S5M + j % 4 * P:C_S5M + (j % 4 + 1) * P]

                def s5_turns(j):
                    q, m = s_turn, s_round
                    ts(q, iota, s5c[:, 7, j:j + 1], None, mult).then_inc(*raises("dve_step"))
                    dve.wait_ge(*latest("dve_step"))
                    ts(m, q, ROUND, ROUND, add, sub).then_inc(*raises("dve_step"))
                    dve.wait_ge(*latest("dve_step"))
                    tt(q, q, m, sub).then_inc(*raises("dve_step"))
                    dve.wait_ge(*latest("dve_step"))
                    stt(q, iota, s5c[:, 6, j:j + 1], q, mult, add).then_inc(*raises("dve_step"))
                    dve.wait_ge(*latest("dve_step"))
                    ts(m, q, ROUND, ROUND, add, sub).then_inc(*raises("dve_step"))
                    dve.wait_ge(*latest("dve_step"))
                    tt(q, q, m, sub).then_inc(*raises("s5_tables"))
                    dve.wait_ge(*latest("s5_tables"))

                def s5_padded_b(j):
                    gr, gi = s5c[:, 13, j:j + 1], s5c[:, 14, j:j + 1]
                    br, bi = bn[:, 0, j, :], bn[:, 1, j, :]
                    ts(b_parts[:, 0, :], bi, gi, None, mult).then_inc(*raises("dve_step"))
                    dve.wait_ge(*latest("dve_step"))
                    ts(b_parts[:, 1, :], bi, gr, None, mult).then_inc(*raises("dve_step"))
                    dve.wait_ge(*latest("dve_step"))
                    stt(b_parts[:, 2, :], br, gr, b_parts[:, 0, :], mult, sub).then_inc(*raises("dve_step"))
                    dve.wait_ge(*latest("dve_step"))
                    stt(b_parts[:, 3, :], br, gi, b_parts[:, 1, :], mult, add).then_inc(*raises("dve_step"))
                    dve.wait_ge(*latest("dve_step"))
                    if j:
                        dve.wait_ge(*filled(f"bT{j - 1}"))
                    for i in range(2):
                        tt(bpad[:, i, :].rearrange("p (g h) -> p g h", h=16), b_parts[:, 2 + i, :].unsqueeze(1).to_broadcast([P, 8, 16]),
                                s5_mask(j).rearrange("p (g h) -> p g h", h=16), mult).then_inc(*raises("s5_b" if i else "dve_step"))
                        dve.wait_ge(*latest("s5_b" if i else "dve_step"))

                def s5_skip(ct):
                    dve.wait_ge(*filled(f"y{ct}"))
                    ps = bank(f"y{ct}")
                    stt(yT[:, ct, :], uT[:, ct, :], col2[:, S2["s5_d"][0] + ct:S2["s5_d"][0] + ct + 1], ps[:, :], mult, add).then_inc(*empties(f"y{ct}"))
                    dve.wait_ge(*emptied(f"y{ct}"))

                s5_turns(0)
                dve.wait_ge(S["s5_b_loaded"].h, 32)
                s5_padded_b(0)
                dve.wait_ge(S["s5_col_a"].h, 4)
                s5_turns(1)
                s5_padded_b(1)
                dve.wait_ge(S["small_loaded"].h, small["layer"])
                V.memset(stat[:, 0, 38:39], 0.0).then_inc(*raises("sheets"))
                dve.wait_ge(*latest("sheets"))
                for i in range(2):
                    tt(lamr[0:1, 2 * i, :], lamr[0:1, 2 * i, :], lamr[0:1, 2 * i + 1, :], mult).then_inc(*raises("dve_step"))
                    dve.wait_ge(*latest("dve_step"))
                    V.reduce_sum(lamr[0:1, 4, 6 + i:7 + i], lamr[0:1, 2 * i, :], AX.X).then_inc(*raises("lam_in" if i else "dve_step"))
                    dve.wait_ge(*latest("lam_in" if i else "dve_step"))
                dve.wait_ge(S["lam_exp"].h, 1)
                tt(lamr[0:1, 4, 0:1], lamr[0:1, 4, 5:6], lamr[0:1, 4, 4:5], sub).then_inc(*raises("dve_step"))
                dve.wait_ge(*latest("dve_step"))
                tt(lamr[0:1, 4, 0:1], lamr[0:1, 4, 0:1], lamr[0:1, 4, 2:3], sub).then_inc(*raises("dve_step"))
                dve.wait_ge(*latest("dve_step"))
                V.tensor_copy(lamr[0:1, 4, 1:2], lamr[0:1, 4, 3:4]).then_inc(*raises("lam_row"))
                dve.wait_ge(*latest("lam_row"))
                dve.wait_ge(*filled("sheet0"))
                ps = bank("sheet0")
                V.tensor_copy(col1[:, :], ps[:, 0:S1_N]).then_inc(*empties("sheet0"))
                dve.wait_ge(*emptied("sheet0"))
                dve.wait_ge(*filled("sheet1"))
                ps = bank("sheet1")
                V.tensor_copy(col2[:, :], ps[:, 0:S2_N]).then_inc(*empties("sheet1"))
                dve.wait_ge(*emptied("sheet1"))
                for j in range(S5_TILES):
                    ct = j // 4
                    cos, sin = s_cos[j % 2], s_sin[j % 2]
                    dve.wait_ge(S["s5_col_a"].h, 4 + j)
                    dve.wait_ge(*filled(f"bu{j}0"))
                    pr = bank(f"bu{j}0")
                    dve.wait_ge(*filled(f"bu{j}1"))
                    pi = bank(f"bu{j}1")
                    tt(s_m[0], pr[:, :], cos, mult).then_inc(*raises("dve_step"))
                    dve.wait_ge(*latest("dve_step"))
                    tt(s_m[1], pi[:, :], sin, mult).then_inc(*raises("dve_step"))
                    dve.wait_ge(*latest("dve_step"))
                    tt(s_m[2], pi[:, :], cos, mult).then_inc(*empties(f"bu{j}1"))
                    dve.wait_ge(*emptied(f"bu{j}1"))
                    tt(s_m[3], pr[:, :], sin, mult).then_inc(*empties(f"bu{j}0"))
                    dve.wait_ge(*emptied(f"bu{j}0"))
                    for i in range(2 * j, min(2 * j + 2, RW_TILES)):
                        token_shift(i)
                    if j >= 4:
                        rotary(2 * j - 8)
                        if j < 7:
                            rotary(2 * j - 7)
                    dve.wait_ge(S["s5_w"].h, 2 * j + 2)
                    for i in range(2):
                        V.tensor_tensor_scan(s_z[i], s5c[:, 3, j:j + 1].to_broadcast([P, T]), s_m[2 * i], 0.0, mult, add).then_inc(*raises("dve_step"))
                        dve.wait_ge(*latest("dve_step"))
                    if j:
                        if j % 4 == 0:
                            dve.wait_ge(*filled(f"y{ct - 1}"))
                        else:
                            dve.wait_ge(S["s5_y"].h, j - ct)
                    tt(s_n[0], s_z[0], cos, mult).then_inc(*raises("s5_n"))
                    dve.wait_ge(*latest("s5_n"))
                    tt(s_n[1], s_z[1], sin, mult).then_inc(*raises("s5_n"))
                    dve.wait_ge(*latest("s5_n"))
                    tt(s_n[2], s_z[0], sin, mult).then_inc(*raises("s5_n"))
                    dve.wait_ge(*latest("s5_n"))
                    tt(s_n[3], s_z[1], cos, mult).then_inc(*raises("s5_n"))
                    dve.wait_ge(*latest("s5_n"))
                    if j == 0:
                        dve.wait_ge(*emptied("cT"))
                    for i in range(2):
                        tt(cpad[:, i, :], cT[:, 2 * i + ct, :], s5_mask(j), mult).then_inc(*raises("s5_c" if i else "dve_step"))
                        dve.wait_ge(*latest("s5_c" if i else "dve_step"))
                    if j == 4:
                        s5_skip(0)
                    if j == 1:
                        dve.wait_ge(*filled("lam"))
                        ps = bank("lam")
                        V.tensor_copy(lamc[:, 0:2], ps[:, 0:2]).then_inc(*empties("lam"))
                        dve.wait_ge(*emptied("lam"))
                        g0 = S2["da_subln_g"][0]
                        tt(lamc[:, 2:3], col2[:, g0:g0 + 1], lamc[:, 1:2], mult).then_inc(*raises("dve_step"))
                        dve.wait_ge(*latest("dve_step"))
                    if j + 2 < S5_TILES:
                        dve.wait_ge(S["s5_col_a"].h, 5 + j)
                        s5_turns(j + 2)
                        s5_padded_b(j + 2)
                rotary(7)
                s5_skip(1)
                dve.wait_ge(*filled("glu1"))
                for n in range(2):
                    dve.wait_ge(*emptied(f"glu{n}"))
                    tt(zT[:, n, :], zT[:, n, :], s_r[:, n, :], mult).then_inc(*raises("s5_g"))
                    dve.wait_ge(*latest("s5_g"))
                dve.wait_ge(*emptied("s5ss"))
                for ct in range(2):
                    g0 = S2["s5_out_g"][0] + ct
                    stt(zT[:, ct, :], zT[:, ct, :], col2[:, g0:g0 + 1], yT[:, 1, :], mult, mult).then_inc(*raises("s5_raw"))
                    dve.wait_ge(*latest("s5_raw"))
                def head_out(h):
                    dve.wait_ge(S["attn_rs"].h, h + 1)
                    stt(oh, oh, lamc[:, 2:3], orr, mult, mult).then_inc(*raises("da_raw"))
                    dve.wait_ge(*latest("da_raw"))

                def attn_maxima(n):
                    h, i = n // NT, n % NT
                    st = stat[:, n % 2, :]
                    for b in range(2):
                        dve.wait_ge(*filled(f"sc{h}{i}{b}"))
                        ps = bank(f"sc{h}{i}{b}")
                        V.reduce_max(st[:, 8 + b:9 + b], ps[:, 0:(i + 1) * P], AX.X).then_inc(*raises("dve_step"))
                        dve.wait_ge(*latest("dve_step"))
                    ts(st[:, 4:6], st[:, 8:10], -0.125, None, mult).then_inc(*raises("attn_max"))
                    dve.wait_ge(*latest("attn_max"))

                attn_maxima(0)
                for n in range(DA_HEADS * NT):
                    h, i = n // NT, n % NT
                    st = stat[:, n % 2, :]
                    w = (i + 1) * P
                    if n + 1 < DA_HEADS * NT:
                        attn_maxima(n + 1)
                    dve.wait_ge(*emptied(f"sc{h}{i}0"))
                    dve.wait_ge(*emptied(f"sc{h}{i}1"))
                    V.reciprocal(st[:, 6:8], st[:, 6:8]).then_inc(*raises("dve_step"))
                    dve.wait_ge(*latest("dve_step"))
                    tt(st[:, 7:8], st[:, 7:8], lamc[:, 0:1], mult).then_inc(*raises("dve_step"))
                    dve.wait_ge(*latest("dve_step"))
                    p0, p1 = AP_[:, 2 * (n % 2), 0:w], AP_[:, 2 * (n % 2) + 1, 0:w]
                    ts(p1, p1, st[:, 7:8], None, mult).then_inc(*raises("dve_step"))
                    dve.wait_ge(*latest("dve_step"))
                    stt(p0, p0, st[:, 6:7], p1, mult, add).then_inc(*raises("attn_p"))
                    dve.wait_ge(*latest("attn_p"))
                    if n % NT == 3 and h:
                        head_out(h - 1)
                head_out(DA_HEADS - 1)
                for j in range(2):
                    def c2(name):
                        return col2[:, S2[name][0] + j:S2[name][0] + j + 1]

                    if j == 0:
                        dve.wait_ge(S["lr_ready"].h, 3)
                        dve.wait_ge(S["hT_da"].h, DA_HEADS)
                    r_, k_, v_ = PR[:, j, 2:], PR[:, 2 + j, 2:], PR[:, 4 + j, 2:]
                    t0, t1 = rw["t0"], rw["t1"]
                    ts(rw["kk"], k_, c2("rw_k_k"), None, mult).then_inc(*raises("rw_kk"))
                    dve.wait_ge(*latest("rw_kk"))
                    dve.wait_ge(*emptied(f"lrw{j}"))
                    V.memset(rP[:, :, 0:1], 1.0).then_inc(*raises("dve_step"))
                    dve.wait_ge(*latest("dve_step"))
                    one = const("one").to_broadcast([P, CH])
                    for c in range(NCH):
                        V.tensor_tensor_scan(rP[:, c, 1:], one, t0[:, c * CH:(c + 1) * CH], 0.0, mult, add).then_inc(*raises("rw_cum" if c == NCH - 1 else "dve_step"))
                        dve.wait_ge(*latest("rw_cum" if c == NCH - 1 else "dve_step"))
                    dve.wait_ge(*filled(f"kss{j}"))
                    ps = bank(f"kss{j}")
                    ts(t1, ps[:, :], 1e-24, None, ALU.max).then_inc(*empties(f"kss{j}"))
                    dve.wait_ge(*emptied(f"kss{j}"))
                    dve.wait_ge(*emptied(f"lra{j}"))
                    ts(t0, rw["a"], -1.0, c2("rw_k_a"), add, mult).then_inc(*raises("dve_step"))
                    dve.wait_ge(*latest("dve_step"))
                    stt(rw["kmod"], t0, 1.0, k_, add, mult).then_inc(*raises("rw_kmod"))
                    dve.wait_ge(*latest("rw_kmod"))

                    def c3(a):
                        return a.rearrange("p (c t) -> p c t", c=NCH)

                    pend = rP[:, :, CH:CH + 1].to_broadcast([P, NCH, CH])
                    dve.wait_ge(S["rw_decay"].h, j + 1)
                    tt(rw["K"], rw["kmod"], rw["iP"], mult).then_inc(*raises("dve_step"))
                    dve.wait_ge(*latest("dve_step"))
                    dve.wait_ge(S["rw_sq"].h, 2 * j + 2)
                    tt(rw["kk"], rw["kk"], t1, mult).then_inc(*raises("dve_step"))
                    dve.wait_ge(*latest("dve_step"))
                    stt(c3(rw["A"]), c3(rw["kk"]), -1.0, rP[:, :, 0:CH], mult, mult).then_inc(*raises("dve_step"))
                    dve.wait_ge(*latest("dve_step"))
                    tt(t0, rw["kk"], rw["a"], mult).then_inc(*raises("dve_step"))
                    dve.wait_ge(*latest("dve_step"))
                    tt(rw["B"], t0, rw["iP"], mult).then_inc(*raises("rw_gram_in"))
                    dve.wait_ge(*latest("rw_gram_in"))
                    dve.wait_ge(S["rw_rk"].h, j + 1)
                    ts(rw["bonus"], rw["bonus"], c2("rw_r_k"), None, mult).then_inc(*raises("rw_bonus"))
                    dve.wait_ge(*latest("rw_bonus"))

                    def add_early(t):
                        dve.wait_ge(*filled(f"wp{t}{j}"))
                        ps = bank(f"wp{t}{j}")
                        xx = x[:, t, j * 512:(j + 1) * 512]
                        stt(xx, xx, ALPHA, ps[:, :], mult, add).then_inc(*empties(f"wp{t}{j}"))
                        dve.wait_ge(*emptied(f"wp{t}{j}"))

                    def q3(a):
                        return a.rearrange("p (i t) -> p i t", t=P)

                    def m3(c):
                        return K[:, c:c + P].unsqueeze(1).to_broadcast([P, NT, P])

                    for hh in range(2):
                        g = f"grABT{j}{hh}"
                        dve.wait_ge(*filled(g))
                        ps = bank(g)
                        tt(q3(mAB[:, hh, :]), q3(ps[:, :]), m3(C_SU), mult).then_inc(*raises("dve_step"))
                        dve.wait_ge(*latest("dve_step"))
                        tt(q3(TiT[:, hh, :]), q3(ps[:, :]), m3(C_L1U), mult).then_inc(*empties(g))
                        dve.wait_ge(*emptied(g))
                        tt(q3(TiT[:, hh, :]), q3(TiT[:, hh, :]), m3(C_ID), add).then_inc(*raises("rw_T"))
                        dve.wait_ge(*latest("rw_T"))
                        g = f"grAB{j}{hh}"
                        dve.wait_ge(*filled(g))
                        ps = bank(g)
                        tt(q3(Ti[:, hh, :]), q3(ps[:, :]), m3(C_L1L), mult).then_inc(*empties(g))
                        dve.wait_ge(*emptied(g))
                        tt(q3(Ti[:, hh, :]), q3(Ti[:, hh, :]), m3(C_ID), add).then_inc(*raises("rw_T"))
                        dve.wait_ge(*latest("rw_T"))

                    def masked(nm, hh):
                        dst, mask = {"RBT": (mRB, C_IU), "RKT": (mRK, C_IU), "AKT": (mAK, C_SU)}[nm]
                        g = f"gr{nm}{j}{hh}"
                        dve.wait_ge(*filled(g))
                        ps = bank(g)
                        tt(q3(dst[:, hh, :]), q3(ps[:, :]), m3(mask), mult).then_inc(*empties(g))
                        dve.wait_ge(*emptied(g))

                    dve.wait_ge(*filled(f"bon{j}"))
                    ps = bank(f"bon{j}")
                    tt(rw["bonus"], ps[:, :], v_, mult).then_inc(*empties(f"bon{j}"))
                    dve.wait_ge(*emptied(f"bon{j}"))
                    add_early(0)
                    dve.wait_ge(S["levels_loaded"].h, 16)
                    for lv in range(len(LEVELS)):
                        for hh in range(2):
                            for i, (g, dst) in list(enumerate(((f"dT{j}{lv}{hh}", Ti), (f"dTT{j}{lv}{hh}", TiT))))[lv == len(LEVELS) - 1:]:
                                dve.wait_ge(*filled(g))
                                ps = bank(g)
                                V.copy_predicated(q3(dst[:, hh, :]), lev[:, lv, i, :].bitcast(u32).unsqueeze(1).to_broadcast([P, NT, P]), q3(ps[:, :])).then_inc(*empties(g))
                                dve.wait_ge(*emptied(g))
                        if lv < 3:
                            for nm, hh in (("RBT", 0), ("RKT", 0), ("AKT", 0), ("RBT", 1), ("RKT", 1), ("AKT", 1))[2 * lv:2 * lv + 2]:
                                masked(nm, hh)
                        if lv == 3:
                            add_early(1)
                    dve.wait_ge(*filled(f"Q{j}"))
                    ps = bank(f"Q{j}")
                    tt(rQ, ps[:, :], rw["R"], add).then_inc(*empties(f"Q{j}"))
                    dve.wait_ge(*emptied(f"Q{j}"))
                    tt(t0.rearrange("p (c k) -> p c k", c=NCH), K[:, C_EYE:C_EYE + CH].unsqueeze(1).to_broadcast([P, NCH, CH]), pend, mult).then_inc(*raises("dve_step"))
                    dve.wait_ge(*latest("dve_step"))
                    for par in range(2):
                        dve.wait_ge(*filled(f"GH{j}{par}"))
                        ps = bank(f"GH{j}{par}")

                        def par3(a):
                            return a.rearrange("p (i q k) -> p i q k", q=2, k=CH)[:, :, par, :]

                        tt(par3(rG), ps[:, 0:256].rearrange("p (i k) -> p i k", k=CH), par3(t0), add).then_inc(*raises("dve_step"))
                        dve.wait_ge(*latest("dve_step"))
                        V.tensor_copy(par3(rH), ps[:, 256:512].rearrange("p (i k) -> p i k", k=CH)).then_inc(*empties(f"GH{j}{par}"))
                        dve.wait_ge(*emptied(f"GH{j}{par}"))
                    V.tensor_copy(rS[:, CH:2 * CH], rH[:, 0:CH]).then_inc(*raises("rw_state"))
                    dve.wait_ge(*latest("rw_state"))
                    add_early(2)
                    for c in range(1, NCH - 1):
                        for hh in range(2):
                            r = slice(64 * hh, 64 * hh + 64)
                            g = f"S{j}{c}{hh}"
                            dve.wait_ge(*filled(g))
                            ps = bank(g)
                            tt(rS[r, (c + 1) * CH:(c + 2) * CH], ps[r, 0:CH], rH[r, c * CH:(c + 1) * CH], add).then_inc(*empties(g))
                            dve.wait_ge(*emptied(g))
                    add_early(3)
                    dve.wait_ge(*filled(f"ym{j}"))
                    ps = bank(f"ym{j}")
                    stt(rY, ps[:, :], -1.0 / CH, rY, mult, add).then_inc(*empties(f"ym{j}"))
                    dve.wait_ge(*emptied(f"ym{j}"))
                    dve.wait_ge(*emptied(f"yv{j}"))
                    tt(rY, rY, t1, mult).then_inc(*raises("dve_step"))
                    dve.wait_ge(*latest("dve_step"))
                    ts(rY, rY, c2("rw_lnx_g"), c2("rw_lnx_b"), mult, add).then_inc(*raises("dve_step"))
                    dve.wait_ge(*latest("dve_step"))
                    tt(rY, rY, rw["bonus"], add).then_inc(*raises("dve_step"))
                    dve.wait_ge(*latest("dve_step"))
                    tt(rY, rY, rw["g"], mult).then_inc(*raises("rw_raw"))
                    dve.wait_ge(*latest("rw_raw"))

                for m in range(MT):
                    for h in range(2):
                        dve.wait_ge(S["mem_high"].h, 2 * m + h + 1)
                        ps = bank(f"mem{m}{h}")
                        at = (slice(None), slice(4 * h, 4 * h + 4), slice(m * P, (m + 1) * P))
                        tt(memT[1][at], ps[:, :].rearrange("p (k t) -> p k t", k=4), as32(memT[0][at]), sub).then_inc(*empties(f"mem{m}{h}"))
                        dve.wait_ge(*emptied(f"mem{m}{h}"))

                def add_half(tag, t, h):
                    dve.wait_ge(*filled(f"{tag}{t}{h}"))
                    ps = bank(f"{tag}{t}{h}")
                    xx = x[:, t, h * 512:(h + 1) * 512]
                    stt(xx, xx, 1.0 if tag == "wo" else ALPHA, ps[:, :], mult, add).then_inc(*empties(f"{tag}{t}{h}"))
                    dve.wait_ge(*emptied(f"{tag}{t}{h}"))
                    V.bn_stats(stat[:, t, 12 + 6 * h:18 + 6 * h], xx).then_inc(*raises("dve_step"))
                    dve.wait_ge(*latest("dve_step"))

                def layer_norm(n, tag, rows, low):
                    def statistics(t):
                        st = stat[:, t, :]
                        if tag == "wo":
                            add_half(tag, t, 0)
                        add_half(tag, t, 1)
                        V.bn_aggr(st[:, 0:2], st[:, 12:24]).then_inc(*raises("dve_step"))
                        dve.wait_ge(*latest("dve_step"))
                        ts(st[:, 2:3], st[:, 0:1], -1.0, None, mult).then_inc(*raises("ln_var"))
                        dve.wait_ge(*latest("ln_var"))

                    def gain(t):
                        dve.wait_ge(S["ln_hat"].h, NT * n + t + 1)
                        xx = x[:, t, 0:LN_SHARE[n]]
                        tt(xx, xx, rows[:, 0, 0:LN_SHARE[n]], mult).then_inc(*raises("dve_step"))
                        dve.wait_ge(*latest("dve_step"))
                        tt(xx, xx, rows[:, 1, 0:LN_SHARE[n]], add).then_inc(*raises("ln_out_dve"))
                        dve.wait_ge(*latest("ln_out_dve"))

                    statistics(0)
                    statistics(1)
                    dve.wait_ge(S["rows_loaded"].h, 32 * (n + 1))
                    for t in range(NT):
                        gain(t)
                        if t + 2 < NT:
                            statistics(t + 2)
                        if n == 1 and t:
                            channels_low(low, t - 1, n + 1)
                    for t in {0: range(NT), 1: (NT - 1,), 2: ()}[n]:
                        channels_low(low, t, n + 1)

                layer_norm(0, "wo", lnrow1, "x1")
                for c in range(first["ca_wkv"], first["ca_wkv"] + 4):
                    chunk_low(c)

                def cross_out(h):
                    for d in range(2):
                        dve.wait_ge(S["o2_high"].h, 2 * h + d + 1)
                        ps = bank(f"co{h}{d}")
                        tt(o2[1][:, 2 * h + d, :], ps[:, :], as32(o2[0][:, 2 * h + d, :]), sub).then_inc(*empties(f"co{h}{d}"))
                        dve.wait_ge(*emptied(f"co{h}{d}"))

                def cross_maximum(n):
                    h, i = n // NT, n % NT
                    st = stat[:, n % 2, :]
                    dve.wait_ge(*filled(f"cs{h}{i}"))
                    ps = bank(f"cs{h}{i}")
                    V.reduce_max(st[:, 8:9], ps[:, 0:N_MEM], AX.X).then_inc(*raises("dve_step"))
                    dve.wait_ge(*latest("dve_step"))
                    ts(st[:, 9:10], st[:, 8:9], -1.0 / 16, None, mult).then_inc(*raises("ca_max"))
                    dve.wait_ge(*latest("ca_max"))

                cross_maximum(0)
                for n in range(MEM_HEADS * NT):
                    h, i = n // NT, n % NT
                    st = stat[:, n % 2, :]
                    if n + 1 < MEM_HEADS * NT:
                        cross_maximum(n + 1)
                    dve.wait_ge(*emptied(f"cs{h}{i}"))
                    V.reciprocal(st[:, 10:11], st[:, 10:11]).then_inc(*raises("dve_step"))
                    dve.wait_ge(*latest("dve_step"))
                    ts(p2[:, n % 2, :], p2[:, n % 2, :], st[:, 10:11], None, mult).then_inc(*raises("ca_p"))
                    dve.wait_ge(*latest("ca_p"))
                    if i == 2 and h:
                        cross_out(h - 1)
                cross_out(MEM_HEADS - 1)
                for t in range(NT):
                    add_half("cw", t, 0)
                layer_norm(1, "cw", lnrow2, "x2")
                V.memset(fa[:, 0:2], 0.0).then_inc(*raises("ffn_a"))
                dve.wait_ge(*latest("ffn_a"))

                def convolution(i):
                    def w(k):
                        return col1[:, k * FT + i:k * FT + i + 1]

                    c = fc[i % 2]
                    if i >= 2:
                        dve.wait_ge(S["hid_low"].h, i - 1)
                    dve.wait_ge(*emptied(f"fa{i}"))
                    ts(c, fa[:, 2:T + 2], w(2), col1[:, 3 * FT + i:3 * FT + i + 1], mult, add).then_inc(*raises("dve_step"))
                    dve.wait_ge(*latest("dve_step"))
                    stt(c, fa[:, 1:T + 1], w(1), c, mult, add).then_inc(*raises("dve_step"))
                    dve.wait_ge(*latest("dve_step"))
                    stt(c, fa[:, 0:T], w(0), c, mult, add).then_inc(*raises("ffn_c"))
                    dve.wait_ge(*latest("ffn_c"))

                def gated(i):
                    dve.wait_ge(*filled(f"fg{i}"))
                    ps = bank(f"fg{i}")
                    dve.wait_ge(S["ffn_s"].h, i + 1)
                    tt(fc[i % 2], ps[:, :], fc[i % 2], mult).then_inc(*empties(f"fg{i}"))
                    dve.wait_ge(*emptied(f"fg{i}"))

                c0 = first["ffn_up"]
                for i in range(0, FT, 2):
                    convolution(i)
                    convolution(i + 1)
                    chunk_low(c0 + 2 + i)
                    gated(i)
                    gated(i + 1)
                    chunk_low(c0 + 3 + i)
                c0 = first["ffn_down"]
                for c in range(c0 + 2, c0 + 8):
                    chunk_low(c)
                for t in range(NT):
                    add_half("dn", t, 0)
                for c in range(c0 + 8, len(chunks)):
                    chunk_low(c)
                layer_norm(2, "dn", lnrow3, None)

            layers(dve, "dve", prologue, body)

        @block.gpsimd
        def _(pool):
            G = nc.gpsimd

            def chunk_low(c):
                pool.wait_ge(S["chunk_high"].h, c + 1)
                G.tensor_tensor(slot(split[1], c), slot(raw, c), as32(slot(split[0], c)), ALU.subtract).then_inc(*raises("chunk_low_pool"))
                pool.wait_ge(*latest("chunk_low_pool"))

            def part_low(name, src, k):
                hT_parts.append(k)
                pool.wait_ge(S["hT_high"].h, len(hT_parts))
                G.tensor_tensor(hT[1][:, k, :], src, as32(hT[0][:, k, :]), ALU.subtract).then_inc(*raises(name))
                pool.wait_ge(*latest(name))

            def prologue():
                pass

            hT_parts = []

            def body(l):
                hT_parts.clear()
                for c in range(1, 3):
                    chunk_low(c)
                lows = {0: [3], 1: [4], 2: [5], 3: [6], 4: [7], 5: [8], 6: [9], 7: [10]}
                for j in range(S5_TILES):
                    pool.wait_ge(*emptied(f"bu{j}1"))
                    pool.wait_ge(*emptied(f"bu{j}0"))
                    G.tensor_tensor(s_m[0], s_m[0], s_m[1], ALU.add).then_inc(*raises("s5_w"))
                    pool.wait_ge(*latest("s5_w"))
                    G.tensor_tensor(s_m[2], s_m[2], s_m[3], ALU.subtract).then_inc(*raises("s5_w"))
                    pool.wait_ge(*latest("s5_w"))
                    for c in lows[j]:
                        chunk_low(c)
                    pool.wait_ge(S["s5_n"].h, 4 * j + 4)
                    G.tensor_tensor(s_n[0], s_n[0], s_n[1], ALU.subtract).then_inc(*raises("s5_x"))
                    pool.wait_ge(*latest("s5_x"))
                    G.tensor_tensor(s_n[2], s_n[2], s_n[3], ALU.add).then_inc(*raises("s5_x"))
                    pool.wait_ge(*latest("s5_x"))
                for ct in range(2):
                    part_low("hT_s5", zT[:, ct, :], 6 + ct)
                for c in range(first["w_out"], first["w_out"] + 2):
                    chunk_low(c)
                for h in range(DA_HEADS):
                    part_low("hT_da", oh, h)
                for j in range(2):
                    r_ = PR[:, j, 2:]

                    def c3(a):
                        return a.rearrange("p (c t) -> p c t", c=NCH)

                    pend = rP[:, :, CH:CH + 1].to_broadcast([P, NCH, CH])
                    pool.wait_ge(S["rw_kmod"].h, j + 1)
                    G.tensor_tensor(rw["bonus"], r_, rw["kmod"], ALU.mult).then_inc(*raises("rw_rk"))
                    pool.wait_ge(*latest("rw_rk"))
                    pool.wait_ge(S["rw_decay"].h, j + 1)
                    G.tensor_tensor(c3(rw["R"]), c3(r_), rP[:, :, 1:], ALU.mult).then_inc(*raises("rw_r"))
                    pool.wait_ge(*latest("rw_r"))
                    pool.wait_ge(S["rw_gram_in"].h, j + 1)
                    G.tensor_tensor(c3(rw["Bh"]), c3(rw["B"]), pend, ALU.mult).then_inc(*raises("pool_step"))
                    pool.wait_ge(*latest("pool_step"))
                    G.tensor_tensor(c3(rw["Kh"]), c3(rw["K"]), pend, ALU.mult).then_inc(*raises("rw_hat"))
                    pool.wait_ge(*latest("rw_hat"))
                    chunk_low(first["w_out"] + 2 + 2 * j)
                    part_low("hT_rw", rY, 4 + j)
                    chunk_low(first["w_out"] + 3 + 2 * j)

                def layer_norm(n, gain):
                    pool.wait_ge(S["rows_loaded"].h, 32 * (n + 1))
                    half = slice(LN_SHARE[n], D)
                    for t in range(NT):
                        pool.wait_ge(S["ln_hat"].h, NT * n + t + 1)
                        G.tensor_tensor(x[:, t, half], x[:, t, half], gain[:, 0, half], ALU.mult).then_inc(*raises("pool_step"))
                        pool.wait_ge(*latest("pool_step"))
                        G.tensor_tensor(x[:, t, half], x[:, t, half], gain[:, 1, half], ALU.add).then_inc(*raises("ln_out_pool"))
                        pool.wait_ge(*latest("ln_out_pool"))
                        if n == 0 and t == 1:
                            chunk_low(first["ca_wq"] - 1)

                layer_norm(0, lnrow1)
                for c in range(first["ca_wq"], first["ca_wkv"]):
                    chunk_low(c)
                for c in range(first["ca_wkv"] + 4, first["ffn_up"] + 1):
                    chunk_low(c)
                layer_norm(1, lnrow2)
                chunk_low(first["ffn_up"] + 1)
                for i in range(FT):
                    pool.wait_ge(S["hid_high"].h, i + 1)
                    G.tensor_tensor(hid[1][:, i, :], fc[i % 2], as32(hid[0][:, i, :]), ALU.subtract).then_inc(*raises("hid_low"))
                    pool.wait_ge(*latest("hid_low"))
                layer_norm(2, lnrow3)

            layers(pool, "pool", prologue, body)


_NAMES = ["x", "mem", "positions", "w_in", "da_lam_q1", "da_lam_k1", "da_lam_q2", "da_lam_k2", "da_subln_g",
          "rw_mu", "rw_w0", "rw_w2", "rw_a0", "rw_a2", "rw_g2", "rw_k_k", "rw_k_a", "rw_r_k", "rw_lnx_g", "rw_lnx_b",
          "s5_a_re", "s5_a_im", "s5_b_re", "s5_b_im", "s5_c_re", "s5_c_im", "s5_d", "s5_log_step", "s5_glu_w",
          "s5_glu_b", "s5_out_g", "w_out", "ln1_g", "ln1_b", "ca_wq", "ca_wkv", "ca_wo", "ln2_g", "ln2_b",
          "ffn_w_up", "ffn_conv_w", "ffn_conv_b", "ffn_w_down", "ln3_g", "ln3_b"]


def kernel(**inputs):
    import numpy as _np
    import concourse.bacc as _bacc
    from concourse import mybir as _mybir
    from concourse.bass_utils import run_bass_kernel_spmd as _run

    nc = _bacc.Bacc("TRN2", target_bir_lowering=False, num_devices=1)
    arrays = {name: _np.ascontiguousarray(inputs[name]) for name in _NAMES}
    arrays.update(constants())
    io = {}
    for name, a in arrays.items():
        io[name] = nc.dram_tensor(f"in_{name}", a.shape, _mybir.dt.from_np(a.dtype), kind="ExternalInput").ap()
    io["out"] = nc.dram_tensor("out_0", (1, T, D), _mybir.dt.float32, kind="ExternalOutput").ap()
    build(nc, io)
    r = _run(nc, [{f"in_{k}": v for k, v in arrays.items()}], core_ids=[0])
    return r.results[0]["out_0"]
```
